# Optimizing a Trainium2 kernel written in Bass

```python
import math
import jax, jax.numpy as jnp
from jax import lax
import numpy as np

D_MODEL = 2048
BATCH = 1
SEQ = 512
DEPTH = 1
DEC_BATCH = 8
DEC_SEQ = 4
PAST_LEN = 4096
PAGE_SIZE = 128

D_MIX = D_MODEL
D_POOL = D_MIX // 2
POOL_WINDOWS = (2, 4, 8, 16)
POOL_GROUP = D_POOL // len(POOL_WINDOWS)
MAX_WIN = max(POOL_WINDOWS)
POOL_STATE = MAX_WIN - 1
D_SGU = D_MIX - D_POOL
SGU_HEADS = 8
SGU_HEAD_DIM = D_SGU // SGU_HEADS
CHUNK = 128
D_IN = D_POOL + 2 * D_SGU
MEM_LEN = 256
MEM_HEADS = 4
MEM_HEAD_DIM = D_MODEL // MEM_HEADS
PEER_HEADS = 8
PEER_N_KEYS = 128
PEER_N_EXPERTS = PEER_N_KEYS * PEER_N_KEYS
PEER_QUERY_DIM = 256
PEER_HALF = PEER_QUERY_DIM // 2
PEER_TOPK = 16
PEER_BLOCK = 128
ALPHA = (2.0 * DEPTH) ** 0.25
BETA = (8.0 * DEPTH) ** -0.25
LN_EPS = 1e-5

kernel_name = "hybrid_pool_sgu_peer_mem_decode_step"

def layer_norm(x, g, b):
    xf = x.astype(jnp.float32)
    mu = jnp.mean(xf, axis=-1, keepdims=True)
    xc = xf - mu
    var = jnp.mean(xc * xc, axis=-1, keepdims=True)
    y = xc * lax.rsqrt(var + LN_EPS) * g.astype(jnp.float32) + b.astype(jnp.float32)
    return y.astype(x.dtype)

def pool_mix(a_ext, n_prev, start_pos, pool_w, pool_scale):
    T = a_ext.shape[1] - n_prev
    af = a_ext.astype(jnp.float32)
    csum = jnp.pad(jnp.cumsum(af, axis=1), ((0, 0), (MAX_WIN, 0), (0, 0)))
    pos = start_pos + jnp.arange(T)
    outs = []
    for g, w in enumerate(POOL_WINDOWS):
        c0, c1 = g * POOL_GROUP, (g + 1) * POOL_GROUP
        hi = csum[:, n_prev + MAX_WIN:n_prev + MAX_WIN + T, c0:c1]
        lo = csum[:, n_prev + MAX_WIN - w:n_prev + MAX_WIN - w + T, c0:c1]
        cnt = jnp.minimum(pos + 1, w).astype(jnp.float32)[None, :, None]
        d = (hi - lo) / cnt - af[:, n_prev:, c0:c1]
        outs.append(jnp.einsum('btc,cd->btd', d.astype(a_ext.dtype), pool_w[g]))
    return jnp.concatenate(outs, axis=-1) * pool_scale

def sgu_mix(u, v_n, sgu_w, sgu_b):
    b_, T, _ = v_n.shape
    pad = (-T) % CHUNK
    vp = jnp.pad(v_n, ((0, 0), (0, pad), (0, 0))).reshape(b_, (T + pad) // CHUNK, CHUNK, SGU_HEADS, SGU_HEAD_DIM)
    mask = jnp.tril(jnp.ones((CHUNK, CHUNK), dtype=bool))
    w = jnp.where(mask[None], sgu_w, 0)
    s = jnp.einsum('hij,bcjhd->bcihd', w, vp) + jnp.transpose(sgu_b)[None, None, :, :, None]
    s = s.reshape(b_, T + pad, D_SGU)[:, :T]
    return u * s

def mem_kv(mem, w_mk, w_mv):
    b_, m, _ = mem.shape
    k = (mem @ w_mk).reshape(b_, m, MEM_HEADS, MEM_HEAD_DIM)
    v = (mem @ w_mv).reshape(b_, m, MEM_HEADS, MEM_HEAD_DIM)
    return k, v

def mem_attend(h, mem_k, mem_v, w_mq, w_mo):
    b_, T, _ = h.shape
    q = (h @ w_mq).reshape(b_, T, MEM_HEADS, MEM_HEAD_DIM)
    s = jnp.einsum('bthd,bmhd->bhtm', q, mem_k).astype(jnp.float32) * (MEM_HEAD_DIM ** -0.5)
    p = jax.nn.softmax(s, axis=-1).astype(mem_v.dtype)
    o = jnp.einsum('bhtm,bmhd->bthd', p, mem_v).reshape(b_, T, D_MODEL)
    return o @ w_mo

def peer_ffn(h, peer_wq, peer_subkeys, peer_u, peer_v):
    b_, T, D = h.shape
    n = b_ * T
    pad = (-n) % PEER_BLOCK
    blocks = jnp.pad(h.reshape(n, D), ((0, pad), (0, 0))).reshape(-1, PEER_BLOCK, D)

    def block(xb):
        q = (xb @ peer_wq).reshape(PEER_BLOCK, PEER_HEADS, 2, PEER_HALF)
        s = jnp.einsum('thpd,pkd->thpk', q, peer_subkeys).astype(jnp.float32)
        sv, si = lax.top_k(s, PEER_TOPK)
        cand = (sv[:, :, 0, :, None] + sv[:, :, 1, None, :]).reshape(PEER_BLOCK, PEER_HEADS, PEER_TOPK * PEER_TOPK)
        cidx = (si[:, :, 0, :, None] * PEER_N_KEYS + si[:, :, 1, None, :]).reshape(PEER_BLOCK, PEER_HEADS, PEER_TOPK * PEER_TOPK)
        fv, fi = lax.top_k(cand, PEER_TOPK)
        eidx = jnp.take_along_axis(cidx, fi, axis=-1)
        gate = jax.nn.softmax(fv, axis=-1).astype(xb.dtype)
        act = jax.nn.gelu(jnp.einsum('thkd,td->thk', peer_u[eidx], xb))
        return jnp.einsum('thk,thkd->td', gate * act, peer_v[eidx])

    out = lax.map(block, blocks).reshape(-1, D)[:n]
    return out.reshape(b_, T, D)

def decoder_layer(h, pool_prev, start_pos, mem_k, mem_v, w_in, pool_w, pool_scale, sgu_ln_g, sgu_ln_b,
                  sgu_w, sgu_b, w_out, ln1_g, ln1_b, w_mq, w_mo, ln2_g, ln2_b,
                  peer_wq, peer_subkeys, peer_u, peer_v, ln3_g, ln3_b):
    z = h @ w_in
    a = z[..., :D_POOL]
    uv = jax.nn.gelu(z[..., D_POOL:])
    u = uv[..., :D_SGU]
    v_n = layer_norm(uv[..., D_SGU:], sgu_ln_g, sgu_ln_b)
    if pool_prev is None:
        a_ext, n_prev = a, 0
    else:
        a_ext, n_prev = jnp.concatenate([pool_prev.astype(a.dtype), a], axis=1), POOL_STATE
    y_pool = pool_mix(a_ext, n_prev, start_pos, pool_w, pool_scale)
    y_sgu = sgu_mix(u, v_n, sgu_w, sgu_b)
    m = jnp.concatenate([y_pool, y_sgu], axis=-1) @ w_out
    h = layer_norm(ALPHA * h + m, ln1_g, ln1_b)
    h = layer_norm(ALPHA * h + mem_attend(h, mem_k, mem_v, w_mq, w_mo), ln2_g, ln2_b)
    h = layer_norm(ALPHA * h + peer_ffn(h, peer_wq, peer_subkeys, peer_u, peer_v), ln3_g, ln3_b)
    return h, a_ext[:, -POOL_STATE:], v_n

def setup_inputs(seed: int = 0) -> dict:
    key = jax.random.key(seed)
    ks = jax.random.split(key, 32)

    def nrm(k, shape, scale=1.0):
        return jax.random.normal(k, shape, dtype=jnp.float32) * scale

    L, D = DEPTH, D_MODEL
    return {
        'x_prompt': nrm(ks[0], (BATCH, SEQ, D)),
        'x_sample': nrm(ks[1], (DEC_BATCH, DEC_SEQ, D)),
        'mem_prompt': nrm(ks[2], (BATCH, MEM_LEN, D)),
        'cache_pool': nrm(ks[3], (L, DEC_BATCH, POOL_STATE, D_POOL)),
        'cache_mem_k': nrm(ks[4], (L, DEC_BATCH, MEM_LEN, MEM_HEADS, MEM_HEAD_DIM)),
        'cache_mem_v': nrm(ks[5], (L, DEC_BATCH, MEM_LEN, MEM_HEADS, MEM_HEAD_DIM), BETA),
        'w_in': nrm(ks[6], (L, D, D_IN), D ** -0.5),
        'pool_w': nrm(ks[7], (L, len(POOL_WINDOWS), POOL_GROUP, POOL_GROUP), POOL_GROUP ** -0.5),
        'pool_scale': 1.0 + nrm(ks[8], (L, D_POOL), 0.02),
        'sgu_ln_g': 1.0 + nrm(ks[9], (L, D_SGU), 0.02),
        'sgu_ln_b': nrm(ks[10], (L, D_SGU), 0.02),
        'sgu_w': nrm(ks[11], (L, SGU_HEADS, CHUNK, CHUNK), CHUNK ** -0.5),
        'sgu_b': 1.0 + nrm(ks[12], (L, SGU_HEADS, CHUNK), 0.02),
        'w_out': nrm(ks[13], (L, D_MIX, D), BETA * D_MIX ** -0.5),
        'ln1_g': 1.0 + nrm(ks[14], (L, D), 0.02),
        'ln1_b': nrm(ks[15], (L, D), 0.02),
        'w_mq': nrm(ks[16], (L, D, D), D ** -0.5),
        'w_mk': nrm(ks[17], (L, D, D), D ** -0.5),
        'w_mv': nrm(ks[18], (L, D, D), BETA * D ** -0.5),
        'w_mo': nrm(ks[19], (L, D, D), BETA * D ** -0.5),
        'ln2_g': 1.0 + nrm(ks[20], (L, D), 0.02),
        'ln2_b': nrm(ks[21], (L, D), 0.02),
        'peer_wq': nrm(ks[22], (L, D, PEER_HEADS * PEER_QUERY_DIM), D ** -0.5),
        'peer_subkeys': nrm(ks[23], (L, 2, PEER_N_KEYS, PEER_HALF), PEER_HALF ** -0.5),
        'peer_u': nrm(ks[24], (L, PEER_N_EXPERTS, D), D ** -0.5),
        'peer_v': nrm(ks[25], (L, PEER_N_EXPERTS, D), BETA),
        'ln3_g': 1.0 + nrm(ks[26], (L, D), 0.02),
        'ln3_b': nrm(ks[27], (L, D), 0.02),
    }

def reference(x_prompt, x_sample, mem_prompt, cache_pool, cache_mem_k, cache_mem_v, w_in, pool_w, pool_scale,
              sgu_ln_g, sgu_ln_b, sgu_w, sgu_b, w_out, ln1_g, ln1_b, w_mq, w_mk, w_mv, w_mo, ln2_g, ln2_b,
              peer_wq, peer_subkeys, peer_u, peer_v, ln3_g, ln3_b):
    hp, hs = x_prompt, x_sample
    pool_p_list, mk_list, mv_list, pool_s_list, vs_list = [], [], [], [], []
    for l in range(DEPTH):
        lw = (w_in[l], pool_w[l], pool_scale[l], sgu_ln_g[l], sgu_ln_b[l], sgu_w[l], sgu_b[l], w_out[l],
              ln1_g[l], ln1_b[l], w_mq[l], w_mo[l], ln2_g[l], ln2_b[l],
              peer_wq[l], peer_subkeys[l], peer_u[l], peer_v[l], ln3_g[l], ln3_b[l])
        mk, mv = mem_kv(mem_prompt, w_mk[l], w_mv[l])
        hp, pool_p, _ = decoder_layer(hp, None, 0, mk, mv, *lw)
        hs, pool_s, v_s = decoder_layer(hs, cache_pool[l], PAST_LEN, cache_mem_k[l], cache_mem_v[l], *lw)
        pool_p_list.append(pool_p)
        mk_list.append(mk)
        mv_list.append(mv)
        pool_s_list.append(pool_s)
        vs_list.append(v_s)
    state_pool_prompt = jnp.stack(pool_p_list)
    state_mem_k_prompt = jnp.stack(mk_list)
    state_mem_v_prompt = jnp.stack(mv_list)
    state_pool_sample = jnp.stack(pool_s_list)
    state_sgu_v_sample = jnp.stack(vs_list)
    return (hp, hs, state_pool_prompt, state_mem_k_prompt, state_mem_v_prompt, state_pool_sample, state_sgu_v_sample)


_drawn_inputs = setup_inputs


def setup_inputs(seed=0):
    import zlib

    import numpy as np

    out = dict(_drawn_inputs(seed))
    spreads = {}
    factors = {'sgu_ln_g': 7.86,
     'sgu_ln_b': 8.426,
     'sgu_b': 2.792,
     'ln3_g': 24.166,
     'ln3_b': 23.602,
     'pool_scale': 3.002}
    for name, (base, spread) in spreads.items():
        noise = np.random.default_rng([zlib.crc32(name.encode()), seed]).standard_normal(out[name].shape)
        drawn = base * np.exp(spread * noise) if base else spread * noise
        out[name] = __import__('jax').numpy.asarray(drawn.astype(out[name].dtype))
    for name, factor in factors.items():
        out[name] = (out[name] * factor).astype(out[name].dtype)
    return out
```

```python
from contextlib import ExitStack

import concourse.bass as bass
from concourse import mybir

ALU = mybir.AluOpType
ACT = mybir.ActivationFunctionType
AX = mybir.AxisListType
F32 = mybir.dt.float32
FR = mybir.dt.float32r
U32 = mybir.dt.uint32

P = 128
D = 2048
KC = D // P
SEQ = 512
NT = SEQ // P
DB, DS = 8, 4
NS = DB * DS
T = SEQ + NS
HT = T // 2
D_POOL = 1024
PC = D_POOL // P
WINDOWS = (2, 4, 8, 16)
STATE = 15
SH = 8
MEM = 256
MT = MEM // P
AH = 4
HC = KC // AH
PH = 8
TOPK = 16
NK = 128
NPAIR = NK // 2
ALPHA = 2.0 ** 0.25
EPS = 1e-5
ASCALE = float(D // AH) ** -0.5
NEG = -3.0e38

MK0, MV0, V0, U0, A0, WO0, MQ0, MO0, WQ0, NPANEL = 0, 16, 32, 40, 48, 56, 72, 88, 104, 120

BASE = 16512
XB = KC * T * 4
H_HI, H_LO, Y_HI, Y_LO = (BASE + n * XB for n in range(4))
RAW = BASE + 4 * XB
W_HI = RAW + 2 * D * 4
W_LO = W_HI + 2 * D * 4
CST = W_LO + 2 * D * 4
TMP = CST + 2368
TOP = 229344


def program(nc, a, o):
    ctx = ExitStack()
    with ctx:
        def at(name, offset, shape, dt=F32):
            size = 4
            for s in shape[1:]:
                size *= s
            assert offset + size <= TOP, name
            return nc.alloc_sbuf_tensor_at(name, shape, dt, offset=offset)

        def sem(name):
            return ctx.enter_context(nc.semaphore(name))

        h_hi = at("h_hi", H_HI, [P, KC, T], FR)
        h_lo = at("h_lo", H_LO, [P, KC, T], FR)
        r = at("r", H_HI, [P, KC, T])
        y_hi = at("y_hi", Y_HI, [P, KC, T], FR)
        y_lo = at("y_lo", Y_LO, [P, KC, T], FR)
        raw = at("raw", RAW, [P, 2, KC, P])
        w_hi = at("w_hi", W_HI, [P, 2, KC, P], FR)
        w_lo = at("w_lo", W_LO, [P, 2, KC, P], FR)
        ident = at("ident", CST, [P, P])
        mean16 = at("mean16", CST + 512, [P, P])
        mean8 = at("mean8", CST + 1024, [P, P])
        ln_g = at("ln_g", CST + 1536, [P, 3, KC])
        ln_b = at("ln_b", CST + 1728, [P, 3, KC])
        sln_g = at("sln_g", CST + 1920, [P, SH])
        sln_b = at("sln_b", CST + 1952, [P, SH])
        pscale = at("pscale", CST + 1984, [P, PC])
        inv_n = at("inv_n", CST + 2016, [P, 4, 16])
        cnt = at("cnt", CST + 2272, [P, 16])
        mu = at("mu", TMP, [P, 2, HT])
        rs = at("rs", TMP + 2176, [P, 2, HT])
        sq = at("sq", TMP + 2 * 2176, [P, 2, 2, HT])
        yt = at("yt", TMP + 4 * 2176, [P, 2, T])
        ya = at("ya", TMP + 6 * 2176, [P, 2, T])

        pp = [ctx.enter_context(nc.psum_tensor(f"pp{i}", [P, 2, 512], F32)) for i in range(2)]
        pt = [ctx.enter_context(nc.psum_tensor(f"pt{i}", [P, 512], F32)) for i in range(2)]
        pl = ctx.enter_context(nc.psum_tensor("pl", [P, 2, 512], F32))

        k_scr = nc.dram_tensor("k_scr", [KC, P, MEM], F32).ap()
        g_scr = nc.dram_tensor("g_scr", [P, NK, T], F32).ap()

        def panels(w):
            return w.rearrange("(k p) (c n) -> p k c n", p=P, n=P)
        w_in = panels(a["w_in"][0])
        streams = [(MK0, panels(a["w_mk"][0]), 0, 16), (MV0, panels(a["w_mv"][0]), 0, 16),
                   (V0, w_in, 16, 8), (U0, w_in, 8, 8), (A0, w_in, 0, 8),
                   (WO0, panels(a["w_out"][0]), 0, 16), (MQ0, panels(a["w_mq"][0]), 0, 16),
                   (MO0, panels(a["w_mo"][0]), 0, 16), (WQ0, panels(a["peer_wq"][0]), 0, 16)]

        raw_in = [sem("raw_in0"), sem("raw_in1")]
        hi_ready = sem("hi_ready")
        lo_ready = sem("lo_ready")
        panel_done = sem("panel_done")
        evacuated = sem("evacuated")

        const_in = sem("const_in")
        bias_in, ws_sin, ident_zero, pool_step, sif_ready = (sem("bias_in"), sem("ws_sin"), sem("ident_zero"),
                                                             sem("pool_step"), sem("sif_ready"))
        ident_ready = sem("ident_ready")
        const_ready = sem("const_ready")
        row_in = [sem("row_in0"), sem("row_in1"), sem("row_in2")]
        tr_done, tr_hi, tr_free = sem("tr_done"), sem("tr_hi"), sem("tr_free")
        kvt_done, kvn_ready = sem("kvt_done"), sem("kvn_ready")
        kt_stored = [sem("kt_stored0"), sem("kt_stored1")]
        nat_stored = [sem("nat_stored0"), sem("nat_stored1")]

        nsem = {"mu": sem("norm_mu"),
                "mu_out": sem("norm_mu_out"),
                "xc": sem("norm_xc"),
                "sq": sem("norm_sq"),
                "var": sem("norm_var"),
                "veps": sem("norm_veps"),
                "std": sem("norm_std"),
                "yt": sem("norm_yt"),
                "ya": sem("norm_ya"),
                "hi": sem("norm_hi"),
                "used": sem("norm_used")}

        class Norm:
            def __init__(self, k, base, n):
                self.k, self.base, self.n = k, base, n

            def wait(self, eng, name, count):
                before = self.k if name in ("mu", "mu_out", "veps", "std") else self.base
                if name == "hi":
                    before -= 8 if self.k else 0
                eng.wait_ge(nsem[name], before + count)
        sgu_norm, norm1, norm2, norm3 = Norm(0, 0, 8), Norm(1, 8, 16), Norm(2, 24, 16), Norm(3, 40, 16)

        block = ctx.enter_context(nc.Block())

        def pe_panel(pe, u, x_hi, x_lo, first=False, n=T):
            s = u[1]
            pe.wait_ge(lo_ready, u[0] + 1)
            if not first:
                pe.wait_ge(evacuated, u[0] - 1)
            parts = [(0, 0, HT), (1, HT, T)] if n == T else [(0, 0, n)]
            for k in range(KC):
                for w, x in ((w_hi, x_hi), (w_hi, x_lo), (w_lo, x_hi)):
                    for b, t0, t1 in parts:
                        last = nc.tensor.matmul(pp[s][:, b, 0:t1 - t0], w[:, s, k, :], x[:, k, t0:t1],
                                                start=(k == 0 and w is w_hi and x is x_hi),
                                                stop=(k == KC - 1 and w is w_lo))
            last.then_inc(panel_done, 1)

        def act_split(act, u, first=False):
            s = u[1]
            act.wait_ge(raw_in[s], u[2])
            if not first:
                act.wait_ge(panel_done, u[0] - 1)
            nc.scalar.activation(w_hi[:, s], raw[:, s], ACT.Copy).then_inc(hi_ready, 1)

        def dve_split(dve, u):
            s = u[1]
            dve.wait_ge(hi_ready, u[0] + 1)
            nc.vector.tensor_tensor(w_lo[:, s], raw[:, s], w_hi[:, s].bitcast(F32),
                                    ALU.subtract).then_inc(lo_ready, 1)

        def num(u):
            return (u, u % 2, 16 * (u // 2 + 1))

        def in_loop(u0, i, d):
            half = (u0 + d) // 2
            return (i * 2 + (u0 + d), d % 2, i * 16 + 16 * (half + 1))

        def pairs(eng, u0, n, body, skip_first=0, skip_last=0, issued=0):
            for c in range(issued, skip_first):
                body(num(u0 + c), c)
            if n - skip_first - skip_last >= 2:
                assert skip_first % 2 == 0
                with eng.Fori(skip_first // 2, (n - skip_last) // 2) as i:
                    for d in range(2):
                        body(in_loop(u0, i, d), i * 2 + d)
            for c in range(n - skip_last, n):
                body(num(u0 + c), c)

        def act_norm(act, nm, gain, bias, buf, hi_out=None, after=None):
            nm.wait(act, "mu", 1)
            nc.scalar.activation(mu[:, :, :], pl[:, :, 0:HT], ACT.Copy).then_inc(nsem["mu_out"], 1)
            for c in range(nm.n):
                nm.wait(act, "xc", c + 1)
                if c >= 2:
                    nm.wait(act, "var", c - 1)
                nc.scalar.activation(sq[:, c % 2], buf[:, c, :].rearrange("p (b t) -> p b t", b=2),
                                     ACT.Square).then_inc(nsem["sq"], 1)
            nm.wait(act, "veps", 1)
            nc.scalar.activation(rs[:, :, :], rs[:, :, :], ACT.Sqrt).then_inc(nsem["std"], 1)
            for c in range(nm.n + 1):
                if c < nm.n:
                    nm.wait(act, "yt", c + 1)
                    if c >= 2:
                        nm.wait(act, "used", c - 1)
                    nc.scalar.activation(ya[:, c % 2, :], yt[:, c % 2, :], ACT.Identity,
                                         scale=gain[:, c:c + 1], bias=bias[:, c:c + 1]).then_inc(nsem["ya"], 1)
                if hi_out is not None and c >= 1:
                    nm.wait(act, "ya", c)
                    nc.scalar.activation(hi_out[:, c - 1, :], ya[:, (c - 1) % 2, :], ACT.Copy).then_inc(nsem["hi"], 1)
                if after is not None:
                    after(c)

        def flat(x):
            return x.rearrange("p b t -> p (b t)")

        def dve_norm(dve, nm, buf, lo_out=None, hi=None, after=None):
            nm.wait(dve, "mu_out", 1)
            for c in range(nm.n):
                nc.vector.tensor_tensor(buf[:, c, :], buf[:, c, :], flat(mu[:, :, :]), ALU.subtract).then_inc(nsem["xc"], 1)
            nm.wait(dve, "var", nm.n)
            nc.vector.tensor_scalar(rs[:, :, :], pl[:, :, 0:HT], EPS, None, ALU.add).then_inc(nsem["veps"], 1)
            nm.wait(dve, "std", 1)
            nc.vector.reciprocal(rs[:, :, :], rs[:, :, :])
            dve.drain()
            for c in range(nm.n + 2):
                if c < nm.n:
                    if c >= 2:
                        nm.wait(dve, "ya", c - 1)
                    nc.vector.tensor_tensor(yt[:, c % 2, :], buf[:, c, :], flat(rs[:, :, :]), ALU.mult)\
                        .then_inc(nsem["yt"], 1)
                if lo_out is not None and 1 <= c <= nm.n:
                    nm.wait(dve, "hi", c)
                    nc.vector.tensor_tensor(lo_out[:, c - 1, :], ya[:, (c - 1) % 2, :],
                                            hi[:, c - 1, :].bitcast(F32), ALU.subtract).then_inc(nsem["used"], 1)
                if after is not None:
                    after(c)

        mem_hi = at("mem_hi", Y_HI, [P, KC, MEM], FR)
        mem_lo = at("mem_lo", Y_HI + KC * MEM * 4, [P, KC, MEM], FR)
        rows = at("rows", Y_LO, [P, 3, D])
        row_tiles = [(a["mem_prompt"][0, t * P:(t + 1) * P, :], P, mem_hi, mem_lo, t * P) for t in range(MT)] + \
                    [(a["x_prompt"][0, t * P:(t + 1) * P, :], P, h_hi, h_lo, t * P) for t in range(NT)] + \
                    [(a["x_sample"].rearrange("b s d -> (b s) d"), NS, h_hi, h_lo, SEQ)]
        NG = KC // 4

        def row_views(m, part):
            _, rn, hi, lo, t0 = row_tiles[m // NG]
            g = m % NG
            ps = pt[m % 2][:, :].rearrange("p (q t) -> p q t", q=4)[:, :, 0:rn]
            return ps, (hi, lo)[part][:, 4 * g:4 * g + 4, t0:t0 + rn]

        kvt = at("kvt", TMP, [P, 2, MEM])
        kvn = at("kvn", TMP + 2048, [P, 2, MT, P])

        vt = at("vt", Y_HI, [P, SH, T])
        st = at("st", Y_HI + SH * T * 4, [P, SH, T])
        sgu_bias = at("sgu_bias", Y_LO, [P, SH, P])
        ws_n = at("ws_n", Y_LO + 4096, [P, SH, P])
        ws_t = at("ws_t", Y_LO + 8192, [P, SH, P])
        ws_s = at("ws_s", Y_LO + 12288, [NS, SH, NS])
        vns = at("vns", Y_LO + 13312, [NS, SH, P])
        vn = at("vn", TMP + 8 * 2176, [P, 2, NT, P])
        ug = at("ug", TMP, [P, 2, T])
        yf = at("yf", TMP + 2 * 2176, [P, 2, T])
        ws_zero, ws_in, ws_tr, ws_cp = sem("ws_zero"), sem("ws_in"), sem("ws_tr"), sem("ws_cp")
        ws_ready = sem("ws_ready")
        vn_ready, s_done, st_ready = sem("vn_ready"), sem("s_done"), sem("st_ready")
        y_ready, ysp_hi, ysp_lo = sem("y_ready"), sem("ysp_hi"), sem("ysp_lo")
        v_state_out = sem("v_state_out")

        ep = at("ep", TMP, [P, 2, 16 + SEQ])
        es = at("es", TMP + 4224, [P, 2, DB, 20])
        fa = at("fa", TMP + 5504, [P, 2, 16 + SEQ])
        fas = at("fas", TMP + 5504 + 4224, [P, 2, DB, 20])
        fb = at("fb", TMP + 11008, [P, 2, 16 + SEQ])
        fbs = at("fbs", TMP + 11008 + 4224, [P, 2, DB, 20])
        yp = at("yp", TMP + 11008, [P, 2, T])
        dp = at("dp", TMP + 16512, [P, 2, T])
        an = at("an", TMP + 20864, [STATE + NS, 2, P])
        cpn = at("cpn", Y_HI + 6 * T * 4, [DB * STATE, D_POOL])
        pw = at("pw", Y_LO + 7 * T * 4, [P, 2, 256])
        cp_in, pw_in, pool_zero = sem("cp_in"), sem("pw_in"), sem("pool_zero")
        ep_ready, es_ready, at_done, an_ready, an_out = (sem("ep_ready"), sem("es_ready"), sem("at_done"),
                                                         sem("an_ready"), sem("an_out"))
        d_ready, pm_done, yp_ready, pp_hi, pp_lo = (sem("d_ready"), sem("pm_done"), sem("yp_ready"),
                                                    sem("pp_hi"), sem("pp_lo"))
        state_out = sem("state_out")

        qt = at("qt", Y_HI, [P, KC, T])
        kv = at("kv", Y_LO, [P, 2, MT, D])
        qm = at("qm", W_HI, [P, KC, 288])
        kr = at("kr", W_HI + KC * 288 * 4, [P, 3, 4, MEM])
        ktp = at("ktp", W_HI, [P, KC, MEM])
        vp = at("vp", W_LO, [P, MT, D])
        ssm = at("ssm", TMP, [NS, AH, MEM])
        pts = at("pts", TMP + 4096, [P, AH * MT, NS])
        smx = at("smx", TMP + 5120, [NS, 4, AH])
        pr = at("pr", TMP + 5248, [P, 2, MEM])
        pst = at("pst", TMP + 7296, [P, 2, 4])
        ptt = at("ptt", TMP + 7328, [P, 2, MT, SEQ])
        qm_zero, qm_ready = sem("qm_zero"), sem("qm_ready")
        kv_in = [sem("kv_in0"), sem("kv_in1")]
        kr_tr, kr_a, kr_d, ks_done = sem("kr_tr"), sem("kr_a"), sem("kr_d"), sem("ks_done")
        ss_max, ss_exp, ss_p, ss_tr, ss_pt, sv_done, so_hi, so_lo = [sem("att_s%d" % n) for n in range(8)]
        kp_in, vp_in = sem("kp_in"), sem("vp_in")
        ps_done, ps_max, ps_exp, ps_p, ps_tr, ps_pt, pv_done, po_hi, po_lo = [sem("att_p%d" % n) for n in range(9)]

        sub_n = at("sub_n", Y_LO, [P, 2, P])
        sub_t = at("sub_t", Y_LO + 1024, [P, 2, P])
        q2 = at("q2", Y_LO + 2048, [P, 2, T])
        sc = at("sc", Y_LO + 6400, [P, 2, NT + 1, P])
        sc2 = at("sc2", Y_LO + 11520, [P, NT + 1, P])
        sv = at("sv", Y_LO + 14080, [P, PH, 2, NT + 1, TOPK])
        si = at("si", Y_LO + 19200, [P, PH, 2, NT + 1, TOPK], U32)
        cand = at("cand", Y_LO + 24320, [P, NT + 1, 256])
        cand2 = at("cand2", Y_LO + 29440, [P, NT + 1, 256])
        fi = at("fi", Y_HI, [P, NT + 1, TOPK], U32)
        ab_u = at("ab_u", Y_HI + 320, [P, 2, NT + 1, TOPK], U32)
        ab_f = at("ab_f", Y_HI + 960, [P, PH, 2, NT + 1, TOPK])
        sif = at("sif", Y_HI + 6080, [P, PH, 2, NT + 1, TOPK])
        eq = at("eq", Y_HI + 11200, [P, 2, NT + 1, TOPK, TOPK])
        sums = at("sums", Y_HI + 21440, [P, 2, 40])
        iota16 = at("iota16", Y_HI + 21760, [P, TOPK])
        PICK_STEPS = 5
        ij = at("ij", TMP, [P, 2, NT + 1, P])
        gw = at("gw", TMP + 5120, [P, NT + 1, P])
        ijt = at("ijt", TMP + 7680, [P, 3, T])
        iota_k = at("iota_k", TMP + 14208, [P, P])
        oh = at("oh", RAW, [P, 2, 2, 4, P])
        gs = at("gs", Y_HI, [P, NK, P])
        sub_in, sub_tr, sub_cp = sem("sub_in"), sem("sub_tr"), sem("sub_cp")
        iota_ready, sc_zero = sem("iota_ready"), sem("sc_zero")
        sc_done, sc_out, top_ready, cand_ready, fin_ready, eq_ready = [sem("sel%d" % n) for n in range(6)]
        g_sub, g_exp, gw_ready, ijt_done, ijt_out = [sem("gate%d" % n) for n in range(5)]
        oh_ready, g_done, g_out, g_stored = [sem("gmat%d" % n) for n in range(4)]

        UB = BASE + 2 * XB
        acc = at("acc", UB, [P, KC, T])
        ut_hi = at("ut_hi", UB + XB, [P, 2, KC, P], FR)
        ut_lo = at("ut_lo", UB + XB + 16384, [P, 2, KC, P], FR)
        u_raw = at("u_raw", UB + XB + 32768, [P, 2, D])
        v_hi = at("v_hi", UB + XB + 49152, [P, 2, D], FR)
        v_raw = at("v_raw", UB + XB + 65536, [P, 2, D])
        v_lo = at("v_lo", UB + XB + 65536, [P, 2, D], FR)
        p_hi = at("p_hi", UB + XB + 81920, [P, 2, 2, T], FR)
        p_lo = at("p_lo", UB + XB + 81920 + 8704, [P, 2, 2, T], FR)
        g2 = at("g2", UB + XB + 81920 + 17408, [P, 2, T])
        ge = at("ge", UB + XB + 81920 + 21760, [P, T])
        ident2 = at("ident2", UB + XB + 81920 + 23936, [P, P])
        mean3 = at("mean3", UB + XB + 81920 + 24448, [P, P])
        ln3_g = at("ln3_g", UB + XB + 81920 + 24960, [P, KC])
        ln3_b = at("ln3_b", UB + XB + 81920 + 25024, [P, KC])
        tables_free, acc_zero, id2_ready, ln3_in = sem("tables_free"), sem("acc_zero"), sem("id2_ready"), sem("ln3_in")
        u_in = [sem("u_in0"), sem("u_in1")]
        v_in = [sem("v_in0"), sem("v_in1")]
        g_in = sem("g_in")
        t_done, t_hi, t_lo = sem("t_done"), sem("t_hi"), sem("t_lo")
        u_done, ge_done, gm_done, ph_done, pl_done = [sem("act%d" % n) for n in range(5)]
        vh_done, vl_done = sem("vh_done"), sem("vl_done")
        vd_done, acc_done = sem("vd_done"), sem("acc_done")
        res = at("res", UB, [P, 2, NT, 4, P])
        ress = at("ress", UB + 16384, [NS, 2, 4, P])
        o_a, o_d = sem("o_a"), sem("o_d")
        o_out = [sem("o_out0"), sem("o_out1")]

        @block.sync
        def _(sp):
            def rows_load(n):
                src, rn = row_tiles[n][:2]
                if n >= 3:
                    sp.wait_ge(tr_done, NG * (n - 2))
                sp.dma_start(rows[0:rn, n % 3, :], src).then_inc(row_in[n % 3], 16)

            def panel_load(view, c0):
                def load(u, c):
                    if not isinstance(u[0], int) or u[0] >= 2:
                        sp.wait_ge(lo_ready, u[0] - 1)
                    sp.dma_start(raw[:, u[1]], view[:, :, c + c0, :]).then_inc(raw_in[u[1]], 16)
                return load

            for n in range(3):
                rows_load(n)
            for c in range(2):
                panel_load(streams[0][1], 0)(num(c), c)
            for n in range(3, len(row_tiles)):
                rows_load(n)
            for u0, view, c0, n in streams:
                load = panel_load(view, c0)
                if u0 == MK0:
                    pairs(sp, u0, n, load, skip_first=2, issued=2)
                elif u0 == MO0:
                    for c in range(2):
                        load(num(u0 + c), c)
                    sp.wait_ge(panel_done, WO0 + 16)
                    for b in range(DB):
                        if b >= 2:
                            sp.wait_ge(kr_tr, AH * (b - 1))
                        sp.dma_start(kv[:, b % 2], a["cache_mem_k"][0, b].rearrange("(t p) h d -> p t (h d)", p=P))\
                            .then_inc(kv_in[b % 2], 16)
                    for b in range(DB):
                        if b < 2:
                            sp.wait_ge(kr_tr, AH * (DB - 1 + b))
                        else:
                            sp.wait_ge(sv_done, b - 1)
                        sp.dma_start(kv[:, b % 2], a["cache_mem_v"][0, b].rearrange("(t p) h d -> p t (h d)", p=P))\
                            .then_inc(kv_in[b % 2], 16)
                        if b == 1:
                            sp.wait_ge(ks_done, DB * AH)
                            for s in range(2):
                                sp.wait_ge(kt_stored[s], 16 * 8)
                                sp.wait_ge(nat_stored[s], 16 * 16)
                            sp.dma_start(ktp[:, :, :], k_scr.rearrange("c p m -> p c m")).then_inc(kp_in, 16)
                            sp.dma_start(vp[:, :, :], o["v"][0, 0].rearrange("(t p) h d -> p t (h d)", p=P))\
                                .then_inc(vp_in, 16)
                    pairs(sp, u0, n, load, skip_first=2, issued=2)
                else:
                    pairs(sp, u0, n, load)
            uv = a["peer_u"][0].rearrange("(i q j) d -> q j i d", q=NPAIR, j=2)
            vv = a["peer_v"][0].rearrange("(i q j) d -> q j i d", q=NPAIR, j=2)
            gv = g_scr.rearrange("i (q j) t -> q i j t", j=2)

            def u_load(q, first=False):
                for j in range(2):
                    if not first:
                        sp.wait_ge(t_done, q * 8 - 4 + 4 * j)
                    sp.dma_start(u_raw[:, j, :], uv[q, j]).then_inc(u_in[j], 16)

            def v_load(q, first=False):
                if not first:
                    sp.wait_ge(vd_done, q * KC)
                for j in range(2):
                    sp.dma_start(v_raw[:, j, :], vv[q, j]).then_inc(v_in[j], 16)

            def g_load(q, first=False):
                if not first:
                    sp.wait_ge(gm_done, q * 2)
                sp.dma_start(g2[:, :, :], gv[q]).then_inc(g_in, 16)

            sp.wait_ge(g_stored, 32 * (NT + 1))
            sp.wait_ge(id2_ready, 1)
            u_load(0, first=True)
            g_load(0, first=True)
            u_load(1)
            g_load(1)
            v_load(0, first=True)
            with sp.Fori(1, NPAIR - 1) as q:
                u_load(q + 1)
                g_load(q + 1)
                v_load(q)
            v_load(NPAIR - 1)

        @block.tensor
        def _(pe):
            mm, turn = nc.tensor.matmul, nc.tensor.transpose
            pe.wait_ge(ident_ready, 3)
            for n in range(len(row_tiles)):
                pe.wait_ge(row_in[n % 3], 16 * (n // 3 + 1))
                rn = row_tiles[n][1]
                for g in range(NG):
                    m = n * NG + g
                    if m >= 2:
                        pe.wait_ge(tr_free, m - 1)
                    for q in range(4):
                        c = 4 * g + q
                        last = turn(pt[m % 2][:, q * P:q * P + rn], rows[0:rn, n % 3, c * P:(c + 1) * P],
                                    ident[0:rn, 0:rn])
                    last.then_inc(tr_done, 1)

            pe.wait_ge(tr_free, NG * len(row_tiles))

            def kv_panel(u, c):
                pe_panel(pe, u, mem_hi, mem_lo, n=MEM)

            def kv_turn(u, c, first=False):
                pe.wait_ge(evacuated, u[0] + 1)
                if not first:
                    pe.wait_ge(kvn_ready, u[0] - 1)
                for m in range(MT):
                    last = turn(pt[u[1]][:, m * P:(m + 1) * P], kvt[:, u[1], m * P:(m + 1) * P], ident[:, :])
                last.then_inc(kvt_done, 1)
            pe_panel(pe, num(0), mem_hi, mem_lo, first=True, n=MEM)
            pe_panel(pe, num(1), mem_hi, mem_lo, first=True, n=MEM)
            kv_turn(num(0), 0, first=True)
            pe_panel(pe, num(2), mem_hi, mem_lo, n=MEM)
            kv_turn(num(1), 0, first=True)
            with pe.Fori(1, V0 // 2 - 1) as i:
                for d in range(2):
                    pe_panel(pe, in_loop(0, i, d + 1), mem_hi, mem_lo, n=MEM)
                    kv_turn(in_loop(0, i, d), 0)
            pe_panel(pe, num(V0 - 1), mem_hi, mem_lo, n=MEM)
            kv_turn(num(V0 - 2), 0)
            kv_turn(num(V0 - 1), 0)

            def summed(u0, n, x_hi, x_lo, buf, nm):
                def sums_of(u, c, start=False, stop=False):
                    pe.wait_ge(evacuated, u + 1)
                    for b in range(2):
                        last = mm(pl[:, b, 0:HT], (mean16 if n == 16 else mean8)[:, :],
                                  buf[:, c, b * HT:(b + 1) * HT], start=start, stop=stop)
                    return last
                pe_panel(pe, num(u0), x_hi, x_lo)
                pe_panel(pe, num(u0 + 1), x_hi, x_lo)
                sums_of(u0, 0, start=True)
                with pe.Fori(1, n // 2) as i:
                    for d in range(2):
                        pe_panel(pe, in_loop(u0, i, d), x_hi, x_lo)
                        sums_of(i * 2 + (u0 + d - 1), i * 2 + (d - 1))
                sums_of(u0 + n - 1, n - 1, stop=True).then_inc(nsem["mu"], 1)

            def variance(nm):
                nm.wait(pe, "mu_out", 1)
                for c in range(nm.n):
                    nm.wait(pe, "sq", c + 1)
                    for b in range(2):
                        last = mm(pl[:, b, 0:HT], (mean16 if nm.n == 16 else mean8)[:, :], sq[:, c % 2, b, :],
                                  start=(c == 0), stop=(c == nm.n - 1))
                    last.then_inc(nsem["var"], 1)

            pe.wait_ge(ws_in, 16)
            for h in range(SH):
                if h >= 2:
                    pe.wait_ge(ws_cp, h - 1)
                else:
                    pe.wait_ge(kvn_ready, V0)
                turn(pt[h % 2][:, 0:P], ws_n[:, h, :], ident[:, :]).then_inc(ws_tr, 1)
            summed(V0, 8, h_hi, h_lo, vt, sgu_norm)
            variance(sgu_norm)
            pe.wait_ge(ws_ready, 1)
            pe.wait_ge(ws_sin, 16 * DB)
            for h in range(SH + 1):
                if h < SH:
                    sgu_norm.wait(pe, "ya", h + 1)
                    if h >= 1:
                        pe.wait_ge(vn_ready, h)
                    for t in range(NT):
                        turn(pt[0][:, t * P:(t + 1) * P], ya[:, h % 2, t * P:(t + 1) * P], ident[:, :])
                    turn(pt[1][0:NS, 0:P], ya[:, h % 2, SEQ:T], ident[:, :]).then_inc(nsem["used"], 1)
                if h >= 1:
                    k = h - 1
                    pe.wait_ge(vn_ready, h)
                    if k >= 2:
                        pe.wait_ge(st_ready, k - 1)
                    for t in range(NT):
                        mm(pp[k % 2][:, 0, t * P:(t + 1) * P], vn[:, k % 2, t, :], ws_t[:, k, :], start=True, stop=True)
                    mm(pp[k % 2][:, 1, 0:NS], vns[:, k, :], ws_s[:, k, :], start=True, stop=True).then_inc(s_done, 1)
            pe.wait_ge(st_ready, SH)
            pairs(pe, U0, 8, lambda u, c: pe_panel(pe, u, h_hi, h_lo))
            pe.wait_ge(cp_in, 16)
            for g in range(4):
                pe_panel(pe, num(A0 + 2 * g), h_hi, h_lo)
                pe_panel(pe, num(A0 + 2 * g + 1), h_hi, h_lo)
                pe.wait_ge(evacuated, A0 + 2 * g + 2)
                if g >= 1:
                    pe.wait_ge(pp_lo, 2 * g)
                for c in range(2):
                    turn(pt[0][:, c * P:c * P + DB * STATE], cpn[:, (2 * g + c) * P:(2 * g + c + 1) * P],
                         ident[0:DB * STATE, 0:DB * STATE])
                    last = turn(pt[1][0:STATE + NS, c * P:(c + 1) * P], dp[:, c, SEQ - STATE:T], ident[:, :])
                last.then_inc(at_done, 1)
                pe.wait_ge(d_ready, g + 1)
                pe.wait_ge(an_ready, g + 1)
                pe.wait_ge(pw_in, 16 * (g + 1))
                for c in range(2):
                    for b in range(2):
                        out = pl[:, b, 0:HT] if c == 0 else pt[b][:, 0:HT]
                        for k in range(2):
                            last = mm(out, pw[:, k, c * P:(c + 1) * P], dp[:, k, b * HT:(b + 1) * HT],
                                      start=(k == 0), stop=(k == 1))
                last.then_inc(pm_done, 1)
            pe.wait_ge(pp_lo, 8)
            pe.wait_ge(ysp_lo, 8)
            summed(WO0, 16, y_hi, y_lo, r, norm1)
            variance(norm1)
            norm1.wait(pe, "used", KC)
            pairs(pe, MQ0, 16, lambda u, c: pe_panel(pe, u, h_hi, h_lo))
            pe.wait_ge(qm_ready, 1)
            pe.wait_ge(evacuated, MO0)
            for n in range(DB * AH + 1):
                if n < DB * AH:
                    b, h = n // AH, n % AH
                    if h == 0:
                        pe.wait_ge(kv_in[b % 2], 16 * (b // 2 + 1))
                    if n >= 1:
                        pe.wait_ge(kr_a, n)
                        pe.wait_ge(kr_d, n)
                    for c in range(4):
                        for m in range(MT):
                            last = turn(pt[c // 2][:, (c % 2) * MEM + m * P:(c % 2) * MEM + (m + 1) * P],
                                        kv[:, b % 2, m, (4 * h + c) * P:(4 * h + c + 1) * P], ident[:, :])
                    last.then_inc(kr_tr, 1)
                if n >= 1:
                    b, h = (n - 1) // AH, (n - 1) % AH
                    pe.wait_ge(kr_a, n)
                    pe.wait_ge(kr_d, n)
                    for c in range(4):
                        last = mm(pp[h // 2][0:NS, h % 2, 0:MEM], qm[:, 4 * h + c, NS * b:NS * (b + 1)],
                                  kr[:, (n - 1) % 3, c, :], start=(b == 0 and c == 0), stop=(b == DB - 1 and c == 3))
                    last.then_inc(ks_done, 1)
            pe.wait_ge(ss_p, 1)
            for m in range(AH * MT):
                last = turn(pt[0][:, m * NS:(m + 1) * NS], ssm[:, m // MT, (m % MT) * P:(m % MT + 1) * P],
                            ident[0:NS, 0:NS])
            last.then_inc(ss_tr, 1)
            pe.wait_ge(ss_pt, 1)
            for b in range(DB):
                pe.wait_ge(kv_in[b % 2], 16 * (b // 2 + 5))
                for c in range(KC):
                    for m in range(MT):
                        last = mm(pl[:, 0, c * NS + DS * b:c * NS + DS * (b + 1)],
                                  kv[:, b % 2, m, c * P:(c + 1) * P], pts[:, (c // 4) * MT + m, DS * b:DS * (b + 1)],
                                  start=(m == 0), stop=(m == MT - 1))
                last.then_inc(sv_done, 1)
            pe.wait_ge(kp_in, 16)
            pe.wait_ge(ss_exp, AH)
            for n in range(AH * NT + 2):
                if n < AH * NT:
                    h, t = n // NT, n % NT
                    if n >= 4:
                        pe.wait_ge(ps_exp, n - 3)
                    for c in range(4):
                        last = mm(pp[n // 2 % 2][:, n % 2, 0:MEM], qt[:, 4 * h + c, t * P:(t + 1) * P],
                                  ktp[:, 4 * h + c, :], start=(c == 0), stop=(c == 3))
                    last.then_inc(ps_done, 1)
                if n >= 2:
                    k = n - 2
                    h, t = k // NT, k % NT
                    pe.wait_ge(ps_p, k + 1)
                    if k >= 2:
                        pe.wait_ge(ps_pt, k - 1)
                    for m in range(MT):
                        last = turn(pt[k % 2][:, m * P:(m + 1) * P], pr[:, k % 2, m * P:(m + 1) * P], ident[:, :])
                    last.then_inc(ps_tr, 1)
                    if t == NT - 1:
                        pe.wait_ge(ps_pt, k + 1)
                        pe.wait_ge(vp_in, 16)
                        for c in range(4):
                            m0 = 4 * h + c
                            if m0 == 0:
                                pe.wait_ge(so_lo, 1)
                            if m0 >= 2:
                                pe.wait_ge(po_lo, m0 - 1)
                            for m in range(MT):
                                last = mm(pl[:, m0 % 2, :], vp[:, m, m0 * P:(m0 + 1) * P], ptt[:, h % 2, m, :],
                                          start=(m == 0), stop=(m == MT - 1))
                            last.then_inc(pv_done, 1)
            pe.wait_ge(po_lo, KC)
            summed(MO0, 16, y_hi, y_lo, r, norm2)
            variance(norm2)
            pe.wait_ge(sub_in, 16)
            for p in range(2):
                last = turn(pt[0][:, p * P:(p + 1) * P], sub_n[:, p, :], ident[:, :])
            last.then_inc(sub_tr, 1)
            norm2.wait(pe, "used", KC)
            pe.wait_ge(sub_cp, 1)

            def select_scores(u, s, first=False):
                pe.wait_ge(evacuated, u + 1)
                if not first:
                    pe.wait_ge(sc_out, u - WQ0)
                for t in range(NT):
                    mm(pl[:, 0, t * P:(t + 1) * P], q2[:, s, t * P:(t + 1) * P], sub_t[:, s, :], start=True, stop=True)
                mm(pl[0:NS, 1, 0:P], q2[:, s, SEQ:T], sub_t[:, s, :], start=True, stop=True).then_inc(sc_done, 1)
            pe_panel(pe, num(WQ0), h_hi, h_lo)
            pe_panel(pe, num(WQ0 + 1), h_hi, h_lo)
            select_scores(WQ0, 0, first=True)
            with pe.Fori(1, 8) as i:
                for d in range(2):
                    pe_panel(pe, in_loop(WQ0, i, d), h_hi, h_lo)
                    select_scores(i * 2 + (WQ0 + d - 1), (d + 1) % 2)
            select_scores(NPANEL - 1, 1)
            pe.wait_ge(gw_ready, 1)
            pe.wait_ge(evacuated, NPANEL)
            for x in range(3):
                dst = (pp[0], pp[1], pl)[x]
                src = gw if x == 2 else ij[:, x]
                for t in range(NT):
                    turn(dst[:, 0, t * P:(t + 1) * P], src[:, t, :], ident[:, :])
                turn(dst[:, 1, 0:NS], src[0:NS, NT, :], ident[0:NS, 0:NS]).then_inc(ijt_done, 1)
            def gate_matrix(n, s, first=False):
                pe.wait_ge(oh_ready, n + 1)
                if not first:
                    pe.wait_ge(g_out, n - 1)
                for q in range(4):
                    last = mm(pt[s][:, q * P:(q + 1) * P], oh[:, s, 0, q, :], oh[:, s, 1, q, :], start=True, stop=True)
                last.then_inc(g_done, 1)
            for n in range(2):
                gate_matrix(n, n, first=True)
            with pe.Fori(1, T // 8) as i:
                for s in range(2):
                    gate_matrix(i * 2 + s, s)

            def turn_rows(q, g):
                j, c0 = g // 4, 4 * (g % 4)
                if g % 4 == 0:
                    pe.wait_ge(u_in[j], q * 16 + 16)
                if isinstance(q, int) and q == 0 and g < 2:
                    pe.wait_ge(g_out, T // 4)
                else:
                    pe.wait_ge(t_lo, q * 8 + (g - 1))
                for c in range(4):
                    last = turn(pt[g % 2][:, c * P:(c + 1) * P], u_raw[:, j, (c0 + c) * P:(c0 + c + 1) * P], ident2[:, :])
                last.then_inc(t_done, 1)

            def scores_of(q, j):
                pe.wait_ge(t_lo, q * 8 + 4 * (j + 1))
                for k in range(KC):
                    for w, x in ((ut_hi, h_hi), (ut_hi, h_lo), (ut_lo, h_hi)):
                        for b in range(2):
                            last = mm(pp[j][:, b, 0:HT], w[:, j, k, :], x[:, k, b * HT:(b + 1) * HT],
                                      start=(k == 0 and w is ut_hi and x is h_hi), stop=(k == KC - 1 and w is ut_lo))
                last.then_inc(u_done, 1)

            def values_of(q, c, par):
                if c < 2:
                    pe.wait_ge(pl_done, q * 2 + 2)
                    pe.wait_ge(vl_done, q * 2 + 2)
                    if isinstance(q, int) and q == NPAIR - 1:
                        pe.wait_ge(acc_done, q * KC)
                    else:
                        pe.wait_ge(ge_done, q * 2 + (3 + c))
                else:
                    pe.wait_ge(acc_done, q * KC + (c - 1))
                for j in range(2):
                    for w, x in ((v_hi, p_hi), (v_hi, p_lo), (v_lo, p_hi)):
                        for b in range(2):
                            last = mm(pp[c % 2][:, b, 0:HT], w[:, j, c * P:(c + 1) * P],
                                      x[:, par, j, b * HT:(b + 1) * HT],
                                      start=(j == 0 and w is v_hi and x is p_hi), stop=(j == 1 and w is v_lo))
                last.then_inc(vd_done, 1)

            def pair_step(q, par, more=True):
                for j in range(2):
                    scores_wait(q, j)
                    scores_of(q, j)
                for g in range(8):
                    values_of(q - 1, 2 * g, 1 - par)
                    values_of(q - 1, 2 * g + 1, 1 - par)
                    if more:
                        turn_rows(q + 1, g)

            def scores_wait(q, j):
                if isinstance(q, int) and q <= 1:
                    if q == 0:
                        pe.wait_ge(ijt_out, 3)
                    else:
                        pe.wait_ge(ge_done, j + 1)
                    return
                pe.wait_ge(acc_done, q * KC - KC - 1 + j)

            pe.wait_ge(id2_ready, 2)
            for g in range(8):
                turn_rows(0, g)
            for j in range(2):
                scores_wait(0, j)
                scores_of(0, j)
            for g in range(8):
                turn_rows(1, g)
            pair_step(1, 1)
            with pe.Fori(1, NPAIR // 2 - 1) as i:
                for par in range(2):
                    pair_step(i * 2 + par, par)
            pair_step(NPAIR - 2, 0)
            pair_step(NPAIR - 1, 1, more=False)
            for c in range(KC):
                values_of(NPAIR - 1, c, 1)
            for c in range(KC):
                norm3.wait(pe, "hi", c + 1)
                for b in range(2):
                    last = mm(pl[:, b, 0:HT], mean3[:, :], r[:, c, b * HT:(b + 1) * HT], start=(c == 0), stop=(c == KC - 1))
            last.then_inc(nsem["mu"], 1)
            norm3.wait(pe, "mu_out", 1)
            for c in range(KC):
                norm3.wait(pe, "sq", c + 1)
                for b in range(2):
                    last = mm(pl[:, b, 0:HT], mean3[:, :], sq[:, c % 2, b, :], start=(c == 0), stop=(c == KC - 1))
                last.then_inc(nsem["var"], 1)
            for c in range(KC):
                norm3.wait(pe, "ya", c + 1)
                if c >= 2:
                    pe.wait_ge(o_a, c - 1)
                    pe.wait_ge(o_d, c - 1)
                for t in range(NT):
                    turn(pp[c % 2][:, 0, t * P:(t + 1) * P], ya[:, c % 2, t * P:(t + 1) * P], ident2[:, :])
                turn(pp[c % 2][0:NS, 1, 0:P], ya[:, c % 2, SEQ:T], ident2[:, :]).then_inc(nsem["used"], 1)

        @block.scalar
        def _(act):
            f = nc.scalar.activation

            def next_split(u):
                if isinstance(u[0], int):
                    act_split(act, num(u[0] + 1), first=u[0] + 1 < 2)
                else:
                    v = u[0] + 1
                    act_split(act, (v, 1 - u[1], u[2] + 16 * u[1]))

            def panel(use, split=True):
                def body(u, c):
                    if split:
                        next_split(u)
                    act.wait_ge(panel_done, u[0] + 1)
                    use(u, c)
                return body

            for m in range(NG * len(row_tiles)):
                act.wait_ge(tr_done, m + 1)
                ps, hi = row_views(m, 0)
                f(hi, ps, ACT.Copy).then_inc(tr_hi, 1)
            act_split(act, num(0), first=True)

            for k in range(2):
                def kv_use(u, c, k=k):
                    if not isinstance(u[0], int) or u[0] >= 2:
                        act.wait_ge(kvt_done, u[0] - 1)
                        if k == 0 or (isinstance(u[0], int) and u[0] < V0 // 2 + 2):
                            act.wait_ge(kt_stored[u[1]], (u[2] - 16) if k == 0 else 16 * 8)
                    f(kvt[:, u[1], :], pp[u[1]][:, 0, 0:MEM], ACT.Copy).then_inc(evacuated, 1)
                pairs(act, k * 16, 16, panel(kv_use), skip_first=2)

            def vt_use(u, c):
                f(vt[:, c, :].rearrange("p (b t) -> p b t", b=2), pp[u[1]][:, :, 0:HT],
                  ACT.Gelu_apprx_tanh).then_inc(evacuated, 1)
            act.wait_ge(kvn_ready, V0)
            for h in range(SH):
                act.wait_ge(ws_tr, h + 1)
                f(ws_t[:, h, :], pt[h % 2][:, 0:P], ACT.Copy).then_inc(ws_cp, 1)
            pairs(act, V0, 8, panel(vt_use))
            for k in range(2):
                act.wait_ge(nat_stored[k], 16 * V0 // 2)
            act.wait_ge(const_in, 16 * 7)
            act_norm(act, sgu_norm, sln_g, sln_b, vt)

            def u_use(u, c):
                if not isinstance(u[0], int) or c >= 2:
                    act.wait_ge(y_ready, c - 1)
                f(ug[:, u[1], :].rearrange("p (b t) -> p b t", b=2), pp[u[1]][:, :, 0:HT],
                  ACT.Gelu_apprx_tanh).then_inc(evacuated, 1)
                act.wait_ge(y_ready, c + 1)
                f(y_hi[:, c + SH, :], yf[:, u[1], :], ACT.Copy).then_inc(ysp_hi, 1)
            act.wait_ge(st_ready, SH)
            pairs(act, U0, 8, panel(u_use), skip_first=2)

            for g in range(4):
                for c in range(2):
                    def a_use(u, _, c=c):
                        if g == 0 and c == 0:
                            act.wait_ge(ysp_lo, SH)
                        if g >= 1:
                            act.wait_ge(pm_done, g)
                        f(dp[:, c, :].rearrange("p (b t) -> p b t", b=2), pp[u[1]][:, :, 0:HT], ACT.Copy)\
                            .then_inc(evacuated, 1)
                    panel(a_use)(num(A0 + 2 * g + c), 0)
                act.wait_ge(at_done, g + 1)
                if g == 0:
                    act.wait_ge(pool_zero, 2)
                else:
                    act.wait_ge(d_ready, g)
                    act.wait_ge(an_out, 16 * (DB + 1) * g)
                for c in range(2):
                    last = f(es[:, c, :, 1:16], pt[0][:, c * P:c * P + DB * STATE].rearrange("p (b s) -> p b s", b=DB),
                             ACT.Copy)
                last.then_inc(es_ready, 1)
                f(an[:, :, :], pt[1][0:STATE + NS, 0:2 * P].rearrange("p (c n) -> p c n", c=2), ACT.Copy)\
                    .then_inc(an_ready, 1)
                act.wait_ge(pm_done, g + 1)
                for c in range(2):
                    if c == 0:
                        f(yp[:, 0, :].rearrange("p (b t) -> p b t", b=2), pl[:, :, 0:HT], ACT.Copy,
                          scale=pscale[:, 2 * g:2 * g + 1]).then_inc(yp_ready, 1)
                    else:
                        for b in range(2):
                            last = f(yp[:, 1, b * HT:(b + 1) * HT], pt[b][:, 0:HT], ACT.Copy,
                                     scale=pscale[:, 2 * g + 1:2 * g + 2])
                        last.then_inc(yp_ready, 1)
                for c in range(2):
                    act.wait_ge(yp_ready, 2 * g + c + 1)
                    f(y_hi[:, 2 * g + c, :], yp[:, c, :], ACT.Copy).then_inc(pp_hi, 1)
            pairs(act, WO0, 16, lambda u, c: next_split(u))
            act_norm(act, norm1, ln_g[:, 0, :], ln_b[:, 0, :], r, h_hi)

            def q_use(u, c):
                f(qt[:, c, :].rearrange("p (b t) -> p b t", b=2), pp[u[1]][:, :, 0:HT], ACT.Copy).then_inc(evacuated, 1)
            pairs(act, MQ0, 14, panel(q_use))
            panel(q_use)(num(MQ0 + 14), 14)
            panel(q_use, split=False)(num(MQ0 + 15), 15)

            act.wait_ge(qm_ready, 1)
            for n in range(DB * AH):
                act.wait_ge(kr_tr, n + 1)
                if n >= 3:
                    act.wait_ge(ks_done, n - 2)
                f(kr[:, n % 3, 0:2, :], pt[0][:, :].rearrange("p (c m) -> p c m", c=2), ACT.Copy).then_inc(kr_a, 1)
            act.wait_ge(ss_max, 1)
            for h in range(AH):
                f(ssm[:, h, :], pp[h // 2][0:NS, h % 2, 0:MEM], ACT.Exp, bias=smx[:, 1, h:h + 1], scale=ASCALE,
                  accum_out=smx[:, 2, h:h + 1]).then_inc(ss_exp, 1)
            act.wait_ge(ss_tr, 1)
            f(pts[:, :, :], pt[0][:, 0:AH * MT * NS].rearrange("p (m t) -> p m t", t=NS), ACT.Copy).then_inc(ss_pt, 1)
            act.wait_ge(sv_done, DB)
            f(y_hi[:, :, SEQ:T], pl[:, 0, :].rearrange("p (c t) -> p c t", c=KC), ACT.Copy).then_inc(so_hi, 1)
            for n in range(AH * NT + 2):
                if n < AH * NT:
                    act.wait_ge(ps_max, n + 1)
                    if n >= 2:
                        act.wait_ge(ps_tr, n - 1)
                    f(pr[:, n % 2, :], pp[n // 2 % 2][:, n % 2, 0:MEM], ACT.Exp, bias=pst[:, n % 2, 1:2], scale=ASCALE,
                      accum_out=pst[:, n % 2, 2:3]).then_inc(ps_exp, 1)
                if n >= 2:
                    k = n - 2
                    h, t = k // NT, k % NT
                    act.wait_ge(ps_tr, k + 1)
                    if h >= 2:
                        act.wait_ge(pv_done, 4 * (h - 1))
                    f(ptt[:, h % 2, :, t * P:(t + 1) * P], pt[k % 2][:, 0:MEM].rearrange("p (m t) -> p m t", m=MT),
                      ACT.Copy).then_inc(ps_pt, 1)
                    if t == NT - 1:
                        for c in range(4):
                            act.wait_ge(pv_done, 4 * h + c + 1)
                            f(y_hi[:, 4 * h + c, 0:SEQ], pl[:, c % 2, :], ACT.Copy).then_inc(po_hi, 1)
            act.wait_ge(pv_done, KC)
            act_split(act, num(MO0))
            pairs(act, MO0, 16, lambda u, c: next_split(u))
            act_norm(act, norm2, ln_g[:, 1, :], ln_b[:, 1, :], r, h_hi)

            act.wait_ge(sub_tr, 1)
            f(sub_t[:, :, :], pt[0][:, 0:2 * P].rearrange("p (c n) -> p c n", c=2), ACT.Copy).then_inc(sub_cp, 1)

            def scores_out(c, s):
                act.wait_ge(sc_done, c + 1)
                if not isinstance(c, int) or c >= 2:
                    act.wait_ge(top_ready, c - 1)
                f(sc[:, s, 0:NT, :], pl[:, 0, :].rearrange("p (t k) -> p t k", t=NT), ACT.Copy)
                f(sc[0:NS, s, NT, :], pl[0:NS, 1, 0:P], ACT.Copy).then_inc(sc_out, 1)

            def wq_use(u, c):
                if not isinstance(u[0], int) or c >= 2:
                    act.wait_ge(sc_done, c - 1)
                f(q2[:, u[1], :].rearrange("p (b t) -> p b t", b=2), pp[u[1]][:, :, 0:HT], ACT.Copy).then_inc(evacuated, 1)
                if not isinstance(u[0], int) or c >= 1:
                    scores_out(c - 1, 1 - u[1])
            act.wait_ge(sc_zero, 1)
            pairs(act, WQ0, 14, panel(wq_use), skip_first=2)
            panel(wq_use)(num(NPANEL - 2), 14)
            panel(wq_use, split=False)(num(NPANEL - 1), 15)
            scores_out(15, 1)
            act.wait_ge(g_sub, 1)
            f(gw[:, :, :], gw[:, :, :], ACT.Exp).then_inc(g_exp, 1)
            for x in range(3):
                act.wait_ge(ijt_done, x + 1)
                src = (pp[0], pp[1], pl)[x]
                f(ijt[:, x, 0:SEQ], src[:, 0, :], ACT.Copy)
                f(ijt[:, x, SEQ:T], src[:, 1, 0:NS], ACT.Copy).then_inc(ijt_out, 1)
            for t in range(NT + 1):
                if t >= 1:
                    act.wait_ge(g_stored, 32 * t)
                n0 = t * (P // 4)
                with act.Fori(0, (P if t < NT else NS) // 8) as i:
                    for s in range(2):
                        act.wait_ge(g_done, i * 2 + (n0 + s + 1))
                        f(gs[:, :, bass.ds(i * 8 + 4 * s, 4)].rearrange("p j t -> p t j"),
                          pt[s][:, :].rearrange("p (t j) -> p t j", t=4), ACT.Copy).then_inc(g_out, 1)

            def rows_hi(q, g):
                act.wait_ge(t_done, q * 8 + (g + 1))
                if not (isinstance(q, int) and q == 0):
                    act.wait_ge(u_done, q * 2)
                f(ut_hi[:, g // 4, 4 * (g % 4):4 * (g % 4) + 4, :], pt[g % 2][:, :].rearrange("p (c i) -> p c i", c=4),
                  ACT.Copy).then_inc(t_hi, 1)

            def v_split(q, count):
                for j in range(2):
                    act.wait_ge(v_in[j], count)
                    if not (isinstance(q, int) and q == 0):
                        act.wait_ge(vd_done, q * KC)
                    f(v_hi[:, j, :], v_raw[:, j, :], ACT.Copy).then_inc(vh_done, 1)

            def gelu_pair(q, par):
                for j in range(2):
                    act.wait_ge(u_done, q * 2 + (j + 1))
                    if not (isinstance(q, int) and q == 0 and j == 0):
                        act.wait_ge(pl_done, q * 2 + j)
                    f(ge[:, :].rearrange("p (b t) -> p b t", b=2), pp[j][:, :, 0:HT], ACT.Gelu_apprx_tanh)\
                        .then_inc(ge_done, 1)
                    act.wait_ge(gm_done, q * 2 + (j + 1))
                    if not isinstance(q, int) or q >= 2:
                        act.wait_ge(vd_done, (q - 1) * KC)
                    f(p_hi[:, par, j, :], ge[:, :], ACT.Copy).then_inc(ph_done, 1)

            for g in range(8):
                rows_hi(0, g)
            gelu_pair(0, 0)
            for g in range(8):
                rows_hi(1, g)

            def act_pair(q, par, more=True):
                v_split(q - 1, q * 16)
                gelu_pair(q, par)
                if more:
                    for g in range(8):
                        rows_hi(q + 1, g)
            act_pair(1, 1)
            with act.Fori(1, NPAIR // 2 - 1) as i:
                for par in range(2):
                    act_pair(i * 2 + par, par)
            act_pair(NPAIR - 2, 0)
            act_pair(NPAIR - 1, 1, more=False)
            v_split(NPAIR - 1, NPAIR * 16)


            def prompt_rows(c):
                if c >= 1:
                    k = c - 1
                    norm3.wait(act, "used", c)
                    if k >= 8 and k % 4 == 0:
                        act.wait_ge(o_out[k // 4 % 2], 32)
                    f(res[:, k // 4 % 2, :, k % 4, :], pp[k % 2][:, 0, :].rearrange("p (t n) -> p t n", t=NT),
                      ACT.Copy).then_inc(o_a, 1)
            act.wait_ge(ln3_in, 32)
            act_norm(act, norm3, ln3_g, ln3_b, r, after=prompt_rows)

        @block.vector
        def _(dve):
            tt, ts, stt, copy = (nc.vector.tensor_tensor, nc.vector.tensor_scalar,
                                 nc.vector.scalar_tensor_tensor, nc.vector.tensor_copy)

            def split_next(u):
                dve_split(dve, (u[0] + 1, 1 - u[1], None))

            dve.wait_ge(const_ready, 1)
            for w, n in enumerate(WINDOWS):
                ts(inv_n[:, w, :], cnt[:, :], float(n), None, ALU.min)
            dve.drain()
            nc.vector.reciprocal(inv_n[:, :, :], inv_n[:, :, :])
            for m in range(NG * len(row_tiles)):
                dve.wait_ge(tr_hi, m + 1)
                ps, hi = row_views(m, 0)
                _, lo = row_views(m, 1)
                tt(lo, ps, hi.bitcast(F32), ALU.subtract).then_inc(tr_free, 1)
            dve_split(dve, num(0))

            def kv_use(u, c):
                split_next(u)
                dve.wait_ge(kvt_done, u[0] + 1)
                if not isinstance(u[0], int) or u[0] >= 2:
                    dve.wait_ge(nat_stored[u[1]], u[2] - 16)
                copy(kvn[:, u[1]], pt[u[1]][:, 0:MEM].rearrange("p (m n) -> p m n", m=MT)).then_inc(kvn_ready, 1)
            pairs(dve, 0, V0, kv_use, skip_first=2)

            pairs(dve, V0, 8, lambda u, c: split_next(u))

            def gate_of_head(c):
                if 1 <= c <= SH:
                    h = c - 1
                    sgu_norm.wait(dve, "used", c)
                    if h >= 2:
                        dve.wait_ge(s_done, h - 1)
                    copy(vn[:, h % 2], pt[0][:, :].rearrange("p (t d) -> p t d", t=NT))
                    copy(vns[:, h, :], pt[1][0:NS, 0:P]).then_inc(vn_ready, 1)
                if c >= 2:
                    h = c - 2
                    dve.wait_ge(s_done, h + 1)
                    tt(st[:, h, 0:SEQ].rearrange("p (t i) -> p t i", t=NT), pp[h % 2][:, 0, :].rearrange("p (t i) -> p t i", t=NT),
                       sgu_bias[:, h:h + 1, :].to_broadcast([P, NT, P]), ALU.add)
                    tt(st[:, h, SEQ:T].rearrange("p (b i) -> p b i", b=DB),
                       pp[h % 2][:, 1, 0:NS].rearrange("p (b i) -> p b i", b=DB),
                       sgu_bias[:, h:h + 1, 0:DS].to_broadcast([P, DB, DS]), ALU.add).then_inc(st_ready, 1)
            dve.wait_ge(bias_in, 16)
            dve_norm(dve, sgu_norm, vt, after=gate_of_head)

            def u_use(u, c):
                split_next(u)
                dve.wait_ge(evacuated, u[0] + 1)
                if not isinstance(u[0], int) or c >= 2:
                    dve.wait_ge(ysp_hi, c - 1)
                tt(yf[:, u[1], :], ug[:, u[1], :], st[:, c, :], ALU.mult).then_inc(y_ready, 1)
                dve.wait_ge(ysp_hi, c + 1)
                tt(y_lo[:, c + SH, :], yf[:, u[1], :], y_hi[:, c + SH, :].bitcast(F32), ALU.subtract).then_inc(ysp_lo, 1)
            dve.drain()
            pairs(dve, U0, 8, u_use, skip_first=2)

            for g, w in enumerate(WINDOWS):
                split_next(num(A0 + 2 * g))
                split_next(num(A0 + 2 * g + 1))
                dve.wait_ge(ep_ready, g + 1)
                dve.wait_ge(es_ready, g + 1)
                src, srcs = ep, es
                step, n = 1, 0
                while step < w:
                    dst, dsts = ((fa, fas), (fb, fbs))[n % 2]
                    lo = 2 * step - 1
                    tt(dst[:, :, lo:], src[:, :, lo:], src[:, :, lo - step:16 + SEQ - step], ALU.add)
                    tt(dsts[:, :, :, lo:], srcs[:, :, :, lo:], srcs[:, :, :, lo - step:20 - step], ALU.add)
                    dve.drain()
                    src, srcs, step, n = dst, dsts, 2 * step, n + 1
                for c in range(2):
                    stt(dp[:, c, SEQ:T].rearrange("p (b s) -> p b s", b=DB), srcs[:, c, :, 16:20], 1.0 / w,
                        es[:, c, :, 16:20], ALU.mult, ALU.subtract)
                stt(dp[:, :, 16:SEQ], src[:, :, 32:], 1.0 / w, ep[:, :, 32:], ALU.mult, ALU.subtract)
                tt(dp[:, :, 0:16], src[:, :, 16:32], inv_n[:, g:g + 1, :].to_broadcast([P, 2, 16]), ALU.mult)
                dve.drain()
                tt(dp[:, :, 0:16], dp[:, :, 0:16], ep[:, :, 16:32], ALU.subtract).then_inc(d_ready, 1)
                for c in range(2):
                    dve.wait_ge(pp_hi, 2 * g + c + 1)
                    if g == 3 and c == 1:
                        dve.wait_ge(pm_done, 4)
                    tt(y_lo[:, 2 * g + c, :], yp[:, c, :], y_hi[:, 2 * g + c, :].bitcast(F32), ALU.subtract)\
                        .then_inc(pp_lo, 1)

            def residual(u, c, free=None):
                split_next(u)
                dve.wait_ge(panel_done, u[0] + 1)
                tt(yt[:, u[1], :], h_hi[:, c, :].bitcast(F32), h_lo[:, c, :].bitcast(F32), ALU.add)
                dve.drain()
                stt(r[:, c, :].rearrange("p (b t) -> p b t", b=2), yt[:, u[1], :].rearrange("p (b t) -> p b t", b=2),
                    ALPHA, pp[u[1]][:, :, 0:HT], ALU.mult, ALU.add).then_inc(evacuated, 1)
            dve.drain()
            pairs(dve, WO0, 16, residual)
            dve_norm(dve, norm1, r, h_lo, h_hi)
            pairs(dve, MQ0, 14, lambda u, c: split_next(u))
            split_next(num(MQ0 + 14))

            dve.wait_ge(qm_zero, 1)
            dve.wait_ge(evacuated, MO0)
            copy(qm[:, :, :].rearrange("p c (b x) -> p c b x", x=36)[:, :, :, 0:DS],
                 qt[:, :, SEQ:T].rearrange("p c (b s) -> p c b s", b=DB)).then_inc(qm_ready, 1)
            for n in range(DB * AH):
                dve.wait_ge(kr_tr, n + 1)
                if n >= 3:
                    dve.wait_ge(ks_done, n - 2)
                copy(kr[:, n % 3, 2:4, :], pt[1][:, :].rearrange("p (c m) -> p c m", c=2)).then_inc(kr_d, 1)
            dve.wait_ge(ks_done, DB * AH)
            for h in range(AH):
                nc.vector.tensor_reduce(smx[:, 0, h:h + 1], pp[h // 2][0:NS, h % 2, 0:MEM], AX.X, ALU.max)
            dve.drain()
            ts(smx[:, 1, :], smx[:, 0, :], -ASCALE, None, ALU.mult).then_inc(ss_max, 1)
            dve.wait_ge(ss_exp, AH)
            nc.vector.reciprocal(smx[:, 3, :], smx[:, 2, :])
            dve.drain()
            for h in range(AH):
                last = ts(ssm[:, h, :], ssm[:, h, :], smx[:, 3, h:h + 1], None, ALU.mult)
            last.then_inc(ss_p, 1)
            dve.wait_ge(so_hi, 1)
            tt(y_lo[:, :, SEQ:T], pl[:, 0, :].rearrange("p (c t) -> p c t", c=KC), y_hi[:, :, SEQ:T].bitcast(F32),
               ALU.subtract).then_inc(so_lo, 1)
            for n in range(AH * NT + 2):
                if n < AH * NT:
                    dve.wait_ge(ps_done, n + 1)
                    if n >= 2:
                        dve.wait_ge(ps_exp, n - 1)
                    nc.vector.tensor_reduce(pst[:, n % 2, 0:1], pp[n // 2 % 2][:, n % 2, 0:MEM], AX.X, ALU.max)
                    dve.drain()
                    ts(pst[:, n % 2, 1:2], pst[:, n % 2, 0:1], -ASCALE, None, ALU.mult).then_inc(ps_max, 1)
                    dve.wait_ge(ps_exp, n + 1)
                    nc.vector.reciprocal(pst[:, n % 2, 3:4], pst[:, n % 2, 2:3])
                    dve.drain()
                    ts(pr[:, n % 2, :], pr[:, n % 2, :], pst[:, n % 2, 3:4], None, ALU.mult).then_inc(ps_p, 1)
                if n >= 2 and (n - 2) % NT == NT - 1:
                    h = (n - 2) // NT
                    for c in range(4):
                        dve.wait_ge(po_hi, 4 * h + c + 1)
                        if h == 0 and c == 0:
                            dve.wait_ge(sv_done, DB)
                        tt(y_lo[:, 4 * h + c, 0:SEQ], pl[:, c % 2, :], y_hi[:, 4 * h + c, 0:SEQ].bitcast(F32),
                           ALU.subtract).then_inc(po_lo, 1)
            dve_split(dve, num(MO0))
            pairs(dve, MO0, 16, residual)
            dve_norm(dve, norm2, r, h_lo, h_hi)

            mx, mi, mr = nc.vector.max, nc.vector.max_index, nc.vector.match_replace
            NT1 = NT + 1

            def top16(vals, spare, best, where):
                for t in range(NT1):
                    mx(best[:, t, 0:8], vals[:, t, :])
                dve.drain()
                for t in range(NT1):
                    mi(where[:, t, 0:8], best[:, t, 0:8], vals[:, t, :])
                    mr(spare[:, t, :], best[:, t, 0:8], vals[:, t, :], NEG)
                dve.drain()
                for t in range(NT1):
                    mx(best[:, t, 8:16], spare[:, t, :])
                dve.drain()
                for t in range(NT1):
                    last = mi(where[:, t, 8:16], best[:, t, 8:16], spare[:, t, :])
                return last

            def pick(h):
                dve.wait_ge(cand_ready, h + 1)
                best = gw[:, :, h * TOPK:(h + 1) * TOPK]
                top16(cand, cand2, best, fi)
                dve.drain()
                nc.vector.tensor_single_scalar(ab_u[:, 0], fi[:, :, :], 4, ALU.logical_shift_right)
                nc.vector.tensor_single_scalar(ab_u[:, 1], fi[:, :, :], 15, ALU.bitwise_and)
                dve.drain()
                copy(ab_f[:, h], ab_u[:, :]).then_inc(fin_ready, 1)
                dve.drain()
                if h >= 1:
                    dve.wait_ge(pool_step, PICK_STEPS * h)
                tt(eq[:, :, :, :, :].rearrange("p x t k y -> p (x t k) y"),
                   iota16[:, :].rearrange("p (n y) -> p n y", n=1).to_broadcast([P, 2 * NT1 * TOPK, TOPK]),
                   ab_f[:, h].rearrange("p x t (k y) -> p (x t k) y", y=1).to_broadcast([P, 2 * NT1 * TOPK, TOPK]),
                   ALU.is_equal).then_inc(eq_ready, 1)

            for c in range(2 * PH):
                if c < 2 * PH - 1:
                    split_next(num(WQ0 + c))
                dve.wait_ge(sc_out, c + 1)
                h, p = c // 2, c % 2
                top16(sc[:, p], sc2, sv[:, h, p], si[:, h, p]).then_inc(top_ready, 1)
                dve.drain()
                copy(sif[:, h, p], si[:, h, p]).then_inc(sif_ready, 1)
                if p == 1 and h >= 1:
                    pick(h - 1)
            pick(PH - 1)
            dve.drain()
            gw4 = gw[:, :, :].rearrange("p t (h k) -> p (t h) k", k=TOPK)
            copy(sums[:, 0, :], gw4[:, :, 0:1].rearrange("p n k -> p (n k)"))
            dve.drain()
            tt(gw4, gw4, sums[:, 0, :].rearrange("p (n k) -> p n k", k=1).to_broadcast([P, 40, TOPK]), ALU.subtract)\
                .then_inc(g_sub, 1)
            dve.wait_ge(g_exp, 1)
            nc.vector.tensor_reduce(sums[:, 0, :], gw4, AX.X, ALU.add)
            dve.drain()
            nc.vector.reciprocal(sums[:, 1, :], sums[:, 0, :])
            dve.drain()
            tt(gw4, gw4, sums[:, 1, :].rearrange("p (n k) -> p n k", k=1).to_broadcast([P, 40, TOPK]), ALU.mult)
            dve.wait_ge(pool_step, PICK_STEPS * PH)
            dve.drain()
            copy(sums[:, 0, 0:1], sums[:, 1, 0:1]).then_inc(gw_ready, 1)
            dve.wait_ge(ijt_out, 3)

            def one_hot(n, s, t0, first=False):
                if not first:
                    dve.wait_ge(g_done, n - 1)
                for q in range(4):
                    ts(oh[:, s, 0, q, :], iota_k[:, :], ijt[:, 0, bass.ds(t0 + q, 1)], None, ALU.is_equal)
                    last = ts(oh[:, s, 1, q, :], iota_k[:, :], ijt[:, 1, bass.ds(t0 + q, 1)],
                              ijt[:, 2, bass.ds(t0 + q, 1)], ALU.is_equal, ALU.mult)
                last.then_inc(oh_ready, 1)
            for n in range(2):
                one_hot(n, n, 4 * n, first=True)
            with dve.Fori(1, T // 8) as i:
                for s in range(2):
                    one_hot(i * 2 + s, s, i * 8 + 4 * s)

            def rows_lo(q, g):
                dve.wait_ge(t_hi, q * 8 + (g + 1))
                c0 = 4 * (g % 4)
                tt(ut_lo[:, g // 4, c0:c0 + 4, :], pt[g % 2][:, :].rearrange("p (c i) -> p c i", c=4),
                   ut_hi[:, g // 4, c0:c0 + 4, :].bitcast(F32), ALU.subtract).then_inc(t_lo, 1)

            def v_split(q):
                for j in range(2):
                    dve.wait_ge(vh_done, q * 2 + (j + 1))
                    tt(v_lo[:, j, :], v_raw[:, j, :], v_hi[:, j, :].bitcast(F32), ALU.subtract).then_inc(vl_done, 1)

            def gate_pair(q, par):
                for j in range(2):
                    if j == 0:
                        dve.wait_ge(g_in, q * 16 + 16)
                    dve.wait_ge(ge_done, q * 2 + (j + 1))
                    tt(ge[:, :], ge[:, :], g2[:, j, :], ALU.mult).then_inc(gm_done, 1)
                    dve.wait_ge(ph_done, q * 2 + (j + 1))
                    tt(p_lo[:, par, j, :], ge[:, :], p_hi[:, par, j, :].bitcast(F32), ALU.subtract).then_inc(pl_done, 1)

            def add_out(q, c):
                dve.wait_ge(vd_done, q * KC + (c + 1))
                a3 = acc[:, c, :].rearrange("p (b t) -> p b t", b=2)
                tt(a3, a3, pp[c % 2][:, :, 0:HT], ALU.add).then_inc(acc_done, 1)

            for g in range(8):
                rows_lo(0, g)
            gate_pair(0, 0)
            for g in range(8):
                rows_lo(1, g)

            def dve_pair(q, par, more=True):
                v_split(q - 1)
                gate_pair(q, par)
                for g in range(8):
                    add_out(q - 1, 2 * g)
                    add_out(q - 1, 2 * g + 1)
                    if more:
                        rows_lo(q + 1, g)
            dve.wait_ge(acc_zero, 1)
            dve_pair(1, 1)
            with dve.Fori(1, NPAIR // 2 - 1) as i:
                for par in range(2):
                    dve_pair(i * 2 + par, par)
            dve_pair(NPAIR - 2, 0)
            dve_pair(NPAIR - 1, 1, more=False)
            v_split(NPAIR - 1)
            for c in range(KC):
                add_out(NPAIR - 1, c)
            for c in range(KC + 2):
                if c < KC:
                    tt(yt[:, c % 2, :], h_hi[:, c, :].bitcast(F32), h_lo[:, c, :].bitcast(F32), ALU.add)
                    dve.drain()
                    stt(r[:, c, :], yt[:, c % 2, :], ALPHA, acc[:, c, :], ALU.mult, ALU.add).then_inc(nsem["hi"], 1)

            def sample_rows(c):
                if 1 <= c <= KC:
                    k = c - 1
                    norm3.wait(dve, "used", c)
                    if k >= 8 and k % 4 == 0:
                        dve.wait_ge(o_out[k // 4 % 2], 32)
                    copy(ress[:, k // 4 % 2, k % 4, :], pp[k % 2][0:NS, 1, 0:P]).then_inc(o_d, 1)
            dve_norm(dve, norm3, r, after=sample_rows)

        @block.gpsimd
        def _(pool):
            g = nc.gpsimd
            g.memset(ident[:, :], 0.0).then_inc(ident_zero, 1)
            g.memset(mean16[:, :], 1.0 / D).then_inc(ident_ready, 1)
            g.memset(mean8[:, :], 1.0 / (D // 2)).then_inc(ident_ready, 1)
            pool.wait_ge(ident_zero, 1)
            g.affine_select(out=ident[:, :], in_=ident[:, :], compare_op=ALU.not_equal, fill=1.0, base=0,
                            pattern=[[-1, P]], channel_multiplier=1).then_inc(ident_ready, 1)
            g.iota(cnt[:, :], pattern=[[1, 16]], base=1, channel_multiplier=0,
                   allow_small_or_imprecise_dtypes=True).then_inc(const_ready, 1)

            def vector_in(dst, src):
                pool.dma_start(dst, src.rearrange("(c p) -> p c", p=P), allow_slow_non_contiguous=True)\
                    .then_inc(const_in, 16)
            for n, name in enumerate(("ln1", "ln2")):
                vector_in(ln_g[:, n, :], a[name + "_g"][0])
                vector_in(ln_b[:, n, :], a[name + "_b"][0])
            vector_in(sln_g[:, :], a["sgu_ln_g"][0])
            vector_in(sln_b[:, :], a["sgu_ln_b"][0])
            vector_in(pscale[:, :], a["pool_scale"][0])
            pool.dma_start(o["ps"][0][:, 0:STATE - DS, :], a["cache_pool"][0][:, DS:STATE, :]).then_inc(state_out, 16)

            def kv_store(k):
                out = o["kv"[k]][0, 0].rearrange("(m p) h d -> p m (h d)", p=P).rearrange("p m (c n) -> p m c n", n=P)

                def body(u, c):
                    if k == 0:
                        pool.wait_ge(evacuated, u[0] + 1)
                        pool.dma_start(k_scr[c], kvt[:, u[1], :]).then_inc(kt_stored[u[1]], 16)
                    pool.wait_ge(kvn_ready, u[0] + 1)
                    pool.dma_start(out[:, :, c, :], kvn[:, u[1]]).then_inc(nat_stored[u[1]], 16)
                return body
            pairs(pool, MK0, 16, kv_store(0))
            pool.dma_start(ws_n[:, :, :], a["sgu_w"][0].rearrange("h i j -> i h j")).then_inc(ws_in, 16)
            pool.dma_start(sgu_bias[:, :, :], a["sgu_b"][0:1].to_broadcast([P, SH, P])).then_inc(bias_in, 16)
            g.memset(ws_s[:, :, :], 0.0).then_inc(ws_zero, 1)
            pairs(pool, MV0, 16, kv_store(1))
            pool.wait_ge(ws_cp, SH)
            g.affine_select(out=ws_t[:, :, :], in_=ws_t[:, :, :], compare_op=ALU.is_ge, fill=0.0, base=0,
                            pattern=[[0, SH], [1, P]], channel_multiplier=-1).then_inc(ws_ready, 1)
            pool.wait_ge(ws_ready, 1)
            pool.wait_ge(ws_zero, 1)
            for b in range(DB):
                pool.dma_start(ws_s[DS * b:DS * (b + 1), :, DS * b:DS * (b + 1)], ws_t[0:DS, :, 0:DS])\
                    .then_inc(ws_sin, 16)
            pool.wait_ge(vn_ready, SH)
            pool.dma_start(o["vs"][0].rearrange("b s d -> (b s) d"), vns[:, :, :].rearrange("p h d -> p (h d)"))\
                .then_inc(v_state_out, 16)
            pool.wait_ge(st_ready, SH)
            pool.dma_start(cpn[:, :], a["cache_pool"][0].rearrange("b s d -> (b s) d")).then_inc(cp_in, 16)
            pool.wait_ge(v_state_out, 16)
            pool.wait_ge(ysp_lo, SH)
            g.memset(ep[:, :, 0:16], 0.0).then_inc(pool_zero, 1)
            g.memset(es[:, :, :, 0:1], 0.0).then_inc(pool_zero, 1)
            for n in range(4):
                if n >= 1:
                    pool.wait_ge(pm_done, n)
                pool.dma_start(pw[:, :, :], a["pool_w"][0, n].rearrange("(k p) d -> p k d", p=P)).then_inc(pw_in, 16)
                pool.wait_ge(evacuated, A0 + 2 * n + 2)
                if n >= 1:
                    pool.wait_ge(d_ready, n)
                g.tensor_copy(ep[:, :, 16:], dp[:, :, 0:SEQ])
                g.tensor_copy(es[:, :, :, 16:20], dp[:, :, SEQ:T].rearrange("p c (b s) -> p c b s", b=DB))\
                    .then_inc(ep_ready, 1)
                pool.wait_ge(an_ready, n + 1)
                cs = slice(2 * n * P, 2 * (n + 1) * P)
                pool.dma_start(o["pp"][0, 0, :, cs], an[0:STATE].rearrange("p c n -> p (c n)")).then_inc(an_out, 16)
                for b in range(DB):
                    pool.dma_start(o["ps"][0, b, STATE - DS:STATE, cs],
                                   an[STATE + DS * b:STATE + DS * (b + 1)].rearrange("p c n -> p (c n)"))\
                        .then_inc(an_out, 16)
            pool.wait_ge(an_out, 16 * 4 * (DB + 1))
            pool.wait_ge(panel_done, MO0)
            g.memset(qm[:, :, :], 0.0).then_inc(qm_zero, 1)
            pool.wait_ge(panel_done, WQ0)
            pool.dma_start(sub_n[:, :, :], a["peer_subkeys"][0].rearrange("s k d -> k s d")).then_inc(sub_in, 16)
            g.memset(sc[:, :, NT, :], 0.0).then_inc(sc_zero, 1)
            norm2.wait(pool, "used", KC)
            g.iota(iota_k[:, :], pattern=[[1, P]], base=0, channel_multiplier=0, allow_small_or_imprecise_dtypes=True)
            g.iota(iota16[:, :], pattern=[[1, TOPK]], base=0, channel_multiplier=0,
                   allow_small_or_imprecise_dtypes=True).then_inc(iota_ready, 1)
            g.memset(ident2[:, :], 0.0).then_inc(ident_zero, 1)
            g.memset(mean3[:, :], 1.0 / D).then_inc(id2_ready, 1)
            pool.wait_ge(ident_zero, 2)
            g.affine_select(out=ident2[:, :], in_=ident2[:, :], compare_op=ALU.not_equal, fill=1.0, base=0,
                            pattern=[[-1, P]], channel_multiplier=1).then_inc(id2_ready, 1)
            for dst, name in ((ln3_g, "ln3_g"), (ln3_b, "ln3_b")):
                pool.dma_start(dst[:, :], a[name][0].rearrange("(c p) -> p c", p=P),
                               allow_slow_non_contiguous=True).then_inc(ln3_in, 16)

            steps = [0]

            def step(ins):
                ins.then_inc(pool_step, 1)
                steps[0] += 1
                pool.wait_ge(pool_step, steps[0])
            pool.wait_ge(iota_ready, 1)
            NT1 = NT + 1

            def picks(h):
                pool.wait_ge(eq_ready, h + 1)
                step(g.tensor_tensor(eq4, eq4, sif[:, h].rearrange("p x t (k y) -> p (x t) k y", k=1)
                                     .to_broadcast([P, 2 * NT1, TOPK, TOPK]), ALU.mult))
                for w in (8, 4, 2):
                    step(g.tensor_tensor(eq4[:, :, :, 0:w], eq4[:, :, :, 0:w], eq4[:, :, :, w:2 * w], ALU.add))
                step(g.tensor_tensor(ij[:, :, :, h * TOPK:(h + 1) * TOPK].rearrange("p x t k -> p (x t) k"),
                                     eq4[:, :, :, 0:1].rearrange("p n k y -> p n (k y)"),
                                     eq4[:, :, :, 1:2].rearrange("p n k y -> p n (k y)"), ALU.add))
            eq4 = eq[:, :, :, :, :].rearrange("p x t k y -> p (x t) k y")

            for h in range(PH):
                pool.wait_ge(sif_ready, 2 * h + 2)
                if h >= 1:
                    pool.wait_ge(fin_ready, h)
                cv = cand[:, :, :].rearrange("p t (x y) -> p t x y", x=TOPK)
                g.tensor_tensor(cv, sv[:, h, 0].rearrange("p t (x y) -> p t x y", y=1).to_broadcast([P, NT1, TOPK, TOPK]),
                                sv[:, h, 1].rearrange("p t (x y) -> p t x y", x=1).to_broadcast([P, NT1, TOPK, TOPK]),
                                ALU.add).then_inc(cand_ready, 1)
                if h >= 1:
                    picks(h - 1)
            picks(PH - 1)
            assert steps[0] == PICK_STEPS * PH
            for t in range(NT + 1):
                n0 = P // 4 * (t + 1) if t < NT else T // 4
                pool.wait_ge(g_out, n0)
                w = P if t < NT else NS
                for c in range(2):
                    pool.dma_start(g_scr[:, 64 * c:64 * (c + 1), t * P:t * P + w], gs[:, 64 * c:64 * (c + 1), 0:w])\
                        .then_inc(g_stored, 16)
            pool.wait_ge(g_stored, 32 * (NT + 1))
            g.memset(acc[:, :, :], 0.0).then_inc(acc_zero, 1)
            xs = o["xs"].rearrange("b s d -> (b s) d")
            for k in range(4):
                pool.wait_ge(o_a, 4 * (k + 1))
                pool.wait_ge(o_d, 4 * (k + 1))
                pool.dma_start(o["xp"][0].rearrange("(t p) d -> p t d", p=P)[:, :, k * 512:(k + 1) * 512],
                               res[:, k % 2].rearrange("p t c n -> p t (c n)")).then_inc(o_out[k % 2], 16)
                pool.dma_start(xs[:, k * 512:(k + 1) * 512], ress[:, k % 2].rearrange("p c n -> p (c n)"))\
                    .then_inc(o_out[k % 2], 16)
            for k in range(2):
                pool.wait_ge(o_out[k], 64)
            for k in range(2):
                pool.wait_ge(kt_stored[k], 16 * 8)
                pool.wait_ge(nat_stored[k], 16 * 16)
            pool.wait_ge(state_out, 16)


_INS = ["x_prompt", "x_sample", "mem_prompt", "cache_pool", "cache_mem_k", "cache_mem_v", "w_in", "pool_w", "pool_scale",
        "sgu_ln_g", "sgu_ln_b", "sgu_w", "sgu_b", "w_out", "ln1_g", "ln1_b", "w_mq", "w_mk", "w_mv", "w_mo",
        "ln2_g", "ln2_b", "peer_wq", "peer_subkeys", "peer_u", "peer_v", "ln3_g", "ln3_b"]
_OUTS = {"xp": (1, SEQ, D), "xs": (DB, DS, D), "pp": (1, 1, STATE, D_POOL), "k": (1, 1, MEM, AH, D // AH),
         "v": (1, 1, MEM, AH, D // AH), "ps": (1, DB, STATE, D_POOL), "vs": (1, DB, DS, D // 2)}


def kernel(**inputs):
    import numpy as _np
    import concourse.bacc as _bacc
    from concourse.bass_utils import run_bass_kernel_spmd as _run

    nc = _bacc.Bacc("TRN2", target_bir_lowering=False, num_devices=1)
    arrays, args = {}, {}
    for name in _INS:
        arr = _np.ascontiguousarray(inputs[name])
        arrays["in_" + name] = arr
        args[name] = nc.dram_tensor("in_" + name, arr.shape, F32, kind="ExternalInput").ap()
    outs = {name: nc.dram_tensor("out_" + name, shape, F32, kind="ExternalOutput").ap() for name, shape in _OUTS.items()}
    program(nc, args, outs)
    res = _run(nc, [arrays], core_ids=[0])
    return tuple(res.results[0]["out_" + name] for name in _OUTS)
```

```python
from contextlib import ExitStack

import concourse.bass as bass
from concourse import mybir

ALU = mybir.AluOpType
ACT = mybir.ActivationFunctionType
AX = mybir.AxisListType
F32 = mybir.dt.float32
FR = mybir.dt.float32r
U32 = mybir.dt.uint32

P = 128
D = 2048
KC = D // P
SEQ = 512
NT = SEQ // P
DB, DS = 8, 4
NS = DB * DS
T = SEQ + NS
HT = T // 2
D_POOL = 1024
PC = D_POOL // P
WINDOWS = (2, 4, 8, 16)
STATE = 15
SH = 8
MEM = 256
MT = MEM // P
AH = 4
HC = KC // AH
PH = 8
TOPK = 16
NK = 128
NPAIR = NK // 2
ALPHA = 2.0 ** 0.25
EPS = 1e-5
ASCALE = float(D // AH) ** -0.5
NEG = -3.0e38

MK0, MV0, V0, U0, A0, WO0, MQ0, MO0, WQ0, NPANEL = 0, 16, 32, 40, 48, 56, 72, 88, 104, 120

BASE = 16512
XB = KC * T * 4
H_HI, H_LO, Y_HI, Y_LO = (BASE + n * XB for n in range(4))
RAW = BASE + 4 * XB
W_HI = RAW + 2 * D * 4
W_LO = W_HI + 2 * D * 4
CST = W_LO + 2 * D * 4
TMP = CST + 2368
TOP = 229344


def program(nc, a, o):
    ctx = ExitStack()
    with ctx:
        def at(name, offset, shape, dt=F32):
            size = 4
            for s in shape[1:]:
                size *= s
            assert offset + size <= TOP, name
            return nc.alloc_sbuf_tensor_at(name, shape, dt, offset=offset)

        def sem(name):
            return ctx.enter_context(nc.semaphore(name))

        h_hi = at("h_hi", H_HI, [P, KC, T], FR)
        h_lo = at("h_lo", H_LO, [P, KC, T], FR)
        r = at("r", H_HI, [P, KC, T])
        y_hi = at("y_hi", Y_HI, [P, KC, T], FR)
        y_lo = at("y_lo", Y_LO, [P, KC, T], FR)
        raw = at("raw", RAW, [P, 2, KC, P])
        w_hi = at("w_hi", W_HI, [P, 2, KC, P], FR)
        w_lo = at("w_lo", W_LO, [P, 2, KC, P], FR)
        ident = at("ident", CST, [P, P])
        mean16 = at("mean16", CST + 512, [P, P])
        mean8 = at("mean8", CST + 1024, [P, P])
        ln_g = at("ln_g", CST + 1536, [P, 3, KC])
        ln_b = at("ln_b", CST + 1728, [P, 3, KC])
        sln_g = at("sln_g", CST + 1920, [P, SH])
        sln_b = at("sln_b", CST + 1952, [P, SH])
        pscale = at("pscale", CST + 1984, [P, PC])
        inv_n = at("inv_n", CST + 2016, [P, 4, 16])
        cnt = at("cnt", CST + 2272, [P, 16])
        mu = at("mu", TMP, [P, 2, HT])
        rs = at("rs", TMP + 2176, [P, 2, HT])
        sq = at("sq", TMP + 2 * 2176, [P, 2, 2, HT])
        yt = at("yt", TMP + 4 * 2176, [P, 2, T])
        ya = at("ya", TMP + 6 * 2176, [P, 2, T])

        pp = [ctx.enter_context(nc.psum_tensor(f"pp{i}", [P, 2, 512], F32)) for i in range(2)]
        pt = [ctx.enter_context(nc.psum_tensor(f"pt{i}", [P, 512], F32)) for i in range(2)]
        pl = ctx.enter_context(nc.psum_tensor("pl", [P, 2, 512], F32))

        k_scr = nc.dram_tensor("k_scr", [KC, P, MEM], F32).ap()
        g_scr = nc.dram_tensor("g_scr", [P, NK, T], F32).ap()

        def panels(w):
            return w.rearrange("(k p) (c n) -> p k c n", p=P, n=P)
        w_in = panels(a["w_in"][0])
        streams = [(MK0, panels(a["w_mk"][0]), 0, 16), (MV0, panels(a["w_mv"][0]), 0, 16),
                   (V0, w_in, 16, 8), (U0, w_in, 8, 8), (A0, w_in, 0, 8),
                   (WO0, panels(a["w_out"][0]), 0, 16), (MQ0, panels(a["w_mq"][0]), 0, 16),
                   (MO0, panels(a["w_mo"][0]), 0, 16), (WQ0, panels(a["peer_wq"][0]), 0, 16)]

        raw_in = [sem("raw_in0"), sem("raw_in1")]
        hi_ready = sem("hi_ready")
        lo_ready = sem("lo_ready")
        panel_done = sem("panel_done")
        evacuated = sem("evacuated")

        const_in = sem("const_in")
        bias_in, ws_sin, ident_zero, pool_step, sif_ready = (sem("bias_in"), sem("ws_sin"), sem("ident_zero"),
                                                             sem("pool_step"), sem("sif_ready"))
        ident_ready = sem("ident_ready")
        const_ready = sem("const_ready")
        row_in = [sem("row_in0"), sem("row_in1"), sem("row_in2")]
        tr_done, tr_hi, tr_free = sem("tr_done"), sem("tr_hi"), sem("tr_free")
        kvt_done, kvn_ready = sem("kvt_done"), sem("kvn_ready")
        kt_stored = [sem("kt_stored0"), sem("kt_stored1")]
        nat_stored = [sem("nat_stored0"), sem("nat_stored1")]

        nsem = {"mu": sem("norm_mu"),
                "mu_out": sem("norm_mu_out"),
                "xc": sem("norm_xc"),
                "sq": sem("norm_sq"),
                "var": sem("norm_var"),
                "veps": sem("norm_veps"),
                "std": sem("norm_std"),
                "yt": sem("norm_yt"),
                "ya": sem("norm_ya"),
                "hi": sem("norm_hi"),
                "used": sem("norm_used")}

        class Norm:
            def __init__(self, k, base, n):
                self.k, self.base, self.n = k, base, n

            def wait(self, eng, name, count):
                before = self.k if name in ("mu", "mu_out", "veps", "std") else self.base
                if name == "hi":
                    before -= 8 if self.k else 0
                eng.wait_ge(nsem[name], before + count)
        sgu_norm, norm1, norm2, norm3 = Norm(0, 0, 8), Norm(1, 8, 16), Norm(2, 24, 16), Norm(3, 40, 16)

        block = ctx.enter_context(nc.Block())

        def pe_panel(pe, u, x_hi, x_lo, first=False, n=T):
            s = u[1]
            pe.wait_ge(lo_ready, u[0] + 1)
            if not first:
                pe.wait_ge(evacuated, u[0] - 1)
            parts = [(0, 0, HT), (1, HT, T)] if n == T else [(0, 0, n)]
            for k in range(KC):
                for w, x in ((w_hi, x_hi), (w_hi, x_lo), (w_lo, x_hi)):
                    for b, t0, t1 in parts:
                        last = nc.tensor.matmul(pp[s][:, b, 0:t1 - t0], w[:, s, k, :], x[:, k, t0:t1],
                                                start=(k == 0 and w is w_hi and x is x_hi),
                                                stop=(k == KC - 1 and w is w_lo))
            last.then_inc(panel_done, 1)

        def act_split(act, u, first=False):
            s = u[1]
            act.wait_ge(raw_in[s], u[2])
            if not first:
                act.wait_ge(panel_done, u[0] - 1)
            nc.scalar.activation(w_hi[:, s], raw[:, s], ACT.Copy).then_inc(hi_ready, 1)

        def dve_split(dve, u):
            s = u[1]
            dve.wait_ge(hi_ready, u[0] + 1)
            nc.vector.tensor_tensor(w_lo[:, s], raw[:, s], w_hi[:, s].bitcast(F32),
                                    ALU.subtract).then_inc(lo_ready, 1)

        def num(u):
            return (u, u % 2, 16 * (u // 2 + 1))

        def in_loop(u0, i, d):
            half = (u0 + d) // 2
            return (i * 2 + (u0 + d), d % 2, i * 16 + 16 * (half + 1))

        def pairs(eng, u0, n, body, skip_first=0, skip_last=0, issued=0):
            for c in range(issued, skip_first):
                body(num(u0 + c), c)
            if n - skip_first - skip_last >= 2:
                assert skip_first % 2 == 0
                with eng.Fori(skip_first // 2, (n - skip_last) // 2) as i:
                    for d in range(2):
                        body(in_loop(u0, i, d), i * 2 + d)
            for c in range(n - skip_last, n):
                body(num(u0 + c), c)

        def act_norm(act, nm, gain, bias, buf, hi_out=None, after=None):
            nm.wait(act, "mu", 1)
            nc.scalar.activation(mu[:, :, :], pl[:, :, 0:HT], ACT.Copy).then_inc(nsem["mu_out"], 1)
            for c in range(nm.n):
                nm.wait(act, "xc", c + 1)
                if c >= 2:
                    nm.wait(act, "var", c - 1)
                nc.scalar.activation(sq[:, c % 2], buf[:, c, :].rearrange("p (b t) -> p b t", b=2),
                                     ACT.Square).then_inc(nsem["sq"], 1)
            nm.wait(act, "veps", 1)
            nc.scalar.activation(rs[:, :, :], rs[:, :, :], ACT.Sqrt).then_inc(nsem["std"], 1)
            for c in range(nm.n + 1):
                if c < nm.n:
                    nm.wait(act, "yt", c + 1)
                    if c >= 2:
                        nm.wait(act, "used", c - 1)
                    nc.scalar.activation(ya[:, c % 2, :], yt[:, c % 2, :], ACT.Identity,
                                         scale=gain[:, c:c + 1], bias=bias[:, c:c + 1]).then_inc(nsem["ya"], 1)
                if hi_out is not None and c >= 1:
                    nm.wait(act, "ya", c)
                    nc.scalar.activation(hi_out[:, c - 1, :], ya[:, (c - 1) % 2, :], ACT.Copy).then_inc(nsem["hi"], 1)
                if after is not None:
                    after(c)

        def flat(x):
            return x.rearrange("p b t -> p (b t)")

        def dve_norm(dve, nm, buf, lo_out=None, hi=None, after=None):
            nm.wait(dve, "mu_out", 1)
            for c in range(nm.n):
                nc.vector.tensor_tensor(buf[:, c, :], buf[:, c, :], flat(mu[:, :, :]), ALU.subtract).then_inc(nsem["xc"], 1)
            nm.wait(dve, "var", nm.n)
            nc.vector.tensor_scalar(rs[:, :, :], pl[:, :, 0:HT], EPS, None, ALU.add).then_inc(nsem["veps"], 1)
            nm.wait(dve, "std", 1)
            nc.vector.reciprocal(rs[:, :, :], rs[:, :, :])
            dve.drain()
            for c in range(nm.n + 2):
                if c < nm.n:
                    if c >= 2:
                        nm.wait(dve, "ya", c - 1)
                    nc.vector.tensor_tensor(yt[:, c % 2, :], buf[:, c, :], flat(rs[:, :, :]), ALU.mult)\
                        .then_inc(nsem["yt"], 1)
                if lo_out is not None and 1 <= c <= nm.n:
                    nm.wait(dve, "hi", c)
                    nc.vector.tensor_tensor(lo_out[:, c - 1, :], ya[:, (c - 1) % 2, :],
                                            hi[:, c - 1, :].bitcast(F32), ALU.subtract).then_inc(nsem["used"], 1)
                if after is not None:
                    after(c)

        mem_hi = at("mem_hi", Y_HI, [P, KC, MEM], FR)
        mem_lo = at("mem_lo", Y_HI + KC * MEM * 4, [P, KC, MEM], FR)
        rows = at("rows", Y_LO, [P, 3, D])
        row_tiles = [(a["mem_prompt"][0, t * P:(t + 1) * P, :], P, mem_hi, mem_lo, t * P) for t in range(MT)] + \
                    [(a["x_prompt"][0, t * P:(t + 1) * P, :], P, h_hi, h_lo, t * P) for t in range(NT)] + \
                    [(a["x_sample"].rearrange("b s d -> (b s) d"), NS, h_hi, h_lo, SEQ)]
        NG = KC // 4

        def row_views(m, part):
            _, rn, hi, lo, t0 = row_tiles[m // NG]
            g = m % NG
            ps = pt[m % 2][:, :].rearrange("p (q t) -> p q t", q=4)[:, :, 0:rn]
            return ps, (hi, lo)[part][:, 4 * g:4 * g + 4, t0:t0 + rn]

        kvt = at("kvt", TMP, [P, 2, MEM])
        kvn = at("kvn", TMP + 2048, [P, 2, MT, P])

        vt = at("vt", Y_HI, [P, SH, T])
        st = at("st", Y_HI + SH * T * 4, [P, SH, T])
        sgu_bias = at("sgu_bias", Y_LO, [P, SH, P])
        ws_n = at("ws_n", Y_LO + 4096, [P, SH, P])
        ws_t = at("ws_t", Y_LO + 8192, [P, SH, P])
        ws_s = at("ws_s", Y_LO + 12288, [NS, SH, NS])
        vns = at("vns", Y_LO + 13312, [NS, SH, P])
        vn = at("vn", TMP + 8 * 2176, [P, 2, NT, P])
        ug = at("ug", TMP, [P, 2, T])
        yf = at("yf", TMP + 2 * 2176, [P, 2, T])
        ws_zero, ws_in, ws_tr, ws_cp = sem("ws_zero"), sem("ws_in"), sem("ws_tr"), sem("ws_cp")
        ws_ready = sem("ws_ready")
        vn_ready, s_done, st_ready = sem("vn_ready"), sem("s_done"), sem("st_ready")
        y_ready, ysp_hi, ysp_lo = sem("y_ready"), sem("ysp_hi"), sem("ysp_lo")
        v_state_out = sem("v_state_out")

        ep = at("ep", TMP, [P, 2, 16 + SEQ])
        es = at("es", TMP + 4224, [P, 2, DB, 20])
        fa = at("fa", TMP + 5504, [P, 2, 16 + SEQ])
        fas = at("fas", TMP + 5504 + 4224, [P, 2, DB, 20])
        fb = at("fb", TMP + 11008, [P, 2, 16 + SEQ])
        fbs = at("fbs", TMP + 11008 + 4224, [P, 2, DB, 20])
        yp = at("yp", TMP + 11008, [P, 2, T])
        dp = at("dp", TMP + 16512, [P, 2, T])
        an = at("an", TMP + 20864, [STATE + NS, 2, P])
        cpn = at("cpn", Y_HI + 6 * T * 4, [DB * STATE, D_POOL])
        pw = at("pw", Y_LO + 7 * T * 4, [P, 2, 256])
        cp_in, pw_in, pool_zero = sem("cp_in"), sem("pw_in"), sem("pool_zero")
        ep_ready, es_ready, at_done, an_ready, an_out = (sem("ep_ready"), sem("es_ready"), sem("at_done"),
                                                         sem("an_ready"), sem("an_out"))
        d_ready, pm_done, yp_ready, pp_hi, pp_lo = (sem("d_ready"), sem("pm_done"), sem("yp_ready"),
                                                    sem("pp_hi"), sem("pp_lo"))
        state_out = sem("state_out")

        qt = at("qt", Y_HI, [P, KC, T])
        kv = at("kv", Y_LO, [P, 2, MT, D])
        qm = at("qm", W_HI, [P, KC, 288])
        kr = at("kr", W_HI + KC * 288 * 4, [P, 3, 4, MEM])
        ktp = at("ktp", W_HI, [P, KC, MEM])
        vp = at("vp", W_LO, [P, MT, D])
        ssm = at("ssm", TMP, [NS, AH, MEM])
        pts = at("pts", TMP + 4096, [P, AH * MT, NS])
        smx = at("smx", TMP + 5120, [NS, 4, AH])
        pr = at("pr", TMP + 5248, [P, 2, MEM])
        pst = at("pst", TMP + 7296, [P, 2, 4])
        ptt = at("ptt", TMP + 7328, [P, 2, MT, SEQ])
        qm_zero, qm_ready = sem("qm_zero"), sem("qm_ready")
        kv_in = [sem("kv_in0"), sem("kv_in1")]
        kr_tr, kr_a, kr_d, ks_done = sem("kr_tr"), sem("kr_a"), sem("kr_d"), sem("ks_done")
        ss_max, ss_exp, ss_p, ss_tr, ss_pt, sv_done, so_hi, so_lo = [sem("att_s%d" % n) for n in range(8)]
        kp_in, vp_in = sem("kp_in"), sem("vp_in")
        ps_done, ps_max, ps_exp, ps_p, ps_tr, ps_pt, pv_done, po_hi, po_lo = [sem("att_p%d" % n) for n in range(9)]

        sc = at("sc", Y_HI, [P, 2 * PH, NT + 1, P])
        sc2 = at("sc2", Y_HI + 40960, [P, NT + 1, P])
        sv = at("sv", Y_HI + 43520, [P, PH, 2, NT + 1, TOPK])
        si = at("si", Y_HI + 48640, [P, PH, 2, NT + 1, TOPK], U32)
        cand = at("cand", Y_HI + 53760, [P, NT + 1, 256])
        cand2 = at("cand2", Y_HI + 58880, [P, NT + 1, 256])
        sub_n = at("sub_n", Y_HI + 58880, [P, 2, P])
        q2 = at("q2", Y_HI + 64000, [P, 2, T])
        sub_t = at("sub_t", Y_HI + 68352, [P, 2, P])
        eq = at("eq", Y_HI, [P, 2, NT + 1, TOPK, TOPK])
        gs = at("gs", Y_HI, [P, NK, P])
        sif = at("sif", TMP, [P, PH, 2, NT + 1, TOPK])
        ab_f = at("ab_f", TMP + 5120, [P, 2, NT + 1, TOPK])
        ab_u = at("ab_u", TMP + 5760, [P, 2, NT + 1, TOPK], U32)
        ijt = at("ijt", TMP, [P, 3, T])
        iota_k = at("iota_k", TMP + 6528, [P, P])
        ge2 = at("ge2", TMP + 7040, [P, 2, T])
        ij = at("ij", TMP + 11392, [P, 2, NT + 1, P])
        gw = at("gw", TMP + 16512, [P, NT + 1, P])
        oh = at("oh", TMP + 11392, [P, 2, 2, 4, P])
        fi = at("fi", TMP + 19584, [P, NT + 1, TOPK], U32)
        sums = at("sums", TMP + 19904, [P, 2, 40])
        iota16 = at("iota16", TMP + 20224, [P, TOPK])
        PICK_STEPS = 5
        sub_in, sub_tr, sub_cp = sem("sub_in"), sem("sub_tr"), sem("sub_cp")
        iota_ready, sc_zero = sem("iota_ready"), sem("sc_zero")
        sc_done, sc_out, top_ready, cand_ready, fin_ready, eq_ready = [sem("sel%d" % n) for n in range(6)]
        g_sub, g_exp, gw_ready, ijt_done, ijt_out = [sem("gate%d" % n) for n in range(5)]
        oh_ready, g_done, g_out, g_stored = [sem("gmat%d" % n) for n in range(4)]

        AHEAD = 20
        PICK_COLS = 12
        TILE_COLS = 6
        acc = at("acc", Y_HI, [P, KC, T])
        v_hi = at("v_hi", Y_LO, [P, 2, D], FR)
        v_raw = at("v_raw", Y_LO + 16384, [P, 2, D])
        v_lo = at("v_lo", Y_LO + 16384, [P, 2, D], FR)
        u_raw = at("u_raw", RAW, [P, 2, D])
        ut_hi = at("ut_hi", W_HI, [P, 2, KC, P], FR)
        ut_lo = at("ut_lo", W_LO, [P, 2, KC, P], FR)
        v2_hi = at("v2_hi", W_HI, [P, 2, D], FR)
        v2_raw = at("v2_raw", RAW, [P, 2, D])
        v2_lo = at("v2_lo", RAW, [P, 2, D], FR)
        vslot = [(v_hi, v_raw, v_lo), (v2_hi, v2_raw, v2_lo)]
        g2 = at("g2", TMP, [P, 2, T])
        p_hi = [at("p_hi0", TMP + 13056, [P, 2, T], FR), at("p_hi1", TMP + 4352, [P, 2, T], FR)]
        p_lo = [at("p_lo0", TMP + 17408, [P, 2, T], FR), at("p_lo1", TMP + 8704, [P, 2, T], FR)]
        p_f = [at("p_f0", TMP + 17408, [P, 2, T]), at("p_f1", TMP + 8704, [P, 2, T])]
        s_scr = nc.dram_tensor("s_scr", [AHEAD, 2, P, T], F32).ap()
        s_in = sem("s_in")
        ge_stored = [sem("ge_stored0"), sem("ge_stored1")]
        acc_zero = sem("acc_zero")
        u_in = [sem("u_in0"), sem("u_in1")]
        v_in = [sem("v_in0"), sem("v_in1")]
        g_in = sem("g_in")
        t_done, t_hi, t_lo = sem("t_done"), sem("t_hi"), sem("t_lo")
        u_done, ge_done, gm_done, ph_done, pl_done = [sem("act%d" % n) for n in range(5)]
        vh_done, vl_done = sem("vh_done"), sem("vl_done")
        vd_done, acc_done = sem("vd_done"), sem("acc_done")

        def gate_columns(eng, column):
            for t in range(NT):
                q0 = (PICK_COLS + t * TILE_COLS) // 2
                if t == 0:
                    for i in range(2):
                        for j in range(2):
                            column(q0 + i, j, (t, i))
                else:
                    with eng.Fori(0, 2) as i:
                        for j in range(2):
                            column(i + q0, j, (t, i))
                for j in range(2):
                    column(q0 + 2, j)
            column(AHEAD - 2, 0, (NT, 0))
            column(AHEAD - 2, 1)
            column(AHEAD - 1, 0)
        assert PICK_COLS + NT * TILE_COLS + 4 == 2 * AHEAD and TILE_COLS == 6

        def group(tile, j, g, s):
            t, i = tile
            return i * 16 + (32 * t + 8 * j + 2 * g + s), i * 64 + (32 * j + 8 * g + 4 * s)
        res = at("res", Y_HI, [P, 2, NT, 4, P])
        ress = at("ress", Y_HI + 16384, [NS, 2, 4, P])
        o_a, o_d = sem("o_a"), sem("o_d")
        o_out = [sem("o_out0"), sem("o_out1")]

        @block.sync
        def _(sp):
            def rows_load(n):
                src, rn = row_tiles[n][:2]
                if n >= 3:
                    sp.wait_ge(tr_done, NG * (n - 2))
                sp.dma_start(rows[0:rn, n % 3, :], src).then_inc(row_in[n % 3], 16)

            def panel_load(view, c0):
                def load(u, c):
                    if not isinstance(u[0], int) or u[0] >= 2:
                        sp.wait_ge(lo_ready, u[0] - 1)
                    sp.dma_start(raw[:, u[1]], view[:, :, c + c0, :]).then_inc(raw_in[u[1]], 16)
                return load

            for n in range(3):
                rows_load(n)
            for c in range(2):
                panel_load(streams[0][1], 0)(num(c), c)
            for n in range(3, len(row_tiles)):
                rows_load(n)
            for u0, view, c0, n in streams:
                load = panel_load(view, c0)
                if u0 == MK0:
                    pairs(sp, u0, n, load, skip_first=2, issued=2)
                elif u0 == MO0:
                    for c in range(2):
                        load(num(u0 + c), c)
                    sp.wait_ge(panel_done, WO0 + 16)
                    for b in range(DB):
                        if b >= 2:
                            sp.wait_ge(kr_tr, AH * (b - 1))
                        sp.dma_start(kv[:, b % 2], a["cache_mem_k"][0, b].rearrange("(t p) h d -> p t (h d)", p=P))\
                            .then_inc(kv_in[b % 2], 16)
                    for b in range(DB):
                        if b < 2:
                            sp.wait_ge(kr_tr, AH * (DB - 1 + b))
                        else:
                            sp.wait_ge(sv_done, b - 1)
                        sp.dma_start(kv[:, b % 2], a["cache_mem_v"][0, b].rearrange("(t p) h d -> p t (h d)", p=P))\
                            .then_inc(kv_in[b % 2], 16)
                        if b == 1:
                            sp.wait_ge(ks_done, DB * AH)
                            for s in range(2):
                                sp.wait_ge(kt_stored[s], 16 * 8)
                                sp.wait_ge(nat_stored[s], 16 * 16)
                            sp.dma_start(ktp[:, :, :], k_scr.rearrange("c p m -> p c m")).then_inc(kp_in, 16)
                            sp.dma_start(vp[:, :, :], o["v"][0, 0].rearrange("(t p) h d -> p t (h d)", p=P))\
                                .then_inc(vp_in, 16)
                    pairs(sp, u0, n, load, skip_first=2, issued=2)
                else:
                    pairs(sp, u0, n, load)
            uv = a["peer_u"][0].rearrange("(i q j) d -> q j i d", q=NPAIR, j=2)
            vv = a["peer_v"][0].rearrange("(i q j) d -> q j i d", q=NPAIR, j=2)
            gv = g_scr.rearrange("i (q j) t -> q i j t", j=2)

            def u_load(q, j, free=None):
                if free is not None:
                    sp.wait_ge(t_done, free)
                sp.dma_start(u_raw[:, j, :], uv[q, j]).then_inc(u_in[j], 16)

            def ge_store(q, j):
                sp.wait_ge(ge_done, q * 2 + (j + 1))
                sp.dma_start(s_scr[q, j], ge2[:, j, :]).then_inc(ge_stored[j], 16)

            def v_load(q, slot=0):
                for j in range(2):
                    sp.dma_start(vslot[slot][1][:, j, :], vv[q, j]).then_inc(v_in[j], 16)

            def g_load(q):
                if not (isinstance(q, int) and q == 0):
                    sp.wait_ge(gm_done, q * 2)
                sp.dma_start(g2[:, :, :], gv[q]).then_inc(g_in, 16)

            def s_load(q, par):
                sp.dma_start(p_f[par][:, :, :], s_scr[q].rearrange("j p t -> p j t")).then_inc(s_in, 16)

            sp.wait_ge(lo_ready, NPANEL)
            for j in range(2):
                u_load(0, j)
            for j in range(2):
                u_load(1, j, 4 * (j + 1))
                if j == 1:
                    ge_store(0, 0)
            with sp.Fori(1, AHEAD - 1) as q:
                u_load(q + 1, 0, q * 8 + 4)
                ge_store(q - 1, 1)
                u_load(q + 1, 1, q * 8 + 8)
                ge_store(q, 0)
            ge_store(AHEAD - 2, 1)
            ge_store(AHEAD - 1, 0)
            sp.wait_ge(g_stored, 32 * (NT + 1))
            g_load(0)
            for j in range(2):
                sp.wait_ge(ge_stored[j], 16)
            s_load(0, 0)
            v_load(0)
            ge_store(AHEAD - 1, 1)
            g_load(1)
            for j in range(2):
                sp.wait_ge(ge_stored[j], 16 * AHEAD)
            s_load(1, 1)
            sp.wait_ge(u_done, 2 * AHEAD)
            sp.wait_ge(vh_done, 2)
            v_load(1, 1)

            def ahead_loads(q, slot):
                g_load(q)
                sp.wait_ge(vd_done, q * KC - KC)
                s_load(q, slot)
                sp.wait_ge(vh_done, q * 2)
                v_load(q, slot)
            with sp.Fori(1, AHEAD // 2 - 1) as i:
                for slot in range(2):
                    ahead_loads(i * 2 + slot, slot)
            ahead_loads(AHEAD - 2, 0)
            sp.wait_ge(vd_done, (AHEAD - 2) * KC)
            for j in range(2):
                u_load(AHEAD, j)
            g_load(AHEAD - 1)
            s_load(AHEAD - 1, 1)
            sp.wait_ge(vd_done, (AHEAD - 1) * KC)
            v_load(AHEAD - 1)
            g_load(AHEAD)
            with sp.Fori(AHEAD, NPAIR - 1) as q:
                for j in range(2):
                    u_load(q + 1, j, q * 8 + (4 * j + 4))
                g_load(q + 1)
                sp.wait_ge(vd_done, q * KC)
                v_load(q)
            sp.wait_ge(vd_done, (NPAIR - 1) * KC)
            v_load(NPAIR - 1)

        @block.tensor
        def _(pe):
            mm, turn = nc.tensor.matmul, nc.tensor.transpose
            pe.wait_ge(ident_ready, 3)
            for n in range(len(row_tiles)):
                pe.wait_ge(row_in[n % 3], 16 * (n // 3 + 1))
                rn = row_tiles[n][1]
                for g in range(NG):
                    m = n * NG + g
                    if m >= 2:
                        pe.wait_ge(tr_free, m - 1)
                    for q in range(4):
                        c = 4 * g + q
                        last = turn(pt[m % 2][:, q * P:q * P + rn], rows[0:rn, n % 3, c * P:(c + 1) * P],
                                    ident[0:rn, 0:rn])
                    last.then_inc(tr_done, 1)

            pe.wait_ge(tr_free, NG * len(row_tiles))

            def kv_panel(u, c):
                pe_panel(pe, u, mem_hi, mem_lo, n=MEM)

            def kv_turn(u, c, first=False):
                pe.wait_ge(evacuated, u[0] + 1)
                if not first:
                    pe.wait_ge(kvn_ready, u[0] - 1)
                for m in range(MT):
                    last = turn(pt[u[1]][:, m * P:(m + 1) * P], kvt[:, u[1], m * P:(m + 1) * P], ident[:, :])
                last.then_inc(kvt_done, 1)
            pe_panel(pe, num(0), mem_hi, mem_lo, first=True, n=MEM)
            pe_panel(pe, num(1), mem_hi, mem_lo, first=True, n=MEM)
            kv_turn(num(0), 0, first=True)
            pe_panel(pe, num(2), mem_hi, mem_lo, n=MEM)
            kv_turn(num(1), 0, first=True)
            with pe.Fori(1, V0 // 2 - 1) as i:
                for d in range(2):
                    pe_panel(pe, in_loop(0, i, d + 1), mem_hi, mem_lo, n=MEM)
                    kv_turn(in_loop(0, i, d), 0)
            pe_panel(pe, num(V0 - 1), mem_hi, mem_lo, n=MEM)
            kv_turn(num(V0 - 2), 0)
            kv_turn(num(V0 - 1), 0)

            def summed(u0, n, x_hi, x_lo, buf, nm):
                def sums_of(u, c, start=False, stop=False):
                    pe.wait_ge(evacuated, u + 1)
                    for b in range(2):
                        last = mm(pl[:, b, 0:HT], (mean16 if n == 16 else mean8)[:, :],
                                  buf[:, c, b * HT:(b + 1) * HT], start=start, stop=stop)
                    return last
                pe_panel(pe, num(u0), x_hi, x_lo)
                pe_panel(pe, num(u0 + 1), x_hi, x_lo)
                sums_of(u0, 0, start=True)
                with pe.Fori(1, n // 2) as i:
                    for d in range(2):
                        pe_panel(pe, in_loop(u0, i, d), x_hi, x_lo)
                        sums_of(i * 2 + (u0 + d - 1), i * 2 + (d - 1))
                sums_of(u0 + n - 1, n - 1, stop=True).then_inc(nsem["mu"], 1)

            def variance(nm):
                nm.wait(pe, "mu_out", 1)
                for c in range(nm.n):
                    nm.wait(pe, "sq", c + 1)
                    for b in range(2):
                        last = mm(pl[:, b, 0:HT], (mean16 if nm.n == 16 else mean8)[:, :], sq[:, c % 2, b, :],
                                  start=(c == 0), stop=(c == nm.n - 1))
                    last.then_inc(nsem["var"], 1)

            pe.wait_ge(ws_in, 16)
            for h in range(SH):
                if h >= 2:
                    pe.wait_ge(ws_cp, h - 1)
                else:
                    pe.wait_ge(kvn_ready, V0)
                turn(pt[h % 2][:, 0:P], ws_n[:, h, :], ident[:, :]).then_inc(ws_tr, 1)
            summed(V0, 8, h_hi, h_lo, vt, sgu_norm)
            variance(sgu_norm)
            pe.wait_ge(ws_ready, 1)
            pe.wait_ge(ws_sin, 16 * DB)
            for h in range(SH + 1):
                if h < SH:
                    sgu_norm.wait(pe, "ya", h + 1)
                    if h >= 1:
                        pe.wait_ge(vn_ready, h)
                    for t in range(NT):
                        turn(pt[0][:, t * P:(t + 1) * P], ya[:, h % 2, t * P:(t + 1) * P], ident[:, :])
                    turn(pt[1][0:NS, 0:P], ya[:, h % 2, SEQ:T], ident[:, :]).then_inc(nsem["used"], 1)
                if h >= 1:
                    k = h - 1
                    pe.wait_ge(vn_ready, h)
                    if k >= 2:
                        pe.wait_ge(st_ready, k - 1)
                    for t in range(NT):
                        mm(pp[k % 2][:, 0, t * P:(t + 1) * P], vn[:, k % 2, t, :], ws_t[:, k, :], start=True, stop=True)
                    mm(pp[k % 2][:, 1, 0:NS], vns[:, k, :], ws_s[:, k, :], start=True, stop=True).then_inc(s_done, 1)
            pe.wait_ge(st_ready, SH)
            pairs(pe, U0, 8, lambda u, c: pe_panel(pe, u, h_hi, h_lo))
            pe.wait_ge(cp_in, 16)
            for g in range(4):
                pe_panel(pe, num(A0 + 2 * g), h_hi, h_lo)
                pe_panel(pe, num(A0 + 2 * g + 1), h_hi, h_lo)
                pe.wait_ge(evacuated, A0 + 2 * g + 2)
                if g >= 1:
                    pe.wait_ge(pp_lo, 2 * g)
                for c in range(2):
                    turn(pt[0][:, c * P:c * P + DB * STATE], cpn[:, (2 * g + c) * P:(2 * g + c + 1) * P],
                         ident[0:DB * STATE, 0:DB * STATE])
                    last = turn(pt[1][0:STATE + NS, c * P:(c + 1) * P], dp[:, c, SEQ - STATE:T], ident[:, :])
                last.then_inc(at_done, 1)
                pe.wait_ge(d_ready, g + 1)
                pe.wait_ge(an_ready, g + 1)
                pe.wait_ge(pw_in, 16 * (g + 1))
                for c in range(2):
                    for b in range(2):
                        out = pl[:, b, 0:HT] if c == 0 else pt[b][:, 0:HT]
                        for k in range(2):
                            last = mm(out, pw[:, k, c * P:(c + 1) * P], dp[:, k, b * HT:(b + 1) * HT],
                                      start=(k == 0), stop=(k == 1))
                last.then_inc(pm_done, 1)
            pe.wait_ge(pp_lo, 8)
            pe.wait_ge(ysp_lo, 8)
            summed(WO0, 16, y_hi, y_lo, r, norm1)
            variance(norm1)
            norm1.wait(pe, "used", KC)
            pairs(pe, MQ0, 16, lambda u, c: pe_panel(pe, u, h_hi, h_lo))
            pe.wait_ge(qm_ready, 1)
            pe.wait_ge(evacuated, MO0)
            for n in range(DB * AH + 1):
                if n < DB * AH:
                    b, h = n // AH, n % AH
                    if h == 0:
                        pe.wait_ge(kv_in[b % 2], 16 * (b // 2 + 1))
                    if n >= 1:
                        pe.wait_ge(kr_a, n)
                        pe.wait_ge(kr_d, n)
                    for c in range(4):
                        for m in range(MT):
                            last = turn(pt[c // 2][:, (c % 2) * MEM + m * P:(c % 2) * MEM + (m + 1) * P],
                                        kv[:, b % 2, m, (4 * h + c) * P:(4 * h + c + 1) * P], ident[:, :])
                    last.then_inc(kr_tr, 1)
                if n >= 1:
                    b, h = (n - 1) // AH, (n - 1) % AH
                    pe.wait_ge(kr_a, n)
                    pe.wait_ge(kr_d, n)
                    for c in range(4):
                        last = mm(pp[h // 2][0:NS, h % 2, 0:MEM], qm[:, 4 * h + c, NS * b:NS * (b + 1)],
                                  kr[:, (n - 1) % 3, c, :], start=(b == 0 and c == 0), stop=(b == DB - 1 and c == 3))
                    last.then_inc(ks_done, 1)
            pe.wait_ge(ss_p, 1)
            for m in range(AH * MT):
                last = turn(pt[0][:, m * NS:(m + 1) * NS], ssm[:, m // MT, (m % MT) * P:(m % MT + 1) * P],
                            ident[0:NS, 0:NS])
            last.then_inc(ss_tr, 1)
            pe.wait_ge(ss_pt, 1)
            for b in range(DB):
                pe.wait_ge(kv_in[b % 2], 16 * (b // 2 + 5))
                for c in range(KC):
                    for m in range(MT):
                        last = mm(pl[:, 0, c * NS + DS * b:c * NS + DS * (b + 1)],
                                  kv[:, b % 2, m, c * P:(c + 1) * P], pts[:, (c // 4) * MT + m, DS * b:DS * (b + 1)],
                                  start=(m == 0), stop=(m == MT - 1))
                last.then_inc(sv_done, 1)
            pe.wait_ge(kp_in, 16)
            pe.wait_ge(ss_exp, AH)
            for n in range(AH * NT + 2):
                if n < AH * NT:
                    h, t = n // NT, n % NT
                    if n >= 4:
                        pe.wait_ge(ps_exp, n - 3)
                    for c in range(4):
                        last = mm(pp[n // 2 % 2][:, n % 2, 0:MEM], qt[:, 4 * h + c, t * P:(t + 1) * P],
                                  ktp[:, 4 * h + c, :], start=(c == 0), stop=(c == 3))
                    last.then_inc(ps_done, 1)
                if n >= 2:
                    k = n - 2
                    h, t = k // NT, k % NT
                    pe.wait_ge(ps_p, k + 1)
                    if k >= 2:
                        pe.wait_ge(ps_pt, k - 1)
                    for m in range(MT):
                        last = turn(pt[k % 2][:, m * P:(m + 1) * P], pr[:, k % 2, m * P:(m + 1) * P], ident[:, :])
                    last.then_inc(ps_tr, 1)
                    if t == NT - 1:
                        pe.wait_ge(ps_pt, k + 1)
                        pe.wait_ge(vp_in, 16)
                        for c in range(4):
                            m0 = 4 * h + c
                            if m0 == 0:
                                pe.wait_ge(so_lo, 1)
                            if m0 >= 2:
                                pe.wait_ge(po_lo, m0 - 1)
                            for m in range(MT):
                                last = mm(pl[:, m0 % 2, :], vp[:, m, m0 * P:(m0 + 1) * P], ptt[:, h % 2, m, :],
                                          start=(m == 0), stop=(m == MT - 1))
                            last.then_inc(pv_done, 1)
            pe.wait_ge(po_lo, KC)
            summed(MO0, 16, y_hi, y_lo, r, norm2)
            variance(norm2)
            pe.wait_ge(sub_in, 16)
            for p in range(2):
                last = turn(pt[0][:, p * P:(p + 1) * P], sub_n[:, p, :], ident[:, :])
            last.then_inc(sub_tr, 1)
            norm2.wait(pe, "used", KC)
            pe.wait_ge(sub_cp, 1)

            def select_scores(u, s, first=False):
                pe.wait_ge(evacuated, u + 1)
                if not first:
                    pe.wait_ge(sc_out, u - WQ0)
                for t in range(NT):
                    mm(pl[:, 0, t * P:(t + 1) * P], q2[:, s, t * P:(t + 1) * P], sub_t[:, s, :], start=True, stop=True)
                mm(pl[0:NS, 1, 0:P], q2[:, s, SEQ:T], sub_t[:, s, :], start=True, stop=True).then_inc(sc_done, 1)
            pe_panel(pe, num(WQ0), h_hi, h_lo)
            pe_panel(pe, num(WQ0 + 1), h_hi, h_lo)
            select_scores(WQ0, 0, first=True)
            with pe.Fori(1, 8) as i:
                for d in range(2):
                    pe_panel(pe, in_loop(WQ0, i, d), h_hi, h_lo)
                    select_scores(i * 2 + (WQ0 + d - 1), (d + 1) % 2)
            select_scores(NPANEL - 1, 1)
            def turn_rows(q, j, g, dst):
                if g == 0:
                    pe.wait_ge(u_in[j], q * 16 + 16)
                if not (isinstance(q, int) and q == 0 and j == 0 and g < 2):
                    pe.wait_ge(t_lo, q * 8 + (4 * j + g - 1))
                for c in range(4):
                    last = turn(dst[:, c * P:(c + 1) * P], u_raw[:, j, (4 * g + c) * P:(4 * g + c + 1) * P], ident[:, :])
                last.then_inc(t_done, 1)

            def scores_of(q, j, between=None):
                pe.wait_ge(t_lo, q * 8 + 4 * (j + 1))
                for k in range(KC):
                    for w, x in ((ut_hi, h_hi), (ut_hi, h_lo), (ut_lo, h_hi)):
                        for b in range(2):
                            last = mm(pp[j][:, b, 0:HT], w[:, j, k, :], x[:, k, b * HT:(b + 1) * HT],
                                      start=(k == 0 and w is ut_hi and x is h_hi), stop=(k == KC - 1 and w is ut_lo))
                    if k == KC - 1:
                        last.then_inc(u_done, 1)
                    if between is not None and k % 4 == 3:
                        between(k // 4)

            def gate_matrix(n, s):
                pe.wait_ge(oh_ready, n + 1)
                if not (isinstance(n, int) and n < 2):
                    pe.wait_ge(g_out, n - 1)
                for x in range(4):
                    last = mm(pt[s][:, x * P:(x + 1) * P], oh[:, s, 0, x, :], oh[:, s, 1, x, :], start=True, stop=True)
                last.then_inc(g_done, 1)

            def ahead_column(q, j, tile=None, last=False):
                if not (isinstance(q, int) and q == 0):
                    pe.wait_ge(ge_done, q * 2 + (j - 1))

                def between(g):
                    if tile is not None:
                        for s in range(2):
                            gate_matrix(group(tile, j, g, s)[0], s)
                    if not last:
                        turn_rows(q + j, 1 - j, g, pl[:, g % 2, :])
                scores_of(q, j, between)

            pe.wait_ge(sc_out, 2 * PH)
            for g in range(4):
                turn_rows(0, 0, g, pl[:, g % 2, :])
            pe.wait_ge(evacuated, NPANEL)
            for j in range(2):
                ahead_column(0, j)
            with pe.Fori(1, PICK_COLS // 2) as q:
                for j in range(2):
                    ahead_column(q, j)
            pe.wait_ge(gw_ready, 1)
            for x in range(3):
                src = gw if x == 2 else ij[:, x]
                if x >= 1:
                    pe.wait_ge(ijt_out, x)
                for t in range(NT):
                    turn(pt[0][:, t * P:(t + 1) * P], src[:, t, :], ident[:, :])
                turn(pt[1][:, 0:NS], src[0:NS, NT, :], ident[0:NS, 0:NS]).then_inc(ijt_done, 1)
            pe.wait_ge(ijt_out, 3)
            gate_columns(pe, ahead_column)
            ahead_column(AHEAD - 1, 1, last=True)
            pe.wait_ge(g_out, T // 4)

            def values_of(q, c, par, slot, scores_between):
                if c < 2:
                    pe.wait_ge(pl_done, q * 2 + 2)
                    pe.wait_ge(vl_done, q * 2 + 2)
                if c < 2 and scores_between:
                    pe.wait_ge(ge_done, q * 2 + (3 + c))
                elif c < 2 and isinstance(q, int) and q == 0:
                    pe.wait_ge(ge_done, 2 * AHEAD - 1 + c)
                else:
                    pe.wait_ge(acc_done, q * KC + (c - 1))
                vh, _, vl = vslot[slot]
                for j in range(2):
                    for w, x in ((vh, p_hi), (vh, p_lo), (vl, p_hi)):
                        for b in range(2):
                            last = mm(pp[c % 2][:, b, 0:HT], w[:, j, c * P:(c + 1) * P],
                                      x[par][:, j, b * HT:(b + 1) * HT],
                                      start=(j == 0 and w is vh and x is p_hi), stop=(j == 1 and w is vl))
                last.then_inc(vd_done, 1)

            def pair_values(q, par, slot=0, scores_between=True, rows_of=None):
                for c in range(KC):
                    values_of(q, c, par, slot, scores_between)
                    if rows_of is not None and c % 2 == 1:
                        turn_rows(rows_of, c // 8, c // 2 % 4, pt[c // 2 % 2])

            for q in range(2):
                pair_values(q, q, q, False)
            with pe.Fori(1, AHEAD // 2 - 1) as i:
                for par in range(2):
                    pair_values(i * 2 + par, par, par, False)
            pair_values(AHEAD - 2, 0, 0, False, rows_of=AHEAD)

            def pair_step(q, par, more=True):
                for j in range(2):
                    pe.wait_ge(acc_done, q * KC - KC - 1 + j)
                    scores_of(q, j)
                pair_values(q - 1, 1 - par, rows_of=q + 1 if more else None)
            with pe.Fori(AHEAD // 2, NPAIR // 2 - 1) as i:
                for par in range(2):
                    pair_step(i * 2 + par, par)
            pair_step(NPAIR - 2, 0)
            pair_step(NPAIR - 1, 1, more=False)
            pair_values(NPAIR - 1, 1, scores_between=False)
            for c in range(KC):
                norm3.wait(pe, "hi", c + 1)
                for b in range(2):
                    last = mm(pl[:, b, 0:HT], mean16[:, :], r[:, c, b * HT:(b + 1) * HT], start=(c == 0), stop=(c == KC - 1))
            last.then_inc(nsem["mu"], 1)
            norm3.wait(pe, "mu_out", 1)
            for c in range(KC):
                norm3.wait(pe, "sq", c + 1)
                for b in range(2):
                    last = mm(pl[:, b, 0:HT], mean16[:, :], sq[:, c % 2, b, :], start=(c == 0), stop=(c == KC - 1))
                last.then_inc(nsem["var"], 1)
            for c in range(KC):
                norm3.wait(pe, "ya", c + 1)
                if c >= 2:
                    pe.wait_ge(o_a, c - 1)
                    pe.wait_ge(o_d, c - 1)
                for t in range(NT):
                    turn(pp[c % 2][:, 0, t * P:(t + 1) * P], ya[:, c % 2, t * P:(t + 1) * P], ident[:, :])
                turn(pp[c % 2][0:NS, 1, 0:P], ya[:, c % 2, SEQ:T], ident[:, :]).then_inc(nsem["used"], 1)

        @block.scalar
        def _(act):
            f = nc.scalar.activation

            def next_split(u):
                if isinstance(u[0], int):
                    act_split(act, num(u[0] + 1), first=u[0] + 1 < 2)
                else:
                    v = u[0] + 1
                    act_split(act, (v, 1 - u[1], u[2] + 16 * u[1]))

            def panel(use, split=True):
                def body(u, c):
                    if split:
                        next_split(u)
                    act.wait_ge(panel_done, u[0] + 1)
                    use(u, c)
                return body

            for m in range(NG * len(row_tiles)):
                act.wait_ge(tr_done, m + 1)
                ps, hi = row_views(m, 0)
                f(hi, ps, ACT.Copy).then_inc(tr_hi, 1)
            act_split(act, num(0), first=True)

            for k in range(2):
                def kv_use(u, c, k=k):
                    if not isinstance(u[0], int) or u[0] >= 2:
                        act.wait_ge(kvt_done, u[0] - 1)
                        if k == 0 or (isinstance(u[0], int) and u[0] < V0 // 2 + 2):
                            act.wait_ge(kt_stored[u[1]], (u[2] - 16) if k == 0 else 16 * 8)
                    f(kvt[:, u[1], :], pp[u[1]][:, 0, 0:MEM], ACT.Copy).then_inc(evacuated, 1)
                pairs(act, k * 16, 16, panel(kv_use), skip_first=2)

            def vt_use(u, c):
                f(vt[:, c, :].rearrange("p (b t) -> p b t", b=2), pp[u[1]][:, :, 0:HT],
                  ACT.Gelu_apprx_tanh).then_inc(evacuated, 1)
            act.wait_ge(kvn_ready, V0)
            for h in range(SH):
                act.wait_ge(ws_tr, h + 1)
                f(ws_t[:, h, :], pt[h % 2][:, 0:P], ACT.Copy).then_inc(ws_cp, 1)
            pairs(act, V0, 8, panel(vt_use))
            for k in range(2):
                act.wait_ge(nat_stored[k], 16 * V0 // 2)
            act.wait_ge(const_in, 16 * 9)
            act_norm(act, sgu_norm, sln_g, sln_b, vt)

            def u_use(u, c):
                if not isinstance(u[0], int) or c >= 2:
                    act.wait_ge(y_ready, c - 1)
                f(ug[:, u[1], :].rearrange("p (b t) -> p b t", b=2), pp[u[1]][:, :, 0:HT],
                  ACT.Gelu_apprx_tanh).then_inc(evacuated, 1)
                act.wait_ge(y_ready, c + 1)
                f(y_hi[:, c + SH, :], yf[:, u[1], :], ACT.Copy).then_inc(ysp_hi, 1)
            act.wait_ge(st_ready, SH)
            pairs(act, U0, 8, panel(u_use), skip_first=2)

            for g in range(4):
                for c in range(2):
                    def a_use(u, _, c=c):
                        if g == 0 and c == 0:
                            act.wait_ge(ysp_lo, SH)
                        if g >= 1:
                            act.wait_ge(pm_done, g)
                        f(dp[:, c, :].rearrange("p (b t) -> p b t", b=2), pp[u[1]][:, :, 0:HT], ACT.Copy)\
                            .then_inc(evacuated, 1)
                    panel(a_use)(num(A0 + 2 * g + c), 0)
                act.wait_ge(at_done, g + 1)
                if g == 0:
                    act.wait_ge(pool_zero, 2)
                else:
                    act.wait_ge(d_ready, g)
                    act.wait_ge(an_out, 16 * (DB + 1) * g)
                for c in range(2):
                    last = f(es[:, c, :, 1:16], pt[0][:, c * P:c * P + DB * STATE].rearrange("p (b s) -> p b s", b=DB),
                             ACT.Copy)
                last.then_inc(es_ready, 1)
                f(an[:, :, :], pt[1][0:STATE + NS, 0:2 * P].rearrange("p (c n) -> p c n", c=2), ACT.Copy)\
                    .then_inc(an_ready, 1)
                act.wait_ge(pm_done, g + 1)
                for c in range(2):
                    if c == 0:
                        f(yp[:, 0, :].rearrange("p (b t) -> p b t", b=2), pl[:, :, 0:HT], ACT.Copy,
                          scale=pscale[:, 2 * g:2 * g + 1]).then_inc(yp_ready, 1)
                    else:
                        for b in range(2):
                            last = f(yp[:, 1, b * HT:(b + 1) * HT], pt[b][:, 0:HT], ACT.Copy,
                                     scale=pscale[:, 2 * g + 1:2 * g + 2])
                        last.then_inc(yp_ready, 1)
                for c in range(2):
                    act.wait_ge(yp_ready, 2 * g + c + 1)
                    f(y_hi[:, 2 * g + c, :], yp[:, c, :], ACT.Copy).then_inc(pp_hi, 1)
            pairs(act, WO0, 16, lambda u, c: next_split(u))
            act_norm(act, norm1, ln_g[:, 0, :], ln_b[:, 0, :], r, h_hi)

            def q_use(u, c):
                f(qt[:, c, :].rearrange("p (b t) -> p b t", b=2), pp[u[1]][:, :, 0:HT], ACT.Copy).then_inc(evacuated, 1)
            pairs(act, MQ0, 14, panel(q_use))
            panel(q_use)(num(MQ0 + 14), 14)
            panel(q_use, split=False)(num(MQ0 + 15), 15)

            act.wait_ge(qm_ready, 1)
            for n in range(DB * AH):
                act.wait_ge(kr_tr, n + 1)
                if n >= 3:
                    act.wait_ge(ks_done, n - 2)
                f(kr[:, n % 3, 0:2, :], pt[0][:, :].rearrange("p (c m) -> p c m", c=2), ACT.Copy).then_inc(kr_a, 1)
            act.wait_ge(ss_max, 1)
            for h in range(AH):
                f(ssm[:, h, :], pp[h // 2][0:NS, h % 2, 0:MEM], ACT.Exp, bias=smx[:, 1, h:h + 1], scale=ASCALE,
                  accum_out=smx[:, 2, h:h + 1]).then_inc(ss_exp, 1)
            act.wait_ge(ss_tr, 1)
            f(pts[:, :, :], pt[0][:, 0:AH * MT * NS].rearrange("p (m t) -> p m t", t=NS), ACT.Copy).then_inc(ss_pt, 1)
            act.wait_ge(sv_done, DB)
            f(y_hi[:, :, SEQ:T], pl[:, 0, :].rearrange("p (c t) -> p c t", c=KC), ACT.Copy).then_inc(so_hi, 1)
            for n in range(AH * NT + 2):
                if n < AH * NT:
                    act.wait_ge(ps_max, n + 1)
                    if n >= 2:
                        act.wait_ge(ps_tr, n - 1)
                    f(pr[:, n % 2, :], pp[n // 2 % 2][:, n % 2, 0:MEM], ACT.Exp, bias=pst[:, n % 2, 1:2], scale=ASCALE,
                      accum_out=pst[:, n % 2, 2:3]).then_inc(ps_exp, 1)
                if n >= 2:
                    k = n - 2
                    h, t = k // NT, k % NT
                    act.wait_ge(ps_tr, k + 1)
                    if h >= 2:
                        act.wait_ge(pv_done, 4 * (h - 1))
                    f(ptt[:, h % 2, :, t * P:(t + 1) * P], pt[k % 2][:, 0:MEM].rearrange("p (m t) -> p m t", m=MT),
                      ACT.Copy).then_inc(ps_pt, 1)
                    if t == NT - 1:
                        for c in range(4):
                            act.wait_ge(pv_done, 4 * h + c + 1)
                            f(y_hi[:, 4 * h + c, 0:SEQ], pl[:, c % 2, :], ACT.Copy).then_inc(po_hi, 1)
            act.wait_ge(pv_done, KC)
            act_split(act, num(MO0))
            pairs(act, MO0, 16, lambda u, c: next_split(u))
            act_norm(act, norm2, ln_g[:, 1, :], ln_b[:, 1, :], r, h_hi)

            act.wait_ge(sub_tr, 1)
            f(sub_t[:, :, :], pt[0][:, 0:2 * P].rearrange("p (c n) -> p c n", c=2), ACT.Copy).then_inc(sub_cp, 1)

            def scores_out(c):
                act.wait_ge(sc_done, c + 1)
                f(sc[:, bass.ds(c, 1), 0:NT, :].rearrange("p x t k -> p (x t) k"),
                  pl[:, 0, :].rearrange("p (t k) -> p t k", t=NT), ACT.Copy)
                f(sc[0:NS, bass.ds(c, 1), NT, :].rearrange("p x k -> p (x k)"), pl[0:NS, 1, 0:P], ACT.Copy)\
                    .then_inc(sc_out, 1)

            def wq_use(u, c):
                if not isinstance(u[0], int) or c >= 2:
                    act.wait_ge(sc_done, c - 1)
                f(q2[:, u[1], :].rearrange("p (b t) -> p b t", b=2), pp[u[1]][:, :, 0:HT], ACT.Copy).then_inc(evacuated, 1)
                if not isinstance(u[0], int) or c >= 1:
                    scores_out(c - 1)
            act.wait_ge(sc_zero, 1)
            pairs(act, WQ0, 14, panel(wq_use), skip_first=2)
            panel(wq_use)(num(NPANEL - 2), 14)
            panel(wq_use, split=False)(num(NPANEL - 1), 15)
            scores_out(15)

            def rows_hi(q, j, g, src, used):
                act.wait_ge(t_done, q * 8 + (4 * j + g + 1))
                if used is not None:
                    act.wait_ge(u_done, used)
                f(ut_hi[:, j, 4 * g:4 * g + 4, :], src.rearrange("p (c i) -> p c i", c=4), ACT.Copy).then_inc(t_hi, 1)

            def ahead_gelu(q, j):
                act.wait_ge(u_done, q * 2 + (j + 1))
                if not (isinstance(q, int) and q == 0):
                    act.wait_ge(ge_stored[j], q * 16)
                f(ge2[:, j, :].rearrange("p (b t) -> p b t", b=2), pp[j][:, :, 0:HT], ACT.Gelu_apprx_tanh)\
                    .then_inc(ge_done, 1)

            def ahead_column(q, j, tile=None):
                if tile is not None and tile[0] >= 1:
                    act.wait_ge(g_stored, 32 * tile[0])
                for g in range(4):
                    if tile is not None:
                        for s in range(2):
                            n, t0 = group(tile, j, g, s)
                            act.wait_ge(g_done, n + 1)
                            f(gs[:, :, bass.ds(t0, 4)].rearrange("p j t -> p t j"),
                              pt[s][:, :].rearrange("p (t j) -> p t j", t=4), ACT.Copy).then_inc(g_out, 1)
                    first = isinstance(q, int) and q == 0 and j == 0
                    rows_hi(q + j, 1 - j, g, pl[:, g % 2, :], None if first else q * 2 + j)
                ahead_gelu(q, j)

            act.wait_ge(panel_done, NPANEL)
            for g in range(4):
                rows_hi(0, 0, g, pl[:, g % 2, :], None)
            for j in range(2):
                ahead_column(0, j)
            with act.Fori(1, PICK_COLS // 2) as q:
                for j in range(2):
                    ahead_column(q, j)
            act.wait_ge(g_sub, 1)
            f(gw[:, :, :], gw[:, :, :], ACT.Exp).then_inc(g_exp, 1)
            for x in range(3):
                act.wait_ge(ijt_done, x + 1)
                f(ijt[:, x, 0:SEQ], pt[0][:, :], ACT.Copy)
                f(ijt[:, x, SEQ:T], pt[1][:, 0:NS], ACT.Copy).then_inc(ijt_out, 1)
            gate_columns(act, ahead_column)

            def v_split_j(q, j, slot=0):
                act.wait_ge(v_in[j], q * 16 + 16)
                f(vslot[slot][0][:, j, :], vslot[slot][1][:, j, :], ACT.Copy).then_inc(vh_done, 1)

            def p_split_hi(q, par):
                for j in range(2):
                    act.wait_ge(gm_done, q * 2 + (j + 1))
                    f(p_hi[par][:, j, :], p_f[par][:, j, :], ACT.Copy).then_inc(ph_done, 1)

            p_split_hi(0, 0)
            for j in range(2):
                v_split_j(0, j)
            ahead_gelu(AHEAD - 1, 1)
            for j in range(2):
                act.wait_ge(ge_stored[j], 16 * AHEAD)

            def act_values(q, slot):
                p_split_hi(q, slot)
                for j in range(2):
                    v_split_j(q, j, slot)
            act_values(1, 1)
            with act.Fori(1, AHEAD // 2 - 1) as i:
                for slot in range(2):
                    act_values(i * 2 + slot, slot)
            act_values(AHEAD - 2, 0)

            def pair_rows(q, g0=0, g1=8):
                for g in range(g0, g1):
                    rows_hi(q, g // 4, g % 4, pt[g % 2][:, :], q * 2)
            pair_rows(AHEAD, 0, 2)
            p_split_hi(AHEAD - 1, 1)
            pair_rows(AHEAD, 2, 8)

            def act_pair(q, par, more=True):
                for j in range(2):
                    v_split_j(q - 1, j)
                for j in range(2):
                    act.wait_ge(u_done, q * 2 + (j + 1))
                    act.wait_ge(vd_done, q * KC - KC)
                    f(p_f[par][:, j, :].rearrange("p (b t) -> p b t", b=2), pp[j][:, :, 0:HT], ACT.Gelu_apprx_tanh)\
                        .then_inc(ge_done, 1)
                    act.wait_ge(gm_done, q * 2 + (j + 1))
                    f(p_hi[par][:, j, :], p_f[par][:, j, :], ACT.Copy).then_inc(ph_done, 1)
                if more:
                    pair_rows(q + 1)
            with act.Fori(AHEAD // 2, NPAIR // 2 - 1) as i:
                for par in range(2):
                    act_pair(i * 2 + par, par)
            act_pair(NPAIR - 2, 0)
            act_pair(NPAIR - 1, 1, more=False)
            for j in range(2):
                v_split_j(NPAIR - 1, j)

            def prompt_rows(c):
                if c >= 1:
                    k = c - 1
                    norm3.wait(act, "used", c)
                    if k >= 8 and k % 4 == 0:
                        act.wait_ge(o_out[k // 4 % 2], 32)
                    f(res[:, k // 4 % 2, :, k % 4, :], pp[k % 2][:, 0, :].rearrange("p (t n) -> p t n", t=NT),
                      ACT.Copy).then_inc(o_a, 1)
            act_norm(act, norm3, ln_g[:, 2, :], ln_b[:, 2, :], r, after=prompt_rows)

        @block.vector
        def _(dve):
            tt, ts, stt, copy = (nc.vector.tensor_tensor, nc.vector.tensor_scalar,
                                 nc.vector.scalar_tensor_tensor, nc.vector.tensor_copy)

            def split_next(u):
                dve_split(dve, (u[0] + 1, 1 - u[1], None))

            dve.wait_ge(const_ready, 1)
            for w, n in enumerate(WINDOWS):
                ts(inv_n[:, w, :], cnt[:, :], float(n), None, ALU.min)
            dve.drain()
            nc.vector.reciprocal(inv_n[:, :, :], inv_n[:, :, :])
            for m in range(NG * len(row_tiles)):
                dve.wait_ge(tr_hi, m + 1)
                ps, hi = row_views(m, 0)
                _, lo = row_views(m, 1)
                tt(lo, ps, hi.bitcast(F32), ALU.subtract).then_inc(tr_free, 1)
            dve_split(dve, num(0))

            def kv_copy(u):
                dve.wait_ge(kvt_done, u[0] + 1)
                if not isinstance(u[0], int) or u[0] >= 2:
                    dve.wait_ge(nat_stored[u[1]], u[2] - 16)
                copy(kvn[:, u[1]], pt[u[1]][:, 0:MEM].rearrange("p (m n) -> p m n", m=MT)).then_inc(kvn_ready, 1)

            def kv_use(u, c):
                split_next(u)
                if not isinstance(u[0], int) or u[0] >= 1:
                    kv_copy((u[0] - 1, 1 - u[1], u[2] - 16 * (1 - u[1])))
            pairs(dve, 0, V0, kv_use, skip_first=4)
            kv_copy(num(V0 - 1))

            pairs(dve, V0, 8, lambda u, c: split_next(u))

            def gate_of_head(c):
                if 1 <= c <= SH:
                    h = c - 1
                    sgu_norm.wait(dve, "used", c)
                    if h >= 2:
                        dve.wait_ge(s_done, h - 1)
                    copy(vn[:, h % 2], pt[0][:, :].rearrange("p (t d) -> p t d", t=NT))
                    copy(vns[:, h, :], pt[1][0:NS, 0:P]).then_inc(vn_ready, 1)
                if c >= 2:
                    h = c - 2
                    dve.wait_ge(s_done, h + 1)
                    tt(st[:, h, 0:SEQ].rearrange("p (t i) -> p t i", t=NT), pp[h % 2][:, 0, :].rearrange("p (t i) -> p t i", t=NT),
                       sgu_bias[:, h:h + 1, :].to_broadcast([P, NT, P]), ALU.add)
                    tt(st[:, h, SEQ:T].rearrange("p (b i) -> p b i", b=DB),
                       pp[h % 2][:, 1, 0:NS].rearrange("p (b i) -> p b i", b=DB),
                       sgu_bias[:, h:h + 1, 0:DS].to_broadcast([P, DB, DS]), ALU.add).then_inc(st_ready, 1)
            dve.wait_ge(bias_in, 16)
            dve_norm(dve, sgu_norm, vt, after=gate_of_head)

            def u_use(u, c):
                split_next(u)
                dve.wait_ge(evacuated, u[0] + 1)
                if not isinstance(u[0], int) or c >= 2:
                    dve.wait_ge(ysp_hi, c - 1)
                tt(yf[:, u[1], :], ug[:, u[1], :], st[:, c, :], ALU.mult).then_inc(y_ready, 1)
                dve.wait_ge(ysp_hi, c + 1)
                tt(y_lo[:, c + SH, :], yf[:, u[1], :], y_hi[:, c + SH, :].bitcast(F32), ALU.subtract).then_inc(ysp_lo, 1)
            dve.drain()
            pairs(dve, U0, 8, u_use, skip_first=2)

            for g, w in enumerate(WINDOWS):
                split_next(num(A0 + 2 * g))
                split_next(num(A0 + 2 * g + 1))
                dve.wait_ge(ep_ready, g + 1)
                dve.wait_ge(es_ready, g + 1)
                src, srcs = ep, es
                step, n = 1, 0
                while step < w:
                    dst, dsts = ((fa, fas), (fb, fbs))[n % 2]
                    lo = 2 * step - 1
                    tt(dst[:, :, lo:], src[:, :, lo:], src[:, :, lo - step:16 + SEQ - step], ALU.add)
                    tt(dsts[:, :, :, lo:], srcs[:, :, :, lo:], srcs[:, :, :, lo - step:20 - step], ALU.add)
                    dve.drain()
                    src, srcs, step, n = dst, dsts, 2 * step, n + 1
                for c in range(2):
                    stt(dp[:, c, SEQ:T].rearrange("p (b s) -> p b s", b=DB), srcs[:, c, :, 16:20], 1.0 / w,
                        es[:, c, :, 16:20], ALU.mult, ALU.subtract)
                stt(dp[:, :, 16:SEQ], src[:, :, 32:], 1.0 / w, ep[:, :, 32:], ALU.mult, ALU.subtract)
                tt(dp[:, :, 0:16], src[:, :, 16:32], inv_n[:, g:g + 1, :].to_broadcast([P, 2, 16]), ALU.mult)
                dve.drain()
                tt(dp[:, :, 0:16], dp[:, :, 0:16], ep[:, :, 16:32], ALU.subtract).then_inc(d_ready, 1)
                for c in range(2):
                    dve.wait_ge(pp_hi, 2 * g + c + 1)
                    if g == 3 and c == 1:
                        dve.wait_ge(pm_done, 4)
                    tt(y_lo[:, 2 * g + c, :], yp[:, c, :], y_hi[:, 2 * g + c, :].bitcast(F32), ALU.subtract)\
                        .then_inc(pp_lo, 1)

            def residual(u, c, free=None):
                split_next(u)
                dve.wait_ge(panel_done, u[0] + 1)
                tt(yt[:, u[1], :], h_hi[:, c, :].bitcast(F32), h_lo[:, c, :].bitcast(F32), ALU.add)
                dve.drain()
                stt(r[:, c, :].rearrange("p (b t) -> p b t", b=2), yt[:, u[1], :].rearrange("p (b t) -> p b t", b=2),
                    ALPHA, pp[u[1]][:, :, 0:HT], ALU.mult, ALU.add).then_inc(evacuated, 1)
            dve.drain()
            pairs(dve, WO0, 16, residual)
            dve_norm(dve, norm1, r, h_lo, h_hi)
            pairs(dve, MQ0, 14, lambda u, c: split_next(u))
            split_next(num(MQ0 + 14))

            dve.wait_ge(qm_zero, 1)
            dve.wait_ge(evacuated, MO0)
            copy(qm[:, :, :].rearrange("p c (b x) -> p c b x", x=36)[:, :, :, 0:DS],
                 qt[:, :, SEQ:T].rearrange("p c (b s) -> p c b s", b=DB)).then_inc(qm_ready, 1)
            for n in range(DB * AH):
                dve.wait_ge(kr_tr, n + 1)
                if n >= 3:
                    dve.wait_ge(ks_done, n - 2)
                copy(kr[:, n % 3, 2:4, :], pt[1][:, :].rearrange("p (c m) -> p c m", c=2)).then_inc(kr_d, 1)
            dve.wait_ge(ks_done, DB * AH)
            for h in range(AH):
                nc.vector.tensor_reduce(smx[:, 0, h:h + 1], pp[h // 2][0:NS, h % 2, 0:MEM], AX.X, ALU.max)
            dve.drain()
            ts(smx[:, 1, :], smx[:, 0, :], -ASCALE, None, ALU.mult).then_inc(ss_max, 1)
            dve.wait_ge(ss_exp, AH)
            nc.vector.reciprocal(smx[:, 3, :], smx[:, 2, :])
            dve.drain()
            for h in range(AH):
                last = ts(ssm[:, h, :], ssm[:, h, :], smx[:, 3, h:h + 1], None, ALU.mult)
            last.then_inc(ss_p, 1)
            dve.wait_ge(so_hi, 1)
            tt(y_lo[:, :, SEQ:T], pl[:, 0, :].rearrange("p (c t) -> p c t", c=KC), y_hi[:, :, SEQ:T].bitcast(F32),
               ALU.subtract).then_inc(so_lo, 1)
            for n in range(AH * NT + 2):
                if n < AH * NT:
                    dve.wait_ge(ps_done, n + 1)
                    if n >= 2:
                        dve.wait_ge(ps_exp, n - 1)
                    nc.vector.tensor_reduce(pst[:, n % 2, 0:1], pp[n // 2 % 2][:, n % 2, 0:MEM], AX.X, ALU.max)
                    dve.drain()
                    ts(pst[:, n % 2, 1:2], pst[:, n % 2, 0:1], -ASCALE, None, ALU.mult).then_inc(ps_max, 1)
                    dve.wait_ge(ps_exp, n + 1)
                    nc.vector.reciprocal(pst[:, n % 2, 3:4], pst[:, n % 2, 2:3])
                    dve.drain()
                    ts(pr[:, n % 2, :], pr[:, n % 2, :], pst[:, n % 2, 3:4], None, ALU.mult).then_inc(ps_p, 1)
                if n >= 2 and (n - 2) % NT == NT - 1:
                    h = (n - 2) // NT
                    for c in range(4):
                        dve.wait_ge(po_hi, 4 * h + c + 1)
                        if h == 0 and c == 0:
                            dve.wait_ge(sv_done, DB)
                        tt(y_lo[:, 4 * h + c, 0:SEQ], pl[:, c % 2, :], y_hi[:, 4 * h + c, 0:SEQ].bitcast(F32),
                           ALU.subtract).then_inc(po_lo, 1)
            dve_split(dve, num(MO0))
            pairs(dve, MO0, 16, residual)
            dve_norm(dve, norm2, r, h_lo, h_hi)

            mx, mi, mr = nc.vector.max, nc.vector.max_index, nc.vector.match_replace
            NT1 = NT + 1

            def top16(vals, spare, best, where, between=lambda: None):
                for t in range(NT1):
                    mx(best[:, t, 0:8], vals[:, t, :])
                dve.drain()
                for t in range(NT1):
                    mi(where[:, t, 0:8], best[:, t, 0:8], vals[:, t, :])
                between()
                for t in range(NT1):
                    mr(spare[:, t, :], best[:, t, 0:8], vals[:, t, :], NEG)
                dve.drain()
                between()
                for t in range(NT1):
                    mx(best[:, t, 8:16], spare[:, t, :])
                dve.drain()
                between()
                for t in range(NT1):
                    last = mi(where[:, t, 8:16], best[:, t, 8:16], spare[:, t, :])
                return last

            def pick(h):
                dve.wait_ge(cand_ready, h + 1)
                best = gw[:, :, h * TOPK:(h + 1) * TOPK]
                next_rows()
                top16(cand, cand2, best, fi, next_rows)
                dve.drain()
                nc.vector.tensor_single_scalar(ab_u[:, 0], fi[:, :, :], 4, ALU.logical_shift_right)
                nc.vector.tensor_single_scalar(ab_u[:, 1], fi[:, :, :], 15, ALU.bitwise_and)
                dve.drain()
                copy(ab_f[:, :], ab_u[:, :]).then_inc(fin_ready, 1)
                next_rows()
                dve.drain()
                if h >= 1:
                    next_rows()
                    dve.wait_ge(pool_step, PICK_STEPS * h)
                tt(eq[:, :, :, :, :].rearrange("p x t k y -> p (x t k) y"),
                   iota16[:, :].rearrange("p (n y) -> p n y", n=1).to_broadcast([P, 2 * NT1 * TOPK, TOPK]),
                   ab_f[:, :].rearrange("p x t (k y) -> p (x t k) y", y=1).to_broadcast([P, 2 * NT1 * TOPK, TOPK]),
                   ALU.is_equal).then_inc(eq_ready, 1)

            def half_list(c):
                dve.wait_ge(sc_out, c + 1)
                h, p = c // 2, c % 2
                top16(sc[:, c], sc2, sv[:, h, p], si[:, h, p])
                dve.drain()
                copy(sif[:, h, p], si[:, h, p]).then_inc(sif_ready, 1)

            for c in range(2 * PH):
                if c < 2 * PH - 1:
                    split_next(num(WQ0 + c))
                if c >= 2:
                    half_list(c - 2)

            def rows_lo(q, j, g, src):
                dve.wait_ge(t_hi, q * 8 + (4 * j + g + 1))
                tt(ut_lo[:, j, 4 * g:4 * g + 4, :], src.rearrange("p (c i) -> p c i", c=4),
                   ut_hi[:, j, 4 * g:4 * g + 4, :].bitcast(F32), ALU.subtract).then_inc(t_lo, 1)
            turned = [0]

            def next_rows():
                n = turned[0]
                if n < 4 * (PICK_COLS + 1):
                    rows_lo(n // 8, n // 4 % 2, n % 4, pl[:, n % 2, :])
                    turned[0] += 1
            for c in (2 * PH - 2, 2 * PH - 1):
                half_list(c)
                next_rows()
                next_rows()
            for h in range(PH):
                pick(h)
            while turned[0] < 4 * (PICK_COLS + 1):
                next_rows()
            dve.drain()
            gw4 = gw[:, :, :].rearrange("p t (h k) -> p (t h) k", k=TOPK)
            copy(sums[:, 0, :], gw4[:, :, 0:1].rearrange("p n k -> p (n k)"))
            dve.drain()
            tt(gw4, gw4, sums[:, 0, :].rearrange("p (n k) -> p n k", k=1).to_broadcast([P, 40, TOPK]), ALU.subtract)\
                .then_inc(g_sub, 1)
            dve.wait_ge(g_exp, 1)
            nc.vector.tensor_reduce(sums[:, 0, :], gw4, AX.X, ALU.add)
            dve.drain()
            nc.vector.reciprocal(sums[:, 1, :], sums[:, 0, :])
            dve.drain()
            tt(gw4, gw4, sums[:, 1, :].rearrange("p (n k) -> p n k", k=1).to_broadcast([P, 40, TOPK]), ALU.mult)
            dve.wait_ge(pool_step, PICK_STEPS * PH)
            dve.drain()
            copy(sums[:, 0, 0:1], sums[:, 1, 0:1]).then_inc(gw_ready, 1)
            dve.wait_ge(ijt_out, 3)

            def one_hot(n, s, t0):
                if not (isinstance(n, int) and n < 2):
                    dve.wait_ge(g_done, n - 1)
                for x in range(4):
                    ts(oh[:, s, 0, x, :], iota_k[:, :], ijt[:, 0, bass.ds(t0 + x, 1)], None, ALU.is_equal)
                    last = ts(oh[:, s, 1, x, :], iota_k[:, :], ijt[:, 1, bass.ds(t0 + x, 1)],
                              ijt[:, 2, bass.ds(t0 + x, 1)], ALU.is_equal, ALU.mult)
                last.then_inc(oh_ready, 1)

            def ahead_column(q, j, tile=None):
                for g in range(4):
                    if tile is not None:
                        for s in range(2):
                            n, t0 = group(tile, j, g, s)
                            one_hot(n, s, t0 + P * tile[0])
                    rows_lo(q + j, 1 - j, g, pl[:, g % 2, :])
            gate_columns(dve, ahead_column)

            def gated(q, par, j):
                if j == 0:
                    dve.wait_ge(g_in, q * 16 + 16)
                tt(p_f[par][:, j, :], p_f[par][:, j, :], g2[:, j, :], ALU.mult).then_inc(gm_done, 1)

            def p_split_lo(q, par, j):
                dve.wait_ge(ph_done, q * 2 + (j + 1))
                tt(p_lo[par][:, j, :], p_f[par][:, j, :], p_hi[par][:, j, :].bitcast(F32), ALU.subtract).then_inc(pl_done, 1)

            def v_split(q, j, slot=0):
                dve.wait_ge(vh_done, q * 2 + (j + 1))
                vh, vr, vl = vslot[slot]
                tt(vl[:, j, :], vr[:, j, :], vh[:, j, :].bitcast(F32), ALU.subtract).then_inc(vl_done, 1)

            def add_out(q, c):
                dve.wait_ge(vd_done, q * KC + (c + 1))
                a3 = acc[:, c, :].rearrange("p (b t) -> p b t", b=2)
                tt(a3, a3, pp[c % 2][:, :, 0:HT], ALU.add).then_inc(acc_done, 1)

            def ahead_gated(q, par, j):
                if j == 0:
                    dve.wait_ge(s_in, q * 16 + 16)
                gated(q, par, j)

            for j in range(2):
                ahead_gated(0, 0, j)
            for j in range(2):
                p_split_lo(0, 0, j)
            for j in range(2):
                v_split(0, j)
            dve.wait_ge(acc_zero, 1)

            def dve_values(q, par, slot, values=True, rows=False):
                for c in range(KC):
                    add_out(q - 1, c)
                    if c in (3, 4):
                        ahead_gated(q, par, c - 3)
                    if c in (6, 7):
                        p_split_lo(q, par, c - 6)
                    if values and c in (9, 11):
                        v_split(q, (c - 9) // 2, slot)
                    if rows and c % 2 == 1:
                        rows_lo(AHEAD, c // 8, c // 2 % 4, pt[c // 2 % 2][:, :])
            dve_values(1, 1, 1)
            with dve.Fori(1, AHEAD // 2 - 1) as i:
                for slot in range(2):
                    dve_values(i * 2 + slot, slot, slot)
            dve_values(AHEAD - 2, 0, 0)
            dve_values(AHEAD - 1, 1, 0, values=False, rows=True)

            def dve_pair(q, par, more=True):
                for j in range(2):
                    v_split(q - 1, j)
                for j in range(2):
                    dve.wait_ge(ge_done, q * 2 + (j + 1))
                    gated(q, par, j)
                    p_split_lo(q, par, j)
                for g in range(8):
                    add_out(q - 1, 2 * g)
                    add_out(q - 1, 2 * g + 1)
                    if more:
                        rows_lo(q + 1, g // 4, g % 4, pt[g % 2][:, :])
            with dve.Fori(AHEAD // 2, NPAIR // 2 - 1) as i:
                for par in range(2):
                    dve_pair(i * 2 + par, par)
            dve_pair(NPAIR - 2, 0)
            dve_pair(NPAIR - 1, 1, more=False)
            for j in range(2):
                v_split(NPAIR - 1, j)
            for c in range(KC):
                add_out(NPAIR - 1, c)
            for c in range(KC + 2):
                if c < KC:
                    tt(yt[:, c % 2, :], h_hi[:, c, :].bitcast(F32), h_lo[:, c, :].bitcast(F32), ALU.add)
                    dve.drain()
                    stt(r[:, c, :], yt[:, c % 2, :], ALPHA, acc[:, c, :], ALU.mult, ALU.add).then_inc(nsem["hi"], 1)

            def sample_rows(c):
                if 1 <= c <= KC:
                    k = c - 1
                    norm3.wait(dve, "used", c)
                    if k >= 8 and k % 4 == 0:
                        dve.wait_ge(o_out[k // 4 % 2], 32)
                    copy(ress[:, k // 4 % 2, k % 4, :], pp[k % 2][0:NS, 1, 0:P]).then_inc(o_d, 1)
            dve_norm(dve, norm3, r, after=sample_rows)

        @block.gpsimd
        def _(pool):
            g = nc.gpsimd
            g.memset(ident[:, :], 0.0).then_inc(ident_zero, 1)
            g.memset(mean16[:, :], 1.0 / D).then_inc(ident_ready, 1)
            g.memset(mean8[:, :], 1.0 / (D // 2)).then_inc(ident_ready, 1)
            pool.wait_ge(ident_zero, 1)
            g.affine_select(out=ident[:, :], in_=ident[:, :], compare_op=ALU.not_equal, fill=1.0, base=0,
                            pattern=[[-1, P]], channel_multiplier=1).then_inc(ident_ready, 1)
            g.iota(cnt[:, :], pattern=[[1, 16]], base=1, channel_multiplier=0,
                   allow_small_or_imprecise_dtypes=True).then_inc(const_ready, 1)

            def vector_in(dst, src):
                pool.dma_start(dst, src.rearrange("(c p) -> p c", p=P), allow_slow_non_contiguous=True)\
                    .then_inc(const_in, 16)
            for n, name in enumerate(("ln1", "ln2", "ln3")):
                vector_in(ln_g[:, n, :], a[name + "_g"][0])
                vector_in(ln_b[:, n, :], a[name + "_b"][0])
            vector_in(sln_g[:, :], a["sgu_ln_g"][0])
            vector_in(sln_b[:, :], a["sgu_ln_b"][0])
            vector_in(pscale[:, :], a["pool_scale"][0])
            pool.dma_start(o["ps"][0][:, 0:STATE - DS, :], a["cache_pool"][0][:, DS:STATE, :]).then_inc(state_out, 16)

            def kv_store(k):
                out = o["kv"[k]][0, 0].rearrange("(m p) h d -> p m (h d)", p=P).rearrange("p m (c n) -> p m c n", n=P)

                def body(u, c):
                    if k == 0:
                        pool.wait_ge(evacuated, u[0] + 1)
                        pool.dma_start(k_scr[c], kvt[:, u[1], :]).then_inc(kt_stored[u[1]], 16)
                    pool.wait_ge(kvn_ready, u[0] + 1)
                    pool.dma_start(out[:, :, c, :], kvn[:, u[1]]).then_inc(nat_stored[u[1]], 16)
                return body
            pairs(pool, MK0, 16, kv_store(0))
            pool.dma_start(ws_n[:, :, :], a["sgu_w"][0].rearrange("h i j -> i h j")).then_inc(ws_in, 16)
            pool.dma_start(sgu_bias[:, :, :], a["sgu_b"][0:1].to_broadcast([P, SH, P])).then_inc(bias_in, 16)
            g.memset(ws_s[:, :, :], 0.0).then_inc(ws_zero, 1)
            pairs(pool, MV0, 16, kv_store(1))
            pool.wait_ge(ws_cp, SH)
            g.affine_select(out=ws_t[:, :, :], in_=ws_t[:, :, :], compare_op=ALU.is_ge, fill=0.0, base=0,
                            pattern=[[0, SH], [1, P]], channel_multiplier=-1).then_inc(ws_ready, 1)
            pool.wait_ge(ws_ready, 1)
            pool.wait_ge(ws_zero, 1)
            for b in range(DB):
                pool.dma_start(ws_s[DS * b:DS * (b + 1), :, DS * b:DS * (b + 1)], ws_t[0:DS, :, 0:DS])\
                    .then_inc(ws_sin, 16)
            pool.wait_ge(vn_ready, SH)
            pool.dma_start(o["vs"][0].rearrange("b s d -> (b s) d"), vns[:, :, :].rearrange("p h d -> p (h d)"))\
                .then_inc(v_state_out, 16)
            pool.wait_ge(st_ready, SH)
            pool.dma_start(cpn[:, :], a["cache_pool"][0].rearrange("b s d -> (b s) d")).then_inc(cp_in, 16)
            pool.wait_ge(v_state_out, 16)
            pool.wait_ge(ysp_lo, SH)
            g.memset(ep[:, :, 0:16], 0.0).then_inc(pool_zero, 1)
            g.memset(es[:, :, :, 0:1], 0.0).then_inc(pool_zero, 1)
            for n in range(4):
                if n >= 1:
                    pool.wait_ge(pm_done, n)
                pool.dma_start(pw[:, :, :], a["pool_w"][0, n].rearrange("(k p) d -> p k d", p=P)).then_inc(pw_in, 16)
                pool.wait_ge(evacuated, A0 + 2 * n + 2)
                if n >= 1:
                    pool.wait_ge(d_ready, n)
                g.tensor_copy(ep[:, :, 16:], dp[:, :, 0:SEQ])
                g.tensor_copy(es[:, :, :, 16:20], dp[:, :, SEQ:T].rearrange("p c (b s) -> p c b s", b=DB))\
                    .then_inc(ep_ready, 1)
                pool.wait_ge(an_ready, n + 1)
                cs = slice(2 * n * P, 2 * (n + 1) * P)
                pool.dma_start(o["pp"][0, 0, :, cs], an[0:STATE].rearrange("p c n -> p (c n)")).then_inc(an_out, 16)
                for b in range(DB):
                    pool.dma_start(o["ps"][0, b, STATE - DS:STATE, cs],
                                   an[STATE + DS * b:STATE + DS * (b + 1)].rearrange("p c n -> p (c n)"))\
                        .then_inc(an_out, 16)
            pool.wait_ge(an_out, 16 * 4 * (DB + 1))
            pool.wait_ge(panel_done, MO0)
            g.memset(qm[:, :, :], 0.0).then_inc(qm_zero, 1)
            pool.wait_ge(panel_done, WQ0)
            pool.dma_start(sub_n[:, :, :], a["peer_subkeys"][0].rearrange("s k d -> k s d")).then_inc(sub_in, 16)
            g.memset(sc[:, :, NT, :], 0.0).then_inc(sc_zero, 1)
            norm2.wait(pool, "used", KC)
            g.iota(iota_k[:, :], pattern=[[1, P]], base=0, channel_multiplier=0, allow_small_or_imprecise_dtypes=True)
            g.iota(iota16[:, :], pattern=[[1, TOPK]], base=0, channel_multiplier=0,
                   allow_small_or_imprecise_dtypes=True).then_inc(iota_ready, 1)

            steps = [0]

            def step(ins):
                ins.then_inc(pool_step, 1)
                steps[0] += 1
                pool.wait_ge(pool_step, steps[0])
            pool.wait_ge(iota_ready, 1)
            NT1 = NT + 1

            def picks(h):
                pool.wait_ge(eq_ready, h + 1)
                step(g.tensor_tensor(eq4, eq4, sif[:, h].rearrange("p x t (k y) -> p (x t) k y", k=1)
                                     .to_broadcast([P, 2 * NT1, TOPK, TOPK]), ALU.mult))
                for w in (8, 4, 2):
                    step(g.tensor_tensor(eq4[:, :, :, 0:w], eq4[:, :, :, 0:w], eq4[:, :, :, w:2 * w], ALU.add))
                step(g.tensor_tensor(ij[:, :, :, h * TOPK:(h + 1) * TOPK].rearrange("p x t k -> p (x t) k"),
                                     eq4[:, :, :, 0:1].rearrange("p n k y -> p n (k y)"),
                                     eq4[:, :, :, 1:2].rearrange("p n k y -> p n (k y)"), ALU.add))
            eq4 = eq[:, :, :, :, :].rearrange("p x t k y -> p (x t) k y")

            for h in range(PH):
                pool.wait_ge(sif_ready, 2 * h + 2)
                if h >= 1:
                    pool.wait_ge(fin_ready, h)
                cv = cand[:, :, :].rearrange("p t (x y) -> p t x y", x=TOPK)
                g.tensor_tensor(cv, sv[:, h, 0].rearrange("p t (x y) -> p t x y", y=1).to_broadcast([P, NT1, TOPK, TOPK]),
                                sv[:, h, 1].rearrange("p t (x y) -> p t x y", x=1).to_broadcast([P, NT1, TOPK, TOPK]),
                                ALU.add).then_inc(cand_ready, 1)
                if h >= 1:
                    picks(h - 1)
            picks(PH - 1)
            assert steps[0] == PICK_STEPS * PH
            for t in range(NT + 1):
                n0 = P // 4 * (t + 1) if t < NT else T // 4
                pool.wait_ge(g_out, n0)
                w = P if t < NT else NS
                for c in range(2):
                    pool.dma_start(g_scr[:, 64 * c:64 * (c + 1), t * P:t * P + w], gs[:, 64 * c:64 * (c + 1), 0:w])\
                        .then_inc(g_stored, 16)
            pool.wait_ge(g_stored, 32 * (NT + 1))
            g.memset(acc[:, :, :], 0.0).then_inc(acc_zero, 1)
            xs = o["xs"].rearrange("b s d -> (b s) d")
            for k in range(4):
                pool.wait_ge(o_a, 4 * (k + 1))
                pool.wait_ge(o_d, 4 * (k + 1))
                pool.dma_start(o["xp"][0].rearrange("(t p) d -> p t d", p=P)[:, :, k * 512:(k + 1) * 512],
                               res[:, k % 2].rearrange("p t c n -> p t (c n)")).then_inc(o_out[k % 2], 16)
                pool.dma_start(xs[:, k * 512:(k + 1) * 512], ress[:, k % 2].rearrange("p c n -> p (c n)"))\
                    .then_inc(o_out[k % 2], 16)
            for k in range(2):
                pool.wait_ge(o_out[k], 64)
            for k in range(2):
                pool.wait_ge(kt_stored[k], 16 * 8)
                pool.wait_ge(nat_stored[k], 16 * 16)
            pool.wait_ge(state_out, 16)


_INS = ["x_prompt", "x_sample", "mem_prompt", "cache_pool", "cache_mem_k", "cache_mem_v", "w_in", "pool_w", "pool_scale",
        "sgu_ln_g", "sgu_ln_b", "sgu_w", "sgu_b", "w_out", "ln1_g", "ln1_b", "w_mq", "w_mk", "w_mv", "w_mo",
        "ln2_g", "ln2_b", "peer_wq", "peer_subkeys", "peer_u", "peer_v", "ln3_g", "ln3_b"]
_OUTS = {"xp": (1, SEQ, D), "xs": (DB, DS, D), "pp": (1, 1, STATE, D_POOL), "k": (1, 1, MEM, AH, D // AH),
         "v": (1, 1, MEM, AH, D // AH), "ps": (1, DB, STATE, D_POOL), "vs": (1, DB, DS, D // 2)}


def kernel(**inputs):
    import numpy as _np
    import concourse.bacc as _bacc
    from concourse.bass_utils import run_bass_kernel_spmd as _run

    nc = _bacc.Bacc("TRN2", target_bir_lowering=False, num_devices=1)
    arrays, args = {}, {}
    for name in _INS:
        arr = _np.ascontiguousarray(inputs[name])
        arrays["in_" + name] = arr
        args[name] = nc.dram_tensor("in_" + name, arr.shape, F32, kind="ExternalInput").ap()
    outs = {name: nc.dram_tensor("out_" + name, shape, F32, kind="ExternalOutput").ap() for name, shape in _OUTS.items()}
    program(nc, args, outs)
    res = _run(nc, [arrays], core_ids=[0])
    return tuple(res.results[0]["out_" + name] for name in _OUTS)
```

```python
from contextlib import ExitStack

import concourse.bass as bass
from concourse import mybir

ALU = mybir.AluOpType
ACT = mybir.ActivationFunctionType
AX = mybir.AxisListType
F32 = mybir.dt.float32
FR = mybir.dt.float32r
U32 = mybir.dt.uint32

P = 128
D = 2048
KC = D // P
SEQ = 512
NT = SEQ // P
DB, DS = 8, 4
NS = DB * DS
T = SEQ + NS
HT = T // 2
D_POOL = 1024
PC = D_POOL // P
WINDOWS = (2, 4, 8, 16)
STATE = 15
SH = 8
MEM = 256
MT = MEM // P
AH = 4
PH = 8
TOPK = 16
NK = 128
NPAIR = NK // 2
ALPHA = 2.0 ** 0.25
EPS = 1e-5
ASCALE = float(D // AH) ** -0.5
NEG = -3.0e38

MK0, MV0, V0, U0, A0, WO0, MQ0, MO0, WQ0, NPANEL = 0, 16, 32, 40, 48, 56, 72, 88, 104, 120

BASE = 16512
XB = KC * T * 4
H_HI, H_LO, Y_HI, Y_LO = (BASE + n * XB for n in range(4))
RAW = BASE + 4 * XB
W_HI = RAW + 2 * D * 4
W_LO = W_HI + 2 * D * 4
CST = W_LO + 2 * D * 4
TMP = CST + 2368
TOP = 229344


def program(nc, a, o):
    ctx = ExitStack()
    with ctx:
        def at(name, offset, shape, dt=F32):
            size = 4
            for s in shape[1:]:
                size *= s
            assert offset + size <= TOP, name
            return nc.alloc_sbuf_tensor_at(name, shape, dt, offset=offset)

        def sem(name):
            return ctx.enter_context(nc.semaphore(name))

        h_hi = at("h_hi", H_HI, [P, KC, T], FR)
        h_lo = at("h_lo", H_LO, [P, KC, T], FR)
        r = at("r", H_HI, [P, KC, T])
        y_hi = at("y_hi", Y_HI, [P, KC, T], FR)
        y_lo = at("y_lo", Y_LO, [P, KC, T], FR)
        raw = at("raw", RAW, [P, 2, KC, P])
        w_hi = at("w_hi", W_HI, [P, 2, KC, P], FR)
        w_lo = at("w_lo", W_LO, [P, 2, KC, P], FR)
        ident = at("ident", CST, [P, P])
        mean16 = at("mean16", CST + 512, [P, P])
        mean8 = at("mean8", CST + 1024, [P, P])
        ln_g = at("ln_g", CST + 1536, [P, 3, KC])
        ln_b = at("ln_b", CST + 1728, [P, 3, KC])
        sln_g = at("sln_g", CST + 1920, [P, SH])
        sln_b = at("sln_b", CST + 1952, [P, SH])
        pscale = at("pscale", CST + 1984, [P, PC])
        inv_n = at("inv_n", CST + 2016, [P, 4, 16])
        cnt = at("cnt", CST + 2272, [P, 16])
        mu = at("mu", TMP, [P, 2, HT])
        rs = at("rs", TMP + 2176, [P, 2, HT])
        sq = at("sq", TMP + 2 * 2176, [P, 2, 2, HT])
        yt = at("yt", TMP + 4 * 2176, [P, 2, T])
        ya = at("ya", TMP + 6 * 2176, [P, 3, T])

        pp = [ctx.enter_context(nc.psum_tensor(f"pp{i}", [P, 2, 512], F32)) for i in range(2)]
        pt = [ctx.enter_context(nc.psum_tensor(f"pt{i}", [P, 512], F32)) for i in range(2)]
        pl = ctx.enter_context(nc.psum_tensor("pl", [P, 2, 512], F32))

        k_scr = nc.dram_tensor("k_scr", [KC, P, MEM], F32).ap()
        g_scr = nc.dram_tensor("g_scr", [P, NK, T], F32).ap()

        def panels(w):
            return w.rearrange("(k p) (c n) -> p k c n", p=P, n=P)
        w_in = panels(a["w_in"][0])
        streams = [(MK0, panels(a["w_mk"][0]), 0, 16), (MV0, panels(a["w_mv"][0]), 0, 16),
                   (V0, w_in, 16, 8), (U0, w_in, 8, 8), (A0, w_in, 0, 8),
                   (WO0, panels(a["w_out"][0]), 0, 16), (MQ0, panels(a["w_mq"][0]), 0, 16),
                   (MO0, panels(a["w_mo"][0]), 0, 16), (WQ0, panels(a["peer_wq"][0]), 0, 16)]

        raw_in = [sem("raw_in0"), sem("raw_in1")]
        hi_ready = sem("hi_ready")
        lo_ready = sem("lo_ready")
        panel_done = sem("panel_done")
        evacuated = sem("evacuated")

        const_in = sem("const_in")
        bias_in, ws_sin, ident_zero, pool_step, sif_ready = (sem("bias_in"), sem("ws_sin"), sem("ident_zero"),
                                                             sem("pool_step"), sem("sif_ready"))
        ident_ready = sem("ident_ready")
        const_ready = sem("const_ready")
        row_in = [sem("row_in0"), sem("row_in1"), sem("row_in2")]
        tr_done, tr_hi, tr_free = sem("tr_done"), sem("tr_hi"), sem("tr_free")
        kvt_done, kvn_ready = sem("kvt_done"), sem("kvn_ready")
        kt_stored = [sem("kt_stored0"), sem("kt_stored1")]
        nat_stored = [sem("nat_stored0"), sem("nat_stored1")]

        nsem = {"mu": sem("norm_mu"),
                "mu_out": sem("norm_mu_out"),
                "xc": sem("norm_xc"),
                "sq": sem("norm_sq"),
                "var": sem("norm_var"),
                "veps": sem("norm_veps"),
                "std": sem("norm_std"),
                "yt": sem("norm_yt"),
                "ya": sem("norm_ya"),
                "hi": sem("norm_hi"),
                "used": sem("norm_used")}
        shift_done, shift_out = sem("shift_done"), sem("shift_out")
        less_mu = sem("less_mu")

        class Norm:
            def __init__(self, k, base, n, slots=2):
                self.k, self.base, self.n, self.slots = k, base, n, slots

            def wait(self, eng, name, count):
                before = self.k if name in ("mu", "mu_out", "veps", "std") else self.base
                if name == "hi":
                    before -= 8 if self.k else 0
                eng.wait_ge(nsem[name], before + count)
        sgu_norm, norm1, norm2, norm3 = Norm(0, 0, 8), Norm(1, 8, 16, 3), Norm(2, 24, 16, 3), Norm(3, 40, 16, 3)

        block = ctx.enter_context(nc.Block())

        def pe_panel(pe, u, x_hi, x_lo, first=False, n=T):
            s = u[1]
            pe.wait_ge(lo_ready, u[0] + 1)
            if not first:
                pe.wait_ge(evacuated, u[0] - 1)
            parts = [(0, 0, HT), (1, HT, T)] if n == T else [(0, 0, n)]
            for k in range(KC):
                for w, x in ((w_hi, x_hi), (w_hi, x_lo), (w_lo, x_hi)):
                    for b, t0, t1 in parts:
                        last = nc.tensor.matmul(pp[s][:, b, 0:t1 - t0], w[:, s, k, :], x[:, k, t0:t1],
                                                start=(k == 0 and w is w_hi and x is x_hi),
                                                stop=(k == KC - 1 and w is w_lo))
            last.then_inc(panel_done, 1)

        def act_split(act, u, first=False):
            s = u[1]
            act.wait_ge(raw_in[s], u[2])
            if not first:
                act.wait_ge(panel_done, u[0] - 1)
            nc.scalar.activation(w_hi[:, s], raw[:, s], ACT.Copy).then_inc(hi_ready, 1)

        def dve_split(dve, u):
            s = u[1]
            dve.wait_ge(hi_ready, u[0] + 1)
            nc.vector.tensor_tensor(w_lo[:, s], raw[:, s], w_hi[:, s].bitcast(F32),
                                    ALU.subtract).then_inc(lo_ready, 1)

        def num(u):
            return (u, u % 2, 16 * (u // 2 + 1))

        def in_loop(u0, i, d):
            half = (u0 + d) // 2
            return (i * 2 + (u0 + d), d % 2, i * 16 + 16 * (half + 1))

        def pairs(eng, u0, n, body, skip_first=0, skip_last=0, issued=0):
            for c in range(issued, skip_first):
                body(num(u0 + c), c)
            if n - skip_first - skip_last >= 2:
                assert skip_first % 2 == 0
                with eng.Fori(skip_first // 2, (n - skip_last) // 2) as i:
                    for d in range(2):
                        body(in_loop(u0, i, d), i * 2 + d)
            for c in range(n - skip_last, n):
                body(num(u0 + c), c)

        def act_norm(act, nm, gain, bias, buf, hi_out=None, after=None):
            nm.wait(act, "mu", 1)
            nc.scalar.activation(mu[:, :, :], pl[:, :, 0:HT], ACT.Copy).then_inc(nsem["mu_out"], 1)
            for c in range(nm.n):
                nm.wait(act, "xc", c + 1)
                if c >= 2:
                    nm.wait(act, "var", c - 1)
                nc.scalar.activation(sq[:, c % 2], buf[:, c, :].rearrange("p (b t) -> p b t", b=2),
                                     ACT.Square).then_inc(nsem["sq"], 1)
            act_apply(act, nm, gain, bias, hi_out, after)

        def act_apply(act, nm, gain, bias, hi_out=None, after=None):
            nm.wait(act, "veps", 1)
            nc.scalar.activation(rs[:, :, :], rs[:, :, :], ACT.Sqrt).then_inc(nsem["std"], 1)
            for c in range(nm.n + 1):
                if c < nm.n:
                    nm.wait(act, "yt", c + 1)
                    if c >= nm.slots:
                        nm.wait(act, "used", c - nm.slots + 1)
                    nc.scalar.activation(ya[:, c % nm.slots, :], yt[:, c % 2, :], ACT.Identity,
                                         scale=gain[:, c:c + 1], bias=bias[:, c:c + 1]).then_inc(nsem["ya"], 1)
                if hi_out is not None and c >= 1:
                    nm.wait(act, "ya", c)
                    nc.scalar.activation(hi_out[:, c - 1, :], ya[:, (c - 1) % nm.slots, :], ACT.Copy).then_inc(nsem["hi"], 1)
                if after is not None:
                    after(c)

        def flat(x):
            return x.rearrange("p b t -> p (b t)")

        def dve_norm(dve, nm, buf, lo_out=None, hi=None, after=None):
            nm.wait(dve, "mu_out", 1)
            for c in range(nm.n):
                nc.vector.tensor_tensor(buf[:, c, :], buf[:, c, :], flat(mu[:, :, :]), ALU.subtract).then_inc(nsem["xc"], 1)
            nm.wait(dve, "var", nm.n)
            nc.vector.tensor_scalar(rs[:, :, :], pl[:, :, 0:HT], EPS, None, ALU.add).then_inc(nsem["veps"], 1)
            dve_apply(dve, nm, buf, lo_out, hi, after)

        def dve_apply(dve, nm, buf, lo_out=None, hi=None, after=None, less=None):
            nm.wait(dve, "std", 1)
            nc.vector.reciprocal(rs[:, :, :], rs[:, :, :])
            dve.drain()
            for c in range(nm.n + 2):
                if c < nm.n:
                    if c >= 2:
                        nm.wait(dve, "ya", c - 1)
                    if less is not None:
                        dve.wait_ge(less_mu, less + c + 1)
                    nc.vector.tensor_tensor(yt[:, c % 2, :], buf[:, c, :], flat(rs[:, :, :]), ALU.mult)\
                        .then_inc(nsem["yt"], 1)
                if lo_out is not None and c >= 2:
                    k = c - 2
                    nm.wait(dve, "hi", k + 1)
                    nc.vector.tensor_tensor(lo_out[:, k, :], ya[:, k % nm.slots, :], hi[:, k, :].bitcast(F32),
                                            ALU.subtract).then_inc(nsem["used"], 1)
                if after is not None:
                    after(c)

        def act_shift(act, k):
            act.wait_ge(shift_done, k)
            nc.scalar.activation(mu[:, :, :], pl[:, :, 0:HT], ACT.Copy, scale=float(KC)).then_inc(shift_out, 1)

        def act_square(act, nm, c, slot, buf=r, squares=sq):
            nm.wait(act, "xc", c + 1)
            if not isinstance(c, int) or c >= 2:
                nm.wait(act, "var", c - 1)
            nc.scalar.activation(squares[:, slot], buf[:, bass.ds(c, 1), :].rearrange("p x (b t) -> p (x b) t", b=2),
                                 ACT.Square).then_inc(nsem["sq"], 1)

        def act_summed(act, u0, nm, split):
            def body(u, c):
                split(u)
                if isinstance(u[0], int) and c == 1:
                    act_shift(act, nm.k)
                elif isinstance(u[0], int) and c == 2:
                    act_square(act, nm, 0, 0)
                    act_square(act, nm, 1, 1)
                elif not isinstance(u[0], int) or c >= 3:
                    act_square(act, nm, c - 1, 1 - u[1])
            pairs(act, u0, KC, body, skip_first=4)
            act_square(act, nm, KC - 1, 1)
            act_split(act, num(u0 + KC + 1))
            act_mean(act, nm)

        def act_mean(act, nm):
            nm.wait(act, "mu", 1)
            nc.scalar.activation(mu[:, :, :], pl[:, :, 0:HT], ACT.Copy).then_inc(nsem["mu_out"], 1)

        def dve_less_shift(nm, c, buf=r):
            nc.vector.tensor_tensor(buf[:, c, :], buf[:, c, :], flat(mu[:, :, :]), ALU.subtract).then_inc(nsem["xc"], 1)

        def dve_variance(dve, nm):
            nm.wait(dve, "mu_out", 1)
            nm.wait(dve, "var", KC)
            nc.vector.tensor_tensor(rs[:, :, :], mu[:, :, :], mu[:, :, :], ALU.mult)
            dve.drain()
            for b in range(2):
                last = nc.vector.scalar_tensor_tensor(rs[:, b, :], pt[b][:, 0:HT], EPS, rs[:, b, :], ALU.add, ALU.subtract)
            last.then_inc(nsem["veps"], 1)

        def pool_less_mean(pool, nm, buf=r):
            nm.wait(pool, "mu_out", 1)
            for c in range(KC):
                nc.gpsimd.tensor_tensor(buf[:, c, :], buf[:, c, :], flat(mu[:, :, :]), ALU.subtract).then_inc(less_mu, 1)

        mem_hi = at("mem_hi", Y_HI, [P, KC, MEM], FR)
        mem_lo = at("mem_lo", Y_HI + KC * MEM * 4, [P, KC, MEM], FR)
        rows = at("rows", Y_LO, [P, 3, D])
        row_tiles = [(a["mem_prompt"][0, t * P:(t + 1) * P, :], P, mem_hi, mem_lo, t * P) for t in range(MT)] + \
                    [(a["x_prompt"][0, t * P:(t + 1) * P, :], P, h_hi, h_lo, t * P) for t in range(NT)] + \
                    [(a["x_sample"].rearrange("b s d -> (b s) d"), NS, h_hi, h_lo, SEQ)]
        NG = KC // 4

        def row_views(m, part):
            _, rn, hi, lo, t0 = row_tiles[m // NG]
            g = m % NG
            ps = pt[m % 2][:, :].rearrange("p (q t) -> p q t", q=4)[:, :, 0:rn]
            return ps, (hi, lo)[part][:, 4 * g:4 * g + 4, t0:t0 + rn]

        kvt = at("kvt", TMP, [P, 2, MEM])
        kvn = at("kvn", TMP + 2048, [P, 2, MT, P])

        vt = at("vt", Y_HI, [P, SH, T])
        st = at("st", Y_HI + SH * T * 4, [P, SH, T])
        sgu_bias = at("sgu_bias", Y_LO, [P, SH, P])
        ws_n = at("ws_n", Y_LO + 4096, [P, SH, P])
        ws_t = at("ws_t", Y_LO + 8192, [P, SH, P])
        ws_s = at("ws_s", Y_LO + 12288, [NS, SH, NS])
        vns = at("vns", Y_LO + 13312, [NS, SH, P])
        vn = at("vn", TMP + 8 * 2176, [P, 2, NT, P])
        ug = at("ug", TMP, [P, 2, T])
        yf = at("yf", TMP + 2 * 2176, [P, 2, T])
        ws_zero, ws_in, ws_tr, ws_cp = sem("ws_zero"), sem("ws_in"), sem("ws_tr"), sem("ws_cp")
        ws_ready = sem("ws_ready")
        vn_ready, s_done, st_ready = sem("vn_ready"), sem("s_done"), sem("st_ready")
        y_ready, ysp_hi, ysp_lo = sem("y_ready"), sem("ysp_hi"), sem("ysp_lo")
        v_state_out = sem("v_state_out")

        ep = at("ep", TMP, [P, 2, 16 + SEQ])
        es = at("es", TMP + 4224, [P, 2, DB, 20])
        fa = at("fa", TMP + 5504, [P, 2, 16 + SEQ])
        fas = at("fas", TMP + 5504 + 4224, [P, 2, DB, 20])
        fb = at("fb", TMP + 11008, [P, 2, 16 + SEQ])
        fbs = at("fbs", TMP + 11008 + 4224, [P, 2, DB, 20])
        yp = at("yp", TMP + 11008, [P, 2, T])
        dp = at("dp", TMP + 16512, [P, 2, T])
        an = at("an", TMP + 20864, [STATE + NS, 2, P])
        cpn = at("cpn", Y_HI + 6 * T * 4, [DB * STATE, D_POOL])
        pw = at("pw", Y_LO + 7 * T * 4, [P, 2, 256])
        cp_in, pw_in, pool_zero = sem("cp_in"), sem("pw_in"), sem("pool_zero")
        ep_ready, es_ready, at_done, an_ready, an_out = (sem("ep_ready"), sem("es_ready"), sem("at_done"),
                                                         sem("an_ready"), sem("an_out"))
        d_ready, pm_done, yp_ready, pp_hi, pp_lo = (sem("d_ready"), sem("pm_done"), sem("yp_ready"),
                                                    sem("pp_hi"), sem("pp_lo"))
        state_out = sem("state_out")

        qt = at("qt", Y_HI, [P, KC, T])
        kv = at("kv", Y_LO, [P, 2, MT, D])
        qm = at("qm", W_HI, [P, KC, 288])
        kr = at("kr", W_HI + KC * 288 * 4, [P, 3, 4, MEM])
        ktp = at("ktp", W_HI, [P, KC, MEM])
        vp = at("vp", W_LO, [P, MT, D])
        ssm = at("ssm", TMP, [NS, AH, MEM])
        pts = at("pts", TMP + 4096, [P, AH * MT, NS])
        smx = at("smx", TMP + 5120, [NS, 4, AH])
        pr = at("pr", TMP + 5248, [P, 2, MEM])
        pst = at("pst", TMP + 7296, [P, 2, 4])
        ptt = [at(f"ptt{h}", TMP + (7328 + 4096 * h if h < 3 else 0), [P, MT, SEQ]) for h in range(AH)]

        def score_bank(n):
            return (pp[0][:, 0, 0:MEM], pp[0][:, 1, 0:MEM], pp[1][:, 0, 0:MEM])[n % 3]
        qm_zero, qm_ready = sem("qm_zero"), sem("qm_ready")
        kv_in = [sem("kv_in0"), sem("kv_in1")]
        kr_tr, kr_a, kr_d, ks_done = sem("kr_tr"), sem("kr_a"), sem("kr_d"), sem("ks_done")
        ss_max, ss_exp, ss_p, ss_tr, ss_pt, sv_done, so_hi, so_lo = [sem("att_s%d" % n) for n in range(8)]
        kp_in, vp_in = sem("kp_in"), sem("vp_in")
        ps_done, ps_max, ps_exp, ps_p, ps_tr, ps_pt, pv_done, po_hi, po_lo = [sem("att_p%d" % n) for n in range(9)]

        sc = at("sc", Y_HI, [P, 2 * PH, NT + 1, P])
        sc2 = at("sc2", Y_HI + 40960, [P, NT + 1, P])
        sv = at("sv", Y_HI + 43520, [P, PH, 2, NT + 1, TOPK])
        si = at("si", Y_HI + 48640, [P, PH, 2, NT + 1, TOPK], U32)
        cand = at("cand", Y_HI + 53760, [P, NT + 1, 256])
        cand2 = at("cand2", Y_HI + 58880, [P, NT + 1, 256])
        sub_n = at("sub_n", Y_HI + 58880, [P, 2, P])
        q2 = at("q2", Y_HI + 64000, [P, 2, T])
        sub_t = at("sub_t", Y_HI + 68352, [P, 2, P])
        eq = at("eq", Y_HI, [P, 2, NT + 1, TOPK, TOPK])
        gs = at("gs", Y_HI, [P, NK, P])
        sif = at("sif", TMP, [P, PH, 2, NT + 1, TOPK])
        ab_f = at("ab_f", TMP + 5120, [P, 2, NT + 1, TOPK])
        ab_u = at("ab_u", TMP + 5760, [P, 2, NT + 1, TOPK], U32)
        ijt = at("ijt", TMP, [P, 3, T])
        iota_k = at("iota_k", TMP + 6528, [P, P])
        ge2 = at("ge2", TMP + 7040, [P, 2, T])
        ij = at("ij", TMP + 11392, [P, 2, NT + 1, P])
        gw = at("gw", TMP + 16512, [P, NT + 1, P])
        oh = at("oh", TMP + 11392, [P, 2, 2, 4, P])
        fi = at("fi", TMP + 19584, [P, NT + 1, TOPK], U32)
        sums = at("sums", TMP + 19904, [P, 2, 40])
        iota16 = at("iota16", TMP + 20224, [P, TOPK])
        PICK_STEPS = 5
        sub_in, sub_tr, sub_cp = sem("sub_in"), sem("sub_tr"), sem("sub_cp")
        iota_ready, sc_zero = sem("iota_ready"), sem("sc_zero")
        sc_done, sc_out, cand_ready, fin_ready, eq_ready = [sem("sel%d" % n) for n in range(5)]
        g_sub, g_exp, gw_ready, ijt_done, ijt_out = [sem("gate%d" % n) for n in range(5)]
        oh_ready, g_done, g_out, g_stored = [sem("gmat%d" % n) for n in range(4)]

        AHEAD = 22
        PICK_COLS = 16
        TILE_COLS = 6
        acc = at("acc", Y_HI, [P, KC, T])
        v_hi = at("v_hi", Y_LO, [P, 2, D], FR)
        v_raw = at("v_raw", Y_LO + 16384, [P, 2, D])
        v_lo = at("v_lo", Y_LO + 16384, [P, 2, D], FR)
        u_raw = at("u_raw", RAW, [P, 2, D])
        ut_hi = at("ut_hi", W_HI, [P, 2, KC, P], FR)
        ut_lo = at("ut_lo", W_LO, [P, 2, KC, P], FR)
        v2_hi = at("v2_hi", W_HI, [P, 2, D], FR)
        v2_raw = at("v2_raw", RAW, [P, 2, D])
        v2_lo = at("v2_lo", RAW, [P, 2, D], FR)
        vslot = [(v_hi, v_raw, v_lo), (v2_hi, v2_raw, v2_lo)]
        g2 = at("g2", TMP, [P, 2, T])
        p_hi = [at("p_hi0", TMP + 13056, [P, 2, T], FR), at("p_hi1", TMP + 4352, [P, 2, T], FR)]
        p_lo = [at("p_lo0", TMP + 17408, [P, 2, T], FR), at("p_lo1", TMP + 8704, [P, 2, T], FR)]
        p_f = [at("p_f0", TMP + 17408, [P, 2, T]), at("p_f1", TMP + 8704, [P, 2, T])]
        sq3 = at("sq3", TMP + 13056, [P, 2, 2, HT])
        s_scr = nc.dram_tensor("s_scr", [AHEAD, 2, P, T], F32).ap()
        s_in = sem("s_in")
        ge_stored = [sem("ge_stored0"), sem("ge_stored1")]
        h_sum, acc_ready = sem("h_sum"), sem("acc_ready")
        u_in = [sem("u_in0"), sem("u_in1")]
        v_in = [sem("v_in0"), sem("v_in1")]
        g_in = sem("g_in")
        t_done, t_hi, t_lo = sem("t_done"), sem("t_hi"), sem("t_lo")
        u_done, ge_done, gm_done, ph_done, pl_done = [sem("act%d" % n) for n in range(5)]
        vh_done, vl_done = sem("vh_done"), sem("vl_done")
        vd_done, acc_done = sem("vd_done"), sem("acc_done")

        def gate_columns(eng, column):
            for t in range(NT):
                q0 = (PICK_COLS + t * TILE_COLS) // 2
                if t == 0:
                    for i in range(2):
                        for j in range(2):
                            column(q0 + i, j, (t, i))
                else:
                    with eng.Fori(0, 2) as i:
                        for j in range(2):
                            column(i + q0, j, (t, i))
                for j in range(2):
                    column(q0 + 2, j)
            column(AHEAD - 2, 0, (NT, 0))
            column(AHEAD - 2, 1)
            column(AHEAD - 1, 0)
        assert PICK_COLS + NT * TILE_COLS + 4 == 2 * AHEAD and TILE_COLS == 6

        def group(tile, j, g, s):
            t, i = tile
            return i * 16 + (32 * t + 8 * j + 2 * g + s), i * 64 + (32 * j + 8 * g + 4 * s)
        res = at("res", Y_LO, [P, 2, NT, 4, P])
        ress = at("ress", Y_LO + 16384, [NS, 2, 4, P])
        o_a, o_d = sem("o_a"), sem("o_d")
        o_out = [sem("o_out0"), sem("o_out1")]

        @block.sync
        def _(sp):
            def rows_load(n):
                src, rn = row_tiles[n][:2]
                if n >= 3:
                    sp.wait_ge(tr_done, NG * (n - 2))
                sp.dma_start(rows[0:rn, n % 3, :], src).then_inc(row_in[n % 3], 16)

            def panel_load(view, c0):
                def load(u, c):
                    if not isinstance(u[0], int) or u[0] >= 2:
                        sp.wait_ge(lo_ready, u[0] - 1)
                    sp.dma_start(raw[:, u[1]], view[:, :, c + c0, :]).then_inc(raw_in[u[1]], 16)
                return load

            for n in range(3):
                rows_load(n)
            for c in range(2):
                panel_load(streams[0][1], 0)(num(c), c)
            for n in range(3, len(row_tiles)):
                rows_load(n)
            for u0, view, c0, n in streams:
                load = panel_load(view, c0)
                if u0 == MK0:
                    pairs(sp, u0, n, load, skip_first=2, issued=2)
                elif u0 == MO0:
                    for c in range(2):
                        load(num(u0 + c), c)
                    sp.wait_ge(panel_done, WO0 + 16)
                    for b in range(DB):
                        if b >= 2:
                            sp.wait_ge(kr_tr, AH * (b - 1))
                        sp.dma_start(kv[:, b % 2], a["cache_mem_k"][0, b].rearrange("(t p) h d -> p t (h d)", p=P))\
                            .then_inc(kv_in[b % 2], 16)
                    for b in range(DB):
                        if b < 2:
                            sp.wait_ge(kr_tr, AH * (DB - 1 + b))
                        else:
                            sp.wait_ge(sv_done, b - 1)
                        sp.dma_start(kv[:, b % 2], a["cache_mem_v"][0, b].rearrange("(t p) h d -> p t (h d)", p=P))\
                            .then_inc(kv_in[b % 2], 16)
                        if b == 1:
                            sp.wait_ge(ks_done, DB * AH)
                            for s in range(2):
                                sp.wait_ge(kt_stored[s], 16 * 8)
                                sp.wait_ge(nat_stored[s], 16 * 16)
                            sp.dma_start(ktp[:, :, :], k_scr.rearrange("c p m -> p c m")).then_inc(kp_in, 16)
                            sp.dma_start(vp[:, :, :], o["v"][0, 0].rearrange("(t p) h d -> p t (h d)", p=P))\
                                .then_inc(vp_in, 16)
                    pairs(sp, u0, n, load, skip_first=2, issued=2)
                else:
                    pairs(sp, u0, n, load)
            uv = a["peer_u"][0].rearrange("(i q j) d -> q j i d", q=NPAIR, j=2)
            vv = a["peer_v"][0].rearrange("(i q j) d -> q j i d", q=NPAIR, j=2)
            gv = g_scr.rearrange("i (q j) t -> q i j t", j=2)

            def u_load(q, j, free=None):
                if free is not None:
                    sp.wait_ge(t_done, free)
                sp.dma_start(u_raw[:, j, :], uv[q, j]).then_inc(u_in[j], 16)

            def ge_store(q, j):
                sp.wait_ge(ge_done, q * 2 + (j + 1))
                sp.dma_start(s_scr[q, j], ge2[:, j, :]).then_inc(ge_stored[j], 16)

            def v_load(q, slot=0):
                for j in range(2):
                    sp.dma_start(vslot[slot][1][:, j, :], vv[q, j]).then_inc(v_in[j], 16)

            def g_load(q):
                if not (isinstance(q, int) and q == 0):
                    sp.wait_ge(gm_done, q * 2)
                sp.dma_start(g2[:, :, :], gv[q]).then_inc(g_in, 16)

            def s_load(q, par):
                sp.dma_start(p_f[par][:, :, :], s_scr[q].rearrange("j p t -> p j t")).then_inc(s_in, 16)

            for j in range(2):
                sp.wait_ge(lo_ready, NPANEL - 1 + j)
                u_load(0, j)
            for j in range(2):
                u_load(1, j, 4 * (j + 1))
                if j == 1:
                    ge_store(0, 0)
            with sp.Fori(1, AHEAD - 1) as q:
                u_load(q + 1, 0, q * 8 + 4)
                ge_store(q - 1, 1)
                u_load(q + 1, 1, q * 8 + 8)
                ge_store(q, 0)
            ge_store(AHEAD - 2, 1)
            ge_store(AHEAD - 1, 0)
            sp.wait_ge(g_stored, 32 * (NT + 1))
            g_load(0)
            for j in range(2):
                sp.wait_ge(ge_stored[j], 16)
            s_load(0, 0)
            v_load(0)
            ge_store(AHEAD - 1, 1)
            g_load(1)
            for j in range(2):
                sp.wait_ge(ge_stored[j], 16 * AHEAD)
            s_load(1, 1)
            sp.wait_ge(u_done, 2 * AHEAD)
            sp.wait_ge(vh_done, 2)
            v_load(1, 1)

            def ahead_loads(q, slot):
                g_load(q)
                sp.wait_ge(vd_done, q * KC - KC)
                s_load(q, slot)
                sp.wait_ge(vh_done, q * 2)
                v_load(q, slot)
            with sp.Fori(1, AHEAD // 2 - 1) as i:
                for slot in range(2):
                    ahead_loads(i * 2 + slot, slot)
            ahead_loads(AHEAD - 2, 0)
            sp.wait_ge(vd_done, (AHEAD - 2) * KC)
            for j in range(2):
                u_load(AHEAD, j)
            g_load(AHEAD - 1)
            s_load(AHEAD - 1, 1)
            sp.wait_ge(vd_done, (AHEAD - 1) * KC)
            v_load(AHEAD - 1)
            g_load(AHEAD)
            with sp.Fori(AHEAD, NPAIR - 1) as q:
                for j in range(2):
                    u_load(q + 1, j, q * 8 + (4 * j + 4))
                g_load(q + 1)
                sp.wait_ge(vd_done, q * KC)
                v_load(q)
            sp.wait_ge(u_done, 2 * NPAIR)
            sp.wait_ge(vh_done, 2 * (NPAIR - 1))
            v_load(NPAIR - 1, 1)

        @block.tensor
        def _(pe):
            mm, turn = nc.tensor.matmul, nc.tensor.transpose
            pe.wait_ge(ident_ready, 3)
            for n in range(len(row_tiles)):
                pe.wait_ge(row_in[n % 3], 16 * (n // 3 + 1))
                rn = row_tiles[n][1]
                for g in range(NG):
                    m = n * NG + g
                    if m >= 2:
                        pe.wait_ge(tr_free, m - 1)
                    for q in range(4):
                        c = 4 * g + q
                        last = turn(pt[m % 2][:, q * P:q * P + rn], rows[0:rn, n % 3, c * P:(c + 1) * P],
                                    ident[0:rn, 0:rn])
                    last.then_inc(tr_done, 1)

            pe.wait_ge(tr_free, NG * len(row_tiles))

            def kv_turn(u, c, first=False):
                pe.wait_ge(evacuated, u[0] + 1)
                if not first:
                    pe.wait_ge(kvn_ready, u[0] - 1)
                for m in range(MT):
                    last = turn(pt[u[1]][:, m * P:(m + 1) * P], kvt[:, u[1], m * P:(m + 1) * P], ident[:, :])
                last.then_inc(kvt_done, 1)
            pe_panel(pe, num(0), mem_hi, mem_lo, first=True, n=MEM)
            pe_panel(pe, num(1), mem_hi, mem_lo, first=True, n=MEM)
            kv_turn(num(0), 0, first=True)
            pe_panel(pe, num(2), mem_hi, mem_lo, n=MEM)
            kv_turn(num(1), 0, first=True)
            with pe.Fori(1, V0 // 2 - 1) as i:
                for d in range(2):
                    pe_panel(pe, in_loop(0, i, d + 1), mem_hi, mem_lo, n=MEM)
                    kv_turn(in_loop(0, i, d), 0)
            pe_panel(pe, num(V0 - 1), mem_hi, mem_lo, n=MEM)
            kv_turn(num(V0 - 2), 0)
            kv_turn(num(V0 - 1), 0)

            def stats(nm, c, slot, start=False, stop=False, buf=r, squares=sq):
                nm.wait(pe, "sq", c + 1)
                for b in range(2):
                    mm(pl[:, b, 0:HT], mean16[:, :], buf[:, c, b * HT:(b + 1) * HT], start=start, stop=stop)
                for b in range(2):
                    last = mm(pt[b][:, 0:HT], mean16[:, :], squares[:, slot, b, :], start=start, stop=stop)
                    if stop and b == 0:
                        last.then_inc(nsem["mu"], 1)
                last.then_inc(nsem["var"], 1)

            def shift_of(buf):
                for b in range(2):
                    last = mm(pl[:, b, 0:HT], mean16[:, :], buf[:, 0, b * HT:(b + 1) * HT], start=True, stop=True)
                last.then_inc(shift_done, 1)

            def squared(u0, nm):
                for c in range(2):
                    pe_panel(pe, num(u0 + c), y_hi, y_lo)
                pe.wait_ge(evacuated, u0 + 1)
                shift_of(r)
                pe_panel(pe, num(u0 + 2), y_hi, y_lo)
                stats(nm, 0, 0, start=True)
                stats(nm, 1, 1)
                pe_panel(pe, num(u0 + 3), y_hi, y_lo)
                stats(nm, 2, 0)
                with pe.Fori(2, KC // 2) as i:
                    for d in range(2):
                        pe_panel(pe, in_loop(u0, i, d), y_hi, y_lo)
                        stats(nm, i * 2 + (d - 1), 1 - d)
                stats(nm, KC - 1, 1, stop=True)

            def first_two(u0, nm):
                pe.wait_ge(lo_ready, u0 + 2)
                pe.wait_ge(evacuated, u0)
                for k in range(KC):
                    nm.wait(pe, "used", k + 1)
                    for s in range(2):
                        for w, x in ((w_hi, h_hi), (w_hi, h_lo), (w_lo, h_hi)):
                            for b in range(2):
                                last = mm(pp[s][:, b, 0:HT], w[:, s, k, :], x[:, k, b * HT:(b + 1) * HT],
                                          start=(k == 0 and w is w_hi and x is h_hi),
                                          stop=(k == KC - 1 and w is w_lo))
                        if k == KC - 1:
                            last.then_inc(panel_done, 1)

            def summed(u0, n, x_hi, x_lo, buf, nm):
                def sums_of(u, c, start=False, stop=False):
                    pe.wait_ge(evacuated, u + 1)
                    for b in range(2):
                        last = mm(pl[:, b, 0:HT], mean8[:, :], buf[:, c, b * HT:(b + 1) * HT], start=start, stop=stop)
                    return last
                pe_panel(pe, num(u0), x_hi, x_lo)
                pe_panel(pe, num(u0 + 1), x_hi, x_lo)
                sums_of(u0, 0, start=True)
                with pe.Fori(1, n // 2) as i:
                    for d in range(2):
                        pe_panel(pe, in_loop(u0, i, d), x_hi, x_lo)
                        sums_of(i * 2 + (u0 + d - 1), i * 2 + (d - 1))
                sums_of(u0 + n - 1, n - 1, stop=True).then_inc(nsem["mu"], 1)

            def variance(nm):
                nm.wait(pe, "mu_out", 1)
                for c in range(nm.n):
                    nm.wait(pe, "sq", c + 1)
                    for b in range(2):
                        last = mm(pl[:, b, 0:HT], mean8[:, :], sq[:, c % 2, b, :],
                                  start=(c == 0), stop=(c == nm.n - 1))
                    last.then_inc(nsem["var"], 1)

            pe.wait_ge(ws_in, 16)
            for h in range(SH):
                if h >= 2:
                    pe.wait_ge(ws_cp, h - 1)
                else:
                    pe.wait_ge(kvn_ready, V0)
                turn(pt[h % 2][:, 0:P], ws_n[:, h, :], ident[:, :]).then_inc(ws_tr, 1)
            summed(V0, 8, h_hi, h_lo, vt, sgu_norm)
            variance(sgu_norm)
            pe.wait_ge(ws_ready, 1)
            pe.wait_ge(ws_sin, 16 * DB)
            for h in range(SH + 1):
                if h < SH:
                    sgu_norm.wait(pe, "ya", h + 1)
                    if h >= 1:
                        pe.wait_ge(vn_ready, h)
                    for t in range(NT):
                        turn(pt[0][:, t * P:(t + 1) * P], ya[:, h % 2, t * P:(t + 1) * P], ident[:, :])
                    turn(pt[1][0:NS, 0:P], ya[:, h % 2, SEQ:T], ident[:, :]).then_inc(nsem["used"], 1)
                if h >= 1:
                    k = h - 1
                    pe.wait_ge(vn_ready, h)
                    if k >= 2:
                        pe.wait_ge(st_ready, k - 1)
                    for t in range(NT):
                        mm(pp[k % 2][:, 0, t * P:(t + 1) * P], vn[:, k % 2, t, :], ws_t[:, k, :], start=True, stop=True)
                    mm(pp[k % 2][:, 1, 0:NS], vns[:, k, :], ws_s[:, k, :], start=True, stop=True).then_inc(s_done, 1)
            pe.wait_ge(st_ready, SH)
            pairs(pe, U0, 8, lambda u, c: pe_panel(pe, u, h_hi, h_lo))
            pe.wait_ge(cp_in, 16)
            for c in range(2):
                pe_panel(pe, num(A0 + c), h_hi, h_lo)
            for g in range(4):
                pe.wait_ge(evacuated, A0 + 2 * g + 2)
                if g >= 1:
                    pe.wait_ge(yp_ready, 2 * g)
                for c in range(2):
                    turn(pt[0][:, c * P:c * P + DB * STATE], cpn[:, (2 * g + c) * P:(2 * g + c + 1) * P],
                         ident[0:DB * STATE, 0:DB * STATE])
                    last = turn(pt[1][0:STATE + NS, c * P:(c + 1) * P], dp[:, c, SEQ - STATE:T], ident[:, :])
                last.then_inc(at_done, 1)
                if g < 3:
                    for c in range(2, 4):
                        pe_panel(pe, num(A0 + 2 * g + c), h_hi, h_lo)
                pe.wait_ge(d_ready, g + 1)
                pe.wait_ge(an_ready, g + 1)
                pe.wait_ge(pw_in, 16 * (g + 1))
                for c in range(2):
                    for b in range(2):
                        out = pl[:, b, 0:HT] if c == 0 else pt[b][:, 0:HT]
                        for k in range(2):
                            last = mm(out, pw[:, k, c * P:(c + 1) * P], dp[:, k, b * HT:(b + 1) * HT],
                                      start=(k == 0), stop=(k == 1))
                last.then_inc(pm_done, 1)
            pe.wait_ge(pp_lo, 8)
            pe.wait_ge(ysp_lo, 8)
            squared(WO0, norm1)
            first_two(MQ0, norm1)
            pairs(pe, MQ0, 16, lambda u, c: pe_panel(pe, u, h_hi, h_lo), skip_first=2, issued=2)
            pe.wait_ge(qm_ready, 1)
            pe.wait_ge(evacuated, MO0)
            for n in range(DB * AH + 1):
                if n < DB * AH:
                    b, h = n // AH, n % AH
                    if h == 0:
                        pe.wait_ge(kv_in[b % 2], 16 * (b // 2 + 1))
                    if n >= 1:
                        pe.wait_ge(kr_a, n)
                        pe.wait_ge(kr_d, n)
                    for c in range(4):
                        for m in range(MT):
                            last = turn(pt[c // 2][:, (c % 2) * MEM + m * P:(c % 2) * MEM + (m + 1) * P],
                                        kv[:, b % 2, m, (4 * h + c) * P:(4 * h + c + 1) * P], ident[:, :])
                    last.then_inc(kr_tr, 1)
                if n >= 1:
                    b, h = (n - 1) // AH, (n - 1) % AH
                    pe.wait_ge(kr_a, n)
                    pe.wait_ge(kr_d, n)
                    for c in range(4):
                        last = mm(pp[h // 2][0:NS, h % 2, 0:MEM], qm[:, 4 * h + c, NS * b:NS * (b + 1)],
                                  kr[:, (n - 1) % 3, c, :], start=(b == 0 and c == 0), stop=(b == DB - 1 and c == 3))
                    last.then_inc(ks_done, 1)
            pe.wait_ge(ss_p, 1)
            for m in range(AH * MT):
                last = turn(pt[0][:, m * NS:(m + 1) * NS], ssm[:, m // MT, (m % MT) * P:(m % MT + 1) * P],
                            ident[0:NS, 0:NS])
            last.then_inc(ss_tr, 1)
            pe.wait_ge(kp_in, 16)
            pe.wait_ge(ss_exp, AH)
            pe.wait_ge(ss_pt, 1)
            for n in range(AH * NT + 2):
                if n < AH * NT:
                    h, t = n // NT, n % NT
                    if n >= 3:
                        pe.wait_ge(ps_exp, n - 2)
                    for c in range(4):
                        last = mm(score_bank(n), qt[:, 4 * h + c, t * P:(t + 1) * P], ktp[:, 4 * h + c, :],
                                  start=(c == 0), stop=(c == 3))
                    last.then_inc(ps_done, 1)
                if n >= 2:
                    k = n - 2
                    pe.wait_ge(ps_p, k + 1)
                    if k >= 2:
                        pe.wait_ge(ps_pt, k - 1)
                    for m in range(MT):
                        last = turn(pt[k % 2][:, m * P:(m + 1) * P], pr[:, k % 2, m * P:(m + 1) * P], ident[:, :])
                    last.then_inc(ps_tr, 1)
                if n % 2 == 1 and n // 2 < DB:
                    b = n // 2
                    pe.wait_ge(kv_in[b % 2], 16 * (b // 2 + 5))
                    for c in range(KC):
                        for m in range(MT):
                            last = mm(pp[1][:, 1, c * NS + DS * b:c * NS + DS * (b + 1)],
                                      kv[:, b % 2, m, c * P:(c + 1) * P],
                                      pts[:, (c // 4) * MT + m, DS * b:DS * (b + 1)],
                                      start=(m == 0), stop=(m == MT - 1))
                    last.then_inc(sv_done, 1)
            pe.wait_ge(vp_in, 16)
            pe.wait_ge(ps_pt, AH * NT)
            for c in range(KC):
                if c >= 2:
                    pe.wait_ge(po_lo, c - 1)
                for m in range(MT):
                    last = mm(pl[:, c % 2, :], vp[:, m, c * P:(c + 1) * P], ptt[c // 4][:, m, :],
                              start=(m == 0), stop=(m == MT - 1))
                last.then_inc(pv_done, 1)
            pe.wait_ge(po_lo, KC)
            pe.wait_ge(so_lo, 1)
            squared(MO0, norm2)
            first_two(WQ0, norm2)
            pe.wait_ge(sub_in, 16)
            for p in range(2):
                last = turn(pt[0][:, p * P:(p + 1) * P], sub_n[:, p, :], ident[:, :])
            last.then_inc(sub_tr, 1)
            pe.wait_ge(sub_cp, 1)

            def select_scores(u, s, first=False):
                pe.wait_ge(evacuated, u + 1)
                if not first:
                    pe.wait_ge(sc_out, u - WQ0)
                for t in range(NT):
                    mm(pl[:, 0, t * P:(t + 1) * P], q2[:, s, t * P:(t + 1) * P], sub_t[:, s, :], start=True, stop=True)
                mm(pl[0:NS, 1, 0:P], q2[:, s, SEQ:T], sub_t[:, s, :], start=True, stop=True).then_inc(sc_done, 1)
            select_scores(WQ0, 0, first=True)
            with pe.Fori(1, 8) as i:
                for d in range(2):
                    pe_panel(pe, in_loop(WQ0, i, d), h_hi, h_lo)
                    select_scores(i * 2 + (WQ0 + d - 1), (d + 1) % 2)
            def turn_rows(q, j, g, dst):
                if g == 0:
                    pe.wait_ge(u_in[j], q * 16 + 16)
                if not (isinstance(q, int) and q == 0 and j == 0 and g < 2):
                    pe.wait_ge(t_lo, q * 8 + (4 * j + g - 1))
                for c in range(4):
                    last = turn(dst[:, c * P:(c + 1) * P], u_raw[:, j, (4 * g + c) * P:(4 * g + c + 1) * P], ident[:, :])
                last.then_inc(t_done, 1)

            def scores_of(q, j, between=None):
                pe.wait_ge(t_lo, q * 8 + 4 * (j + 1))
                for k in range(KC):
                    for w, x in ((ut_hi, h_hi), (ut_hi, h_lo), (ut_lo, h_hi)):
                        for b in range(2):
                            last = mm(pp[j][:, b, 0:HT], w[:, j, k, :], x[:, k, b * HT:(b + 1) * HT],
                                      start=(k == 0 and w is ut_hi and x is h_hi), stop=(k == KC - 1 and w is ut_lo))
                    if k == KC - 1:
                        last.then_inc(u_done, 1)
                    if between is not None and k % 4 == 1:
                        between(k // 4)

            def gate_matrix(n, s):
                pe.wait_ge(oh_ready, n + 1)
                if not (isinstance(n, int) and n < 2):
                    pe.wait_ge(g_out, n - 1)
                for x in range(4):
                    last = mm(pt[s][:, x * P:(x + 1) * P], oh[:, s, 0, x, :], oh[:, s, 1, x, :], start=True, stop=True)
                last.then_inc(g_done, 1)

            def ahead_column(q, j, tile=None, last=False):
                if not (isinstance(q, int) and q == 0):
                    pe.wait_ge(ge_done, q * 2 + (j - 1))

                def between(g):
                    if not last:
                        turn_rows(q + j, 1 - j, g, pl[:, g % 2, :])
                    if tile is not None:
                        for s in range(2):
                            gate_matrix(group(tile, j, g, s)[0], s)
                scores_of(q, j, between)

            for g in range(4):
                turn_rows(0, 0, g, pt[g % 2][:, :])
                if g == 1:
                    select_scores(NPANEL - 1, 1)
            pe.wait_ge(sc_out, 2 * PH)
            pe.wait_ge(evacuated, NPANEL)
            for j in range(2):
                ahead_column(0, j)
            with pe.Fori(1, PICK_COLS // 2) as q:
                for j in range(2):
                    ahead_column(q, j)
            pe.wait_ge(gw_ready, 1)
            for x in range(3):
                src = gw if x == 2 else ij[:, x]
                if x >= 1:
                    pe.wait_ge(ijt_out, x)
                for t in range(NT):
                    turn(pt[0][:, t * P:(t + 1) * P], src[:, t, :], ident[:, :])
                turn(pt[1][:, 0:NS], src[0:NS, NT, :], ident[0:NS, 0:NS]).then_inc(ijt_done, 1)
            pe.wait_ge(ijt_out, 3)
            gate_columns(pe, ahead_column)
            ahead_column(AHEAD - 1, 1, last=True)
            pe.wait_ge(g_out, T // 4)

            def values_of(q, c, par, slot, scores_between):
                if c < 2:
                    pe.wait_ge(pl_done, q * 2 + 2)
                    pe.wait_ge(vl_done, q * 2 + 2)
                if c < 2 and scores_between:
                    pe.wait_ge(ge_done, q * 2 + (3 + c))
                elif c < 2 and isinstance(q, int) and q == 0:
                    pe.wait_ge(ge_done, 2 * AHEAD - 1 + c)
                else:
                    pe.wait_ge(acc_done, q * KC + (c - 1))
                vh, _, vl = vslot[slot]
                for j in range(2):
                    for w, x in ((vh, p_hi), (vh, p_lo), (vl, p_hi)):
                        for b in range(2):
                            last = mm(pp[c % 2][:, b, 0:HT], w[:, j, c * P:(c + 1) * P],
                                      x[par][:, j, b * HT:(b + 1) * HT],
                                      start=(j == 0 and w is vh and x is p_hi), stop=(j == 1 and w is vl))
                last.then_inc(vd_done, 1)

            def pair_values(q, par, slot=0, scores_between=True, rows_of=None):
                for c in range(KC):
                    values_of(q, c, par, slot, scores_between)
                    if rows_of is not None and c % 2 == 1:
                        turn_rows(rows_of, c // 8, c // 2 % 4, pt[c // 2 % 2])

            for q in range(2):
                pair_values(q, q, q, False)
            with pe.Fori(1, AHEAD // 2 - 1) as i:
                for par in range(2):
                    pair_values(i * 2 + par, par, par, False)
            pair_values(AHEAD - 2, 0, 0, False, rows_of=AHEAD)

            def pair_step(q, par, more=True):
                for j in range(2):
                    pe.wait_ge(acc_done, q * KC - KC - 1 + j)
                    scores_of(q, j)
                pair_values(q - 1, 1 - par, rows_of=q + 1 if more else None)
            with pe.Fori(AHEAD // 2, NPAIR // 2 - 1) as i:
                for par in range(2):
                    pair_step(i * 2 + par, par)
            pair_step(NPAIR - 2, 0)
            pair_step(NPAIR - 1, 1, more=False)
            pe.wait_ge(t_lo, NPAIR * 8)
            for c in range(KC):
                values_of(NPAIR - 1, c, 1, 1, False)
                if c == 1:
                    pe.wait_ge(acc_done, (NPAIR - 1) * KC + 1)
                    shift_of(acc)
                elif c == 2:
                    stats(norm3, 0, 0, start=True, buf=acc, squares=sq3)
                    stats(norm3, 1, 1, buf=acc, squares=sq3)
                elif c >= 3:
                    stats(norm3, c - 1, (c - 1) % 2, buf=acc, squares=sq3)
            stats(norm3, KC - 1, 1, stop=True, buf=acc, squares=sq3)
            norm3.wait(pe, "veps", 1)
            for c in range(KC):
                norm3.wait(pe, "ya", c + 1)
                if c >= 2:
                    pe.wait_ge(o_a, c - 1)
                    pe.wait_ge(o_d, c - 1)
                for t in range(NT):
                    turn(pp[c % 2][:, 0, t * P:(t + 1) * P], ya[:, c % 3, t * P:(t + 1) * P], ident[:, :])
                turn(pp[c % 2][0:NS, 1, 0:P], ya[:, c % 3, SEQ:T], ident[:, :]).then_inc(nsem["used"], 1)

        @block.scalar
        def _(act):
            f = nc.scalar.activation

            def next_split(u):
                if isinstance(u[0], int):
                    act_split(act, num(u[0] + 1), first=u[0] + 1 < 2)
                else:
                    v = u[0] + 1
                    act_split(act, (v, 1 - u[1], u[2] + 16 * u[1]))

            def panel(use, split=True):
                def body(u, c):
                    if split:
                        next_split(u)
                    act.wait_ge(panel_done, u[0] + 1)
                    use(u, c)
                return body

            for m in range(NG * len(row_tiles)):
                act.wait_ge(tr_done, m + 1)
                ps, hi = row_views(m, 0)
                f(hi, ps, ACT.Copy).then_inc(tr_hi, 1)
            act_split(act, num(0), first=True)

            for k in range(2):
                def kv_use(u, c, k=k):
                    if not isinstance(u[0], int) or u[0] >= 2:
                        act.wait_ge(kvt_done, u[0] - 1)
                        if k == 0 or (isinstance(u[0], int) and u[0] < V0 // 2 + 2):
                            act.wait_ge(kt_stored[u[1]], (u[2] - 16) if k == 0 else 16 * 8)
                    f(kvt[:, u[1], :], pp[u[1]][:, 0, 0:MEM], ACT.Copy).then_inc(evacuated, 1)
                pairs(act, k * 16, 16, panel(kv_use), skip_first=2)

            def vt_use(u, c):
                f(vt[:, c, :].rearrange("p (b t) -> p b t", b=2), pp[u[1]][:, :, 0:HT],
                  ACT.Gelu_apprx_tanh).then_inc(evacuated, 1)
            act.wait_ge(kvn_ready, V0)
            for h in range(SH):
                act.wait_ge(ws_tr, h + 1)
                f(ws_t[:, h, :], pt[h % 2][:, 0:P], ACT.Copy).then_inc(ws_cp, 1)
            pairs(act, V0, 8, panel(vt_use))
            for k in range(2):
                act.wait_ge(nat_stored[k], 16 * V0 // 2)
            act.wait_ge(const_in, 16 * 9)
            act_norm(act, sgu_norm, sln_g, sln_b, vt)

            def u_use(u, c):
                if not isinstance(u[0], int) or c >= 2:
                    act.wait_ge(y_ready, c - 1)
                f(ug[:, u[1], :].rearrange("p (b t) -> p b t", b=2), pp[u[1]][:, :, 0:HT],
                  ACT.Gelu_apprx_tanh).then_inc(evacuated, 1)
                act.wait_ge(y_ready, c + 1)
                f(y_hi[:, c + SH, :], yf[:, u[1], :], ACT.Copy).then_inc(ysp_hi, 1)
            act.wait_ge(st_ready, SH)
            pairs(act, U0, 8, panel(u_use), skip_first=2)

            for g in range(4):
                for c in range(2):
                    def a_use(u, _, c=c):
                        if g == 0 and c == 0:
                            act.wait_ge(ysp_lo, SH)
                        if g >= 1:
                            act.wait_ge(pm_done, g)
                        f(dp[:, c, :].rearrange("p (b t) -> p b t", b=2), pp[u[1]][:, :, 0:HT], ACT.Copy)\
                            .then_inc(evacuated, 1)
                    panel(a_use, split=(g == 0 or c == 1))(num(A0 + 2 * g + c), 0)
                act.wait_ge(at_done, g + 1)
                if g == 0:
                    act.wait_ge(pool_zero, 2)
                else:
                    act.wait_ge(d_ready, g)
                    act.wait_ge(an_out, 16 * (DB + 1) * g)
                for c in range(2):
                    last = f(es[:, c, :, 1:16], pt[0][:, c * P:c * P + DB * STATE].rearrange("p (b s) -> p b s", b=DB),
                             ACT.Copy)
                last.then_inc(es_ready, 1)
                f(an[:, :, :], pt[1][0:STATE + NS, 0:2 * P].rearrange("p (c n) -> p c n", c=2), ACT.Copy)\
                    .then_inc(an_ready, 1)
                if g < 3:
                    act_split(act, num(A0 + 2 * g + 3))
                act.wait_ge(pm_done, g + 1)
                for c in range(2):
                    if c == 0:
                        f(yp[:, 0, :].rearrange("p (b t) -> p b t", b=2), pl[:, :, 0:HT], ACT.Copy,
                          scale=pscale[:, 2 * g:2 * g + 1]).then_inc(yp_ready, 1)
                    else:
                        for b in range(2):
                            last = f(yp[:, 1, b * HT:(b + 1) * HT], pt[b][:, 0:HT], ACT.Copy,
                                     scale=pscale[:, 2 * g + 1:2 * g + 2])
                        last.then_inc(yp_ready, 1)
                for c in range(2):
                    act.wait_ge(yp_ready, 2 * g + c + 1)
                    f(y_hi[:, 2 * g + c, :], yp[:, c, :], ACT.Copy).then_inc(pp_hi, 1)
            act_summed(act, WO0, norm1, next_split)
            act_apply(act, norm1, ln_g[:, 0, :], ln_b[:, 0, :], h_hi)

            def q_use(u, c):
                f(qt[:, c, :].rearrange("p (b t) -> p b t", b=2), pp[u[1]][:, :, 0:HT], ACT.Copy).then_inc(evacuated, 1)
            panel(q_use, split=False)(num(MQ0), 0)
            pairs(act, MQ0, 14, panel(q_use), skip_first=2, issued=1)
            panel(q_use)(num(MQ0 + 14), 14)
            panel(q_use, split=False)(num(MQ0 + 15), 15)

            act.wait_ge(qm_ready, 1)
            for n in range(DB * AH):
                act.wait_ge(kr_tr, n + 1)
                if n >= 3:
                    act.wait_ge(ks_done, n - 2)
                f(kr[:, n % 3, 0:2, :], pt[0][:, :].rearrange("p (c m) -> p c m", c=2), ACT.Copy).then_inc(kr_a, 1)
            act.wait_ge(ss_max, 1)
            for h in range(AH):
                f(ssm[:, h, :], pp[h // 2][0:NS, h % 2, 0:MEM], ACT.Exp, bias=smx[:, 1, h:h + 1], scale=ASCALE,
                  accum_out=smx[:, 2, h:h + 1]).then_inc(ss_exp, 1)
            act.wait_ge(ss_tr, 1)
            f(pts[:, :, :], pt[0][:, 0:AH * MT * NS].rearrange("p (m t) -> p m t", t=NS), ACT.Copy).then_inc(ss_pt, 1)
            for n in range(AH * NT + 2):
                if n < AH * NT:
                    act.wait_ge(ps_max, n + 1)
                    if n >= 2:
                        act.wait_ge(ps_tr, n - 1)
                    f(pr[:, n % 2, :], score_bank(n), ACT.Exp, bias=pst[:, n % 2, 1:2], scale=ASCALE,
                      accum_out=pst[:, n % 2, 2:3]).then_inc(ps_exp, 1)
                if n >= 2:
                    k = n - 2
                    h, t = k // NT, k % NT
                    act.wait_ge(ps_tr, k + 1)
                    f(ptt[h][:, :, t * P:(t + 1) * P], pt[k % 2][:, 0:MEM].rearrange("p (m t) -> p m t", m=MT),
                      ACT.Copy).then_inc(ps_pt, 1)
            act.wait_ge(sv_done, DB)
            f(y_hi[:, :, SEQ:T], pp[1][:, 1, :].rearrange("p (c t) -> p c t", c=KC), ACT.Copy).then_inc(so_hi, 1)
            for c in range(KC):
                act.wait_ge(pv_done, c + 1)
                f(y_hi[:, c, 0:SEQ], pl[:, c % 2, :], ACT.Copy).then_inc(po_hi, 1)
            act.wait_ge(pv_done, KC)
            act_split(act, num(MO0))
            act_summed(act, MO0, norm2, next_split)
            act_apply(act, norm2, ln_g[:, 1, :], ln_b[:, 1, :], h_hi)

            act.wait_ge(sub_tr, 1)
            f(sub_t[:, :, :], pt[0][:, 0:2 * P].rearrange("p (c n) -> p c n", c=2), ACT.Copy).then_inc(sub_cp, 1)

            def scores_out(c):
                act.wait_ge(sc_done, c + 1)
                f(sc[:, bass.ds(c, 1), 0:NT, :].rearrange("p x t k -> p (x t) k"),
                  pl[:, 0, :].rearrange("p (t k) -> p t k", t=NT), ACT.Copy)
                f(sc[0:NS, bass.ds(c, 1), NT, :].rearrange("p x k -> p (x k)"), pl[0:NS, 1, 0:P], ACT.Copy)\
                    .then_inc(sc_out, 1)

            def wq_use(u, c):
                if not isinstance(u[0], int) or c >= 2:
                    act.wait_ge(sc_done, c - 1)
                f(q2[:, u[1], :].rearrange("p (b t) -> p b t", b=2), pp[u[1]][:, :, 0:HT], ACT.Copy).then_inc(evacuated, 1)
                if not isinstance(u[0], int) or c >= 1:
                    scores_out(c - 1)
            act.wait_ge(sc_zero, 1)
            panel(wq_use, split=False)(num(WQ0), 0)
            pairs(act, WQ0, 14, panel(wq_use), skip_first=2, issued=1)
            panel(wq_use)(num(NPANEL - 2), 14)
            panel(wq_use, split=False)(num(NPANEL - 1), 15)
            def rows_hi(q, j, g, src, used):
                act.wait_ge(t_done, q * 8 + (4 * j + g + 1))
                if used is not None:
                    act.wait_ge(u_done, used)
                f(ut_hi[:, j, 4 * g:4 * g + 4, :], src.rearrange("p (c i) -> p c i", c=4), ACT.Copy).then_inc(t_hi, 1)

            def ahead_gelu(q, j):
                act.wait_ge(u_done, q * 2 + (j + 1))
                if not (isinstance(q, int) and q == 0):
                    act.wait_ge(ge_stored[j], q * 16)
                f(ge2[:, j, :].rearrange("p (b t) -> p b t", b=2), pp[j][:, :, 0:HT], ACT.Gelu_apprx_tanh)\
                    .then_inc(ge_done, 1)

            def ahead_column(q, j, tile=None):
                for g in range(4):
                    first = isinstance(q, int) and q == 0 and j == 0
                    rows_hi(q + j, 1 - j, g, pl[:, g % 2, :], None if first else q * 2 + j)
                    if tile is not None and tile[0] >= 1 and g == 0:
                        act.wait_ge(g_stored, 32 * tile[0])
                    if tile is not None:
                        for s in range(2):
                            n, t0 = group(tile, j, g, s)
                            act.wait_ge(g_done, n + 1)
                            f(gs[:, :, bass.ds(t0, 4)].rearrange("p j t -> p t j"),
                              pt[s][:, :].rearrange("p (t j) -> p t j", t=4), ACT.Copy).then_inc(g_out, 1)
                ahead_gelu(q, j)

            act.wait_ge(panel_done, NPANEL)
            for g in range(4):
                rows_hi(0, 0, g, pt[g % 2][:, :], None)
                if g == 1:
                    scores_out(15)
            for j in range(2):
                ahead_column(0, j)
            with act.Fori(1, PICK_COLS // 2 - 1) as q:
                for j in range(2):
                    ahead_column(q, j)
            act.wait_ge(g_sub, 1)
            f(gw[:, :, :], gw[:, :, :], ACT.Exp).then_inc(g_exp, 1)
            for j in range(2):
                ahead_column(PICK_COLS // 2 - 1, j)
            for x in range(3):
                act.wait_ge(ijt_done, x + 1)
                f(ijt[:, x, 0:SEQ], pt[0][:, :], ACT.Copy)
                f(ijt[:, x, SEQ:T], pt[1][:, 0:NS], ACT.Copy).then_inc(ijt_out, 1)
            gate_columns(act, ahead_column)

            def v_split_j(q, j, slot=0):
                act.wait_ge(v_in[j], q * 16 + 16)
                f(vslot[slot][0][:, j, :], vslot[slot][1][:, j, :], ACT.Copy).then_inc(vh_done, 1)

            def p_split_hi(q, par):
                for j in range(2):
                    act.wait_ge(gm_done, q * 2 + (j + 1))
                    f(p_hi[par][:, j, :], p_f[par][:, j, :], ACT.Copy).then_inc(ph_done, 1)

            p_split_hi(0, 0)
            for j in range(2):
                v_split_j(0, j)
            ahead_gelu(AHEAD - 1, 1)
            for j in range(2):
                act.wait_ge(ge_stored[j], 16 * AHEAD)

            def act_values(q, slot):
                p_split_hi(q, slot)
                for j in range(2):
                    v_split_j(q, j, slot)
            act_values(1, 1)
            with act.Fori(1, AHEAD // 2 - 1) as i:
                for slot in range(2):
                    act_values(i * 2 + slot, slot)
            act_values(AHEAD - 2, 0)

            def pair_rows(q, g0=0, g1=8):
                for g in range(g0, g1):
                    rows_hi(q, g // 4, g % 4, pt[g % 2][:, :], q * 2)
            pair_rows(AHEAD, 0, 2)
            p_split_hi(AHEAD - 1, 1)
            pair_rows(AHEAD, 2, 8)

            def act_pair(q, par, more=True):
                for j in range(2):
                    v_split_j(q - 1, j)
                for j in range(2):
                    act.wait_ge(u_done, q * 2 + (j + 1))
                    act.wait_ge(vd_done, q * KC - KC)
                    f(p_f[par][:, j, :].rearrange("p (b t) -> p b t", b=2), pp[j][:, :, 0:HT], ACT.Gelu_apprx_tanh)\
                        .then_inc(ge_done, 1)
                    act.wait_ge(gm_done, q * 2 + (j + 1))
                    f(p_hi[par][:, j, :], p_f[par][:, j, :], ACT.Copy).then_inc(ph_done, 1)
                if more:
                    pair_rows(q + 1)
            with act.Fori(AHEAD // 2, NPAIR // 2 - 1) as i:
                for par in range(2):
                    act_pair(i * 2 + par, par)
            act_pair(NPAIR - 2, 0)
            act_pair(NPAIR - 1, 1, more=False)
            for j in range(2):
                v_split_j(NPAIR - 1, j, 1)

            def prompt_rows(c):
                if c >= 1:
                    k = c - 1
                    norm3.wait(act, "used", c)
                    if k >= 8 and k % 4 == 0:
                        act.wait_ge(o_out[k // 4 % 2], 32)
                    f(res[:, k // 4 % 2, :, k % 4, :], pp[k % 2][:, 0, :].rearrange("p (t n) -> p t n", t=NT),
                      ACT.Copy).then_inc(o_a, 1)
            act_shift(act, norm3.k)
            for c in range(KC):
                act_square(act, norm3, c, c % 2, acc, sq3)
            act_mean(act, norm3)
            act_apply(act, norm3, ln_g[:, 2, :], ln_b[:, 2, :], after=prompt_rows)

        @block.vector
        def _(dve):
            tt, ts, stt, copy = (nc.vector.tensor_tensor, nc.vector.tensor_scalar,
                                 nc.vector.scalar_tensor_tensor, nc.vector.tensor_copy)

            def split_next(u):
                dve_split(dve, (u[0] + 1, 1 - u[1], None))

            dve.wait_ge(const_ready, 1)
            for w, n in enumerate(WINDOWS):
                ts(inv_n[:, w, :], cnt[:, :], float(n), None, ALU.min)
            dve.drain()
            nc.vector.reciprocal(inv_n[:, :, :], inv_n[:, :, :])
            for m in range(NG * len(row_tiles)):
                dve.wait_ge(tr_hi, m + 1)
                ps, hi = row_views(m, 0)
                _, lo = row_views(m, 1)
                tt(lo, ps, hi.bitcast(F32), ALU.subtract).then_inc(tr_free, 1)
            dve_split(dve, num(0))

            def kv_copy(u):
                dve.wait_ge(kvt_done, u[0] + 1)
                if not isinstance(u[0], int) or u[0] >= 2:
                    dve.wait_ge(nat_stored[u[1]], u[2] - 16)
                copy(kvn[:, u[1]], pt[u[1]][:, 0:MEM].rearrange("p (m n) -> p m n", m=MT)).then_inc(kvn_ready, 1)

            def kv_use(u, c):
                split_next(u)
                if not isinstance(u[0], int) or u[0] >= 1:
                    kv_copy((u[0] - 1, 1 - u[1], u[2] - 16 * (1 - u[1])))
            pairs(dve, 0, V0, kv_use, skip_first=4)
            kv_copy(num(V0 - 1))

            pairs(dve, V0, 8, lambda u, c: split_next(u))

            def gate_of_head(c):
                if 1 <= c <= SH:
                    h = c - 1
                    sgu_norm.wait(dve, "used", c)
                    if h >= 2:
                        dve.wait_ge(s_done, h - 1)
                    copy(vn[:, h % 2], pt[0][:, :].rearrange("p (t d) -> p t d", t=NT))
                    copy(vns[:, h, :], pt[1][0:NS, 0:P]).then_inc(vn_ready, 1)
                if c >= 2:
                    h = c - 2
                    dve.wait_ge(s_done, h + 1)
                    tt(st[:, h, 0:SEQ].rearrange("p (t i) -> p t i", t=NT),
                       pp[h % 2][:, 0, :].rearrange("p (t i) -> p t i", t=NT),
                       sgu_bias[:, h:h + 1, :].to_broadcast([P, NT, P]), ALU.add)
                    tt(st[:, h, SEQ:T].rearrange("p (b i) -> p b i", b=DB),
                       pp[h % 2][:, 1, 0:NS].rearrange("p (b i) -> p b i", b=DB),
                       sgu_bias[:, h:h + 1, 0:DS].to_broadcast([P, DB, DS]), ALU.add).then_inc(st_ready, 1)
            dve.wait_ge(bias_in, 16)
            dve_norm(dve, sgu_norm, vt, after=gate_of_head)

            def u_use(u, c):
                split_next(u)
                dve.wait_ge(evacuated, u[0] + 1)
                if not isinstance(u[0], int) or c >= 2:
                    dve.wait_ge(ysp_hi, c - 1)
                tt(yf[:, u[1], :], ug[:, u[1], :], st[:, c, :], ALU.mult).then_inc(y_ready, 1)
                dve.wait_ge(ysp_hi, c + 1)
                tt(y_lo[:, c + SH, :], yf[:, u[1], :], y_hi[:, c + SH, :].bitcast(F32), ALU.subtract).then_inc(ysp_lo, 1)
            dve.drain()
            pairs(dve, U0, 8, u_use, skip_first=2)

            for g, w in enumerate(WINDOWS):
                if g == 0:
                    split_next(num(A0))
                split_next(num(A0 + 2 * g + 1))
                dve.wait_ge(ep_ready, g + 1)
                dve.wait_ge(es_ready, g + 1)
                src, srcs = ep, es
                step, n = 1, 0
                while step < w:
                    dst, dsts = ((fa, fas), (fb, fbs))[n % 2]
                    lo = 2 * step - 1
                    tt(dst[:, :, lo:], src[:, :, lo:], src[:, :, lo - step:16 + SEQ - step], ALU.add)
                    tt(dsts[:, :, :, lo:], srcs[:, :, :, lo:], srcs[:, :, :, lo - step:20 - step], ALU.add)
                    dve.drain()
                    src, srcs, step, n = dst, dsts, 2 * step, n + 1
                for c in range(2):
                    stt(dp[:, c, SEQ:T].rearrange("p (b s) -> p b s", b=DB), srcs[:, c, :, 16:20], 1.0 / w,
                        es[:, c, :, 16:20], ALU.mult, ALU.subtract)
                stt(dp[:, :, 16:SEQ], src[:, :, 32:], 1.0 / w, ep[:, :, 32:], ALU.mult, ALU.subtract)
                tt(dp[:, :, 0:16], src[:, :, 16:32], inv_n[:, g:g + 1, :].to_broadcast([P, 2, 16]), ALU.mult)
                dve.drain()
                tt(dp[:, :, 0:16], dp[:, :, 0:16], ep[:, :, 16:32], ALU.subtract).then_inc(d_ready, 1)
                if g < 3:
                    split_next(num(A0 + 2 * g + 2))
                for c in range(2):
                    dve.wait_ge(pp_hi, 2 * g + c + 1)
                    if g == 3 and c == 1:
                        dve.wait_ge(pm_done, 4)
                    tt(y_lo[:, 2 * g + c, :], yp[:, c, :], y_hi[:, 2 * g + c, :].bitcast(F32), ALU.subtract)\
                        .then_inc(pp_lo, 1)

            def residual(nm, u, c):
                split_next(u)
                dve.wait_ge(panel_done, u[0] + 1)
                tt(yt[:, u[1], :], h_hi[:, c, :].bitcast(F32), h_lo[:, c, :].bitcast(F32), ALU.add)
                dve.drain()
                stt(r[:, c, :].rearrange("p (b t) -> p b t", b=2), yt[:, u[1], :].rearrange("p (b t) -> p b t", b=2),
                    ALPHA, pp[u[1]][:, :, 0:HT], ALU.mult, ALU.add).then_inc(evacuated, 1)
                dve.drain()
                if isinstance(u[0], int) and c == 1:
                    dve.wait_ge(shift_out, nm.k)
                    dve_less_shift(nm, 0)
                if not isinstance(u[0], int) or c >= 1:
                    dve_less_shift(nm, c)

            def residual_norm(u0, nm, less):
                pairs(dve, u0, KC, lambda u, c: residual(nm, u, c), skip_first=2)
                dve_split(dve, num(u0 + KC + 1))
                dve_variance(dve, nm)
                dve_apply(dve, nm, r, h_lo, h_hi, less=less)
            dve.drain()
            residual_norm(WO0, norm1, 0)
            pairs(dve, MQ0, 14, lambda u, c: split_next(u), skip_first=2, issued=1)
            split_next(num(MQ0 + 14))

            dve.wait_ge(qm_zero, 1)
            dve.wait_ge(evacuated, MO0)
            copy(qm[:, :, :].rearrange("p c (b x) -> p c b x", x=36)[:, :, :, 0:DS],
                 qt[:, :, SEQ:T].rearrange("p c (b s) -> p c b s", b=DB)).then_inc(qm_ready, 1)
            for n in range(DB * AH):
                dve.wait_ge(kr_tr, n + 1)
                if n >= 3:
                    dve.wait_ge(ks_done, n - 2)
                copy(kr[:, n % 3, 2:4, :], pt[1][:, :].rearrange("p (c m) -> p c m", c=2)).then_inc(kr_d, 1)
            dve.wait_ge(ks_done, DB * AH)
            for h in range(AH):
                nc.vector.tensor_reduce(smx[:, 0, h:h + 1], pp[h // 2][0:NS, h % 2, 0:MEM], AX.X, ALU.max)
            dve.drain()
            ts(smx[:, 1, :], smx[:, 0, :], -ASCALE, None, ALU.mult).then_inc(ss_max, 1)
            dve.wait_ge(ss_exp, AH)
            nc.vector.reciprocal(smx[:, 3, :], smx[:, 2, :])
            dve.drain()
            for h in range(AH):
                last = ts(ssm[:, h, :], ssm[:, h, :], smx[:, 3, h:h + 1], None, ALU.mult)
            last.then_inc(ss_p, 1)
            for n in range(AH * NT):
                dve.wait_ge(ps_done, n + 1)
                if n >= 2:
                    dve.wait_ge(ps_exp, n - 1)
                nc.vector.tensor_reduce(pst[:, n % 2, 0:1], score_bank(n), AX.X, ALU.max)
                dve.drain()
                ts(pst[:, n % 2, 1:2], pst[:, n % 2, 0:1], -ASCALE, None, ALU.mult).then_inc(ps_max, 1)
                dve.wait_ge(ps_exp, n + 1)
                nc.vector.reciprocal(pst[:, n % 2, 3:4], pst[:, n % 2, 2:3])
                dve.drain()
                ts(pr[:, n % 2, :], pr[:, n % 2, :], pst[:, n % 2, 3:4], None, ALU.mult).then_inc(ps_p, 1)
            dve.wait_ge(so_hi, 1)
            tt(y_lo[:, :, SEQ:T], pp[1][:, 1, :].rearrange("p (c t) -> p c t", c=KC), y_hi[:, :, SEQ:T].bitcast(F32),
               ALU.subtract).then_inc(so_lo, 1)
            for c in range(KC):
                dve.wait_ge(po_hi, c + 1)
                tt(y_lo[:, c, 0:SEQ], pl[:, c % 2, :], y_hi[:, c, 0:SEQ].bitcast(F32), ALU.subtract).then_inc(po_lo, 1)
            dve_split(dve, num(MO0))
            residual_norm(MO0, norm2, KC)

            mx, mi, mr = nc.vector.max, nc.vector.max_index, nc.vector.match_replace
            NT1 = NT + 1

            def top16(vals, spare, best, where, between=lambda: None):
                for t in range(NT1):
                    mx(best[:, t, 0:8], vals[:, t, :])
                dve.drain()
                for t in range(NT1):
                    mi(where[:, t, 0:8], best[:, t, 0:8], vals[:, t, :])
                between()
                for t in range(NT1):
                    mr(spare[:, t, :], best[:, t, 0:8], vals[:, t, :], NEG)
                dve.drain()
                between()
                for t in range(NT1):
                    mx(best[:, t, 8:16], spare[:, t, :])
                dve.drain()
                between()
                for t in range(NT1):
                    last = mi(where[:, t, 8:16], best[:, t, 8:16], spare[:, t, :])
                return last

            def pick(h):
                dve.wait_ge(cand_ready, h + 1)
                best = gw[:, :, h * TOPK:(h + 1) * TOPK]
                next_rows()
                top16(cand, cand2, best, fi, next_rows)
                dve.drain()
                nc.vector.tensor_single_scalar(ab_u[:, 0], fi[:, :, :], 4, ALU.logical_shift_right)
                nc.vector.tensor_single_scalar(ab_u[:, 1], fi[:, :, :], 15, ALU.bitwise_and)
                dve.drain()
                copy(ab_f[:, :], ab_u[:, :]).then_inc(fin_ready, 1)
                next_rows()
                dve.drain()
                if h >= 1:
                    next_rows()
                    dve.wait_ge(pool_step, PICK_STEPS * h)
                tt(eq[:, :, :, :, :].rearrange("p x t k y -> p (x t k) y"),
                   iota16[:, :].rearrange("p (n y) -> p n y", n=1).to_broadcast([P, 2 * NT1 * TOPK, TOPK]),
                   ab_f[:, :].rearrange("p x t (k y) -> p (x t k) y", y=1).to_broadcast([P, 2 * NT1 * TOPK, TOPK]),
                   ALU.is_equal).then_inc(eq_ready, 1)

            def half_list(c, between=lambda: None):
                dve.wait_ge(sc_out, c + 1)
                h, p = c // 2, c % 2
                top16(sc[:, c], sc2, sv[:, h, p], si[:, h, p], between)
                dve.drain()
                copy(sif[:, h, p], si[:, h, p]).then_inc(sif_ready, 1)

            for c in range(2 * PH):
                if 1 <= c < 2 * PH - 1:
                    split_next(num(WQ0 + c))
                if c >= 2:
                    half_list(c - 2)

            def rows_lo(q, j, g, src):
                dve.wait_ge(t_hi, q * 8 + (4 * j + g + 1))
                tt(ut_lo[:, j, 4 * g:4 * g + 4, :], src.rearrange("p (c i) -> p c i", c=4),
                   ut_hi[:, j, 4 * g:4 * g + 4, :].bitcast(F32), ALU.subtract).then_inc(t_lo, 1)
            turned = [0]

            def next_rows():
                n = turned[0]
                if n < 4 * (PICK_COLS + 1):
                    rows_lo(n // 8, n // 4 % 2, n % 4, pt[n % 2][:, :] if n < 4 else pl[:, n % 2, :])
                    turned[0] += 1
            for n in range(4):
                next_rows()
            for c in (2 * PH - 2, 2 * PH - 1):
                half_list(c, next_rows)
            for h in range(PH):
                pick(h)
            while turned[0] < 4 * (PICK_COLS - 1):
                next_rows()
            dve.drain()
            gw4 = gw[:, :, :].rearrange("p t (h k) -> p (t h) k", k=TOPK)
            copy(sums[:, 0, :], gw4[:, :, 0:1].rearrange("p n k -> p (n k)"))
            dve.drain()
            tt(gw4, gw4, sums[:, 0, :].rearrange("p (n k) -> p n k", k=1).to_broadcast([P, 40, TOPK]), ALU.subtract)\
                .then_inc(g_sub, 1)
            dve.wait_ge(g_exp, 1)
            nc.vector.tensor_reduce(sums[:, 0, :], gw4, AX.X, ALU.add)
            dve.drain()
            nc.vector.reciprocal(sums[:, 1, :], sums[:, 0, :])
            dve.drain()
            tt(gw4, gw4, sums[:, 1, :].rearrange("p (n k) -> p n k", k=1).to_broadcast([P, 40, TOPK]), ALU.mult)
            while turned[0] < 4 * (PICK_COLS + 1):
                next_rows()
            dve.wait_ge(pool_step, PICK_STEPS * PH)
            dve.drain()
            copy(sums[:, 0, 0:1], sums[:, 1, 0:1]).then_inc(gw_ready, 1)
            dve.wait_ge(ijt_out, 3)

            def one_hot(n, s, t0):
                if not (isinstance(n, int) and n < 2):
                    dve.wait_ge(g_done, n - 1)
                for x in range(4):
                    ts(oh[:, s, 0, x, :], iota_k[:, :], ijt[:, 0, bass.ds(t0 + x, 1)], None, ALU.is_equal)
                    last = ts(oh[:, s, 1, x, :], iota_k[:, :], ijt[:, 1, bass.ds(t0 + x, 1)],
                              ijt[:, 2, bass.ds(t0 + x, 1)], ALU.is_equal, ALU.mult)
                last.then_inc(oh_ready, 1)

            def ahead_column(q, j, tile=None):
                for g in range(4):
                    if tile is not None:
                        for s in range(2):
                            n, t0 = group(tile, j, g, s)
                            one_hot(n, s, t0 + P * tile[0])
                    rows_lo(q + j, 1 - j, g, pl[:, g % 2, :])
            gate_columns(dve, ahead_column)

            def gated(q, par, j):
                if j == 0:
                    dve.wait_ge(g_in, q * 16 + 16)
                tt(p_f[par][:, j, :], p_f[par][:, j, :], g2[:, j, :], ALU.mult).then_inc(gm_done, 1)

            def p_split_lo(q, par, j):
                dve.wait_ge(ph_done, q * 2 + (j + 1))
                tt(p_lo[par][:, j, :], p_f[par][:, j, :], p_hi[par][:, j, :].bitcast(F32), ALU.subtract).then_inc(pl_done, 1)

            def v_split_half(q, j, half, slot=0):
                vh, vr, vl = vslot[slot]
                cs = slice(half * D // 2, (half + 1) * D // 2)
                if half == 0:
                    dve.wait_ge(vh_done, q * 2 + (j + 1))
                last = tt(vl[:, j, cs], vr[:, j, cs], vh[:, j, cs].bitcast(F32), ALU.subtract)
                if half == 1:
                    last.then_inc(vl_done, 1)

            def v_split(q, j, slot=0):
                for half in range(2):
                    v_split_half(q, j, half, slot)

            def add_out(q, c):
                dve.wait_ge(vd_done, q * KC + (c + 1))
                a3 = acc[:, c, :].rearrange("p (b t) -> p b t", b=2)
                tt(a3, a3, pp[c % 2][:, :, 0:HT], ALU.add).then_inc(acc_done, 1)

            def ahead_gated(q, par, j):
                if j == 0:
                    dve.wait_ge(s_in, q * 16 + 16)
                gated(q, par, j)

            for j in range(2):
                ahead_gated(0, 0, j)
            for j in range(2):
                p_split_lo(0, 0, j)
            for j in range(2):
                v_split(0, j)

            def dve_values(q, par, slot, values=True, rows=False):
                for c in range(KC):
                    if isinstance(q, int) and q == 1:
                        dve.wait_ge(acc_ready, c + 1)
                    add_out(q - 1, c)
                    if c in (3, 4):
                        ahead_gated(q, par, c - 3)
                    if c in (5, 6):
                        p_split_lo(q, par, c - 5)
                    if values and c in (8, 10, 12, 14):
                        v_split_half(q, (c - 8) // 4, (c - 8) // 2 % 2, slot)
                    if rows and c % 2 == 1:
                        rows_lo(AHEAD, c // 8, c // 2 % 4, pt[c // 2 % 2][:, :])
            dve_values(1, 1, 1)
            with dve.Fori(1, AHEAD // 2 - 1) as i:
                for slot in range(2):
                    dve_values(i * 2 + slot, slot, slot)
            dve_values(AHEAD - 2, 0, 0)
            dve_values(AHEAD - 1, 1, 0, values=False, rows=True)

            def dve_pair(q, par, more=True):
                for j in range(2):
                    v_split(q - 1, j)
                for j in range(2):
                    dve.wait_ge(ge_done, q * 2 + (j + 1))
                    gated(q, par, j)
                    if j == 1:
                        add_out(q - 1, 0)
                    p_split_lo(q, par, j)
                for g in range(8):
                    if g > 0:
                        add_out(q - 1, 2 * g)
                    add_out(q - 1, 2 * g + 1)
                    if more:
                        rows_lo(q + 1, g // 4, g % 4, pt[g % 2][:, :])
                    elif g >= 4:
                        v_split_half(NPAIR - 1, (g - 4) // 2, g % 2, 1)
            with dve.Fori(AHEAD // 2, NPAIR // 2 - 1) as i:
                for par in range(2):
                    dve_pair(i * 2 + par, par)
            dve_pair(NPAIR - 2, 0)
            dve_pair(NPAIR - 1, 1, more=False)
            for c in range(KC):
                add_out(NPAIR - 1, c)
                dve.drain()
                if c == 1:
                    dve.wait_ge(shift_out, norm3.k)
                    dve_less_shift(norm3, 0, acc)
                if c >= 1:
                    dve_less_shift(norm3, c, acc)

            def sample_rows(c):
                if 1 <= c <= KC:
                    k = c - 1
                    norm3.wait(dve, "used", c)
                    if k >= 8 and k % 4 == 0:
                        dve.wait_ge(o_out[k // 4 % 2], 32)
                    copy(ress[:, k // 4 % 2, k % 4, :], pp[k % 2][0:NS, 1, 0:P]).then_inc(o_d, 1)
            dve_variance(dve, norm3)
            dve_apply(dve, norm3, acc, after=sample_rows, less=2 * KC)

        @block.gpsimd
        def _(pool):
            g = nc.gpsimd
            g.memset(ident[:, :], 0.0).then_inc(ident_zero, 1)
            g.memset(mean16[:, :], 1.0 / D).then_inc(ident_ready, 1)
            g.memset(mean8[:, :], 1.0 / (D // 2)).then_inc(ident_ready, 1)
            pool.wait_ge(ident_zero, 1)
            g.affine_select(out=ident[:, :], in_=ident[:, :], compare_op=ALU.not_equal, fill=1.0, base=0,
                            pattern=[[-1, P]], channel_multiplier=1).then_inc(ident_ready, 1)
            g.iota(cnt[:, :], pattern=[[1, 16]], base=1, channel_multiplier=0,
                   allow_small_or_imprecise_dtypes=True).then_inc(const_ready, 1)

            def vector_in(dst, src):
                pool.dma_start(dst, src.rearrange("(c p) -> p c", p=P), allow_slow_non_contiguous=True)\
                    .then_inc(const_in, 16)
            for n, name in enumerate(("ln1", "ln2", "ln3")):
                vector_in(ln_g[:, n, :], a[name + "_g"][0])
                vector_in(ln_b[:, n, :], a[name + "_b"][0])
            vector_in(sln_g[:, :], a["sgu_ln_g"][0])
            vector_in(sln_b[:, :], a["sgu_ln_b"][0])
            vector_in(pscale[:, :], a["pool_scale"][0])
            pool.dma_start(o["ps"][0][:, 0:STATE - DS, :], a["cache_pool"][0][:, DS:STATE, :]).then_inc(state_out, 16)

            def kv_store(k):
                out = o["kv"[k]][0, 0].rearrange("(m p) h d -> p m (h d)", p=P).rearrange("p m (c n) -> p m c n", n=P)

                def body(u, c):
                    if k == 0:
                        pool.wait_ge(evacuated, u[0] + 1)
                        pool.dma_start(k_scr[c], kvt[:, u[1], :]).then_inc(kt_stored[u[1]], 16)
                    pool.wait_ge(kvn_ready, u[0] + 1)
                    pool.dma_start(out[:, :, c, :], kvn[:, u[1]]).then_inc(nat_stored[u[1]], 16)
                return body
            pairs(pool, MK0, 16, kv_store(0))
            pool.dma_start(ws_n[:, :, :], a["sgu_w"][0].rearrange("h i j -> i h j")).then_inc(ws_in, 16)
            pool.dma_start(sgu_bias[:, :, :], a["sgu_b"][0:1].to_broadcast([P, SH, P])).then_inc(bias_in, 16)
            g.memset(ws_s[:, :, :], 0.0).then_inc(ws_zero, 1)
            pairs(pool, MV0, 16, kv_store(1))
            pool.wait_ge(ws_cp, SH)
            g.affine_select(out=ws_t[:, :, :], in_=ws_t[:, :, :], compare_op=ALU.is_ge, fill=0.0, base=0,
                            pattern=[[0, SH], [1, P]], channel_multiplier=-1).then_inc(ws_ready, 1)
            pool.wait_ge(ws_ready, 1)
            pool.wait_ge(ws_zero, 1)
            for b in range(DB):
                pool.dma_start(ws_s[DS * b:DS * (b + 1), :, DS * b:DS * (b + 1)], ws_t[0:DS, :, 0:DS])\
                    .then_inc(ws_sin, 16)
            pool.wait_ge(vn_ready, SH)
            pool.dma_start(o["vs"][0].rearrange("b s d -> (b s) d"), vns[:, :, :].rearrange("p h d -> p (h d)"))\
                .then_inc(v_state_out, 16)
            pool.wait_ge(st_ready, SH)
            pool.dma_start(cpn[:, :], a["cache_pool"][0].rearrange("b s d -> (b s) d")).then_inc(cp_in, 16)
            pool.wait_ge(v_state_out, 16)
            pool.wait_ge(ysp_lo, SH)
            g.memset(ep[:, :, 0:16], 0.0).then_inc(pool_zero, 1)
            g.memset(es[:, :, :, 0:1], 0.0).then_inc(pool_zero, 1)
            for n in range(4):
                if n >= 1:
                    pool.wait_ge(pm_done, n)
                pool.dma_start(pw[:, :, :], a["pool_w"][0, n].rearrange("(k p) d -> p k d", p=P)).then_inc(pw_in, 16)
                pool.wait_ge(evacuated, A0 + 2 * n + 2)
                if n >= 1:
                    pool.wait_ge(d_ready, n)
                g.tensor_copy(ep[:, :, 16:], dp[:, :, 0:SEQ])
                g.tensor_copy(es[:, :, :, 16:20], dp[:, :, SEQ:T].rearrange("p c (b s) -> p c b s", b=DB))\
                    .then_inc(ep_ready, 1)
                pool.wait_ge(an_ready, n + 1)
                cs = slice(2 * n * P, 2 * (n + 1) * P)
                pool.dma_start(o["pp"][0, 0, :, cs], an[0:STATE].rearrange("p c n -> p (c n)")).then_inc(an_out, 16)
                for b in range(DB):
                    pool.dma_start(o["ps"][0, b, STATE - DS:STATE, cs],
                                   an[STATE + DS * b:STATE + DS * (b + 1)].rearrange("p c n -> p (c n)"))\
                        .then_inc(an_out, 16)
            pool.wait_ge(an_out, 16 * 4 * (DB + 1))
            pool_less_mean(pool, norm1)
            pool.wait_ge(panel_done, MO0)
            g.memset(qm[:, :, :], 0.0).then_inc(qm_zero, 1)
            pool_less_mean(pool, norm2)
            pool.wait_ge(panel_done, WQ0)
            pool.dma_start(sub_n[:, :, :], a["peer_subkeys"][0].rearrange("s k d -> k s d")).then_inc(sub_in, 16)
            g.memset(sc[:, :, NT, :], 0.0).then_inc(sc_zero, 1)
            norm2.wait(pool, "used", KC)
            g.iota(iota_k[:, :], pattern=[[1, P]], base=0, channel_multiplier=0, allow_small_or_imprecise_dtypes=True)
            g.iota(iota16[:, :], pattern=[[1, TOPK]], base=0, channel_multiplier=0,
                   allow_small_or_imprecise_dtypes=True).then_inc(iota_ready, 1)

            steps = [0]

            def step(ins):
                ins.then_inc(pool_step, 1)
                steps[0] += 1
                pool.wait_ge(pool_step, steps[0])
            pool.wait_ge(iota_ready, 1)
            NT1 = NT + 1

            def picks(h):
                pool.wait_ge(eq_ready, h + 1)
                step(g.tensor_tensor(eq4, eq4, sif[:, h].rearrange("p x t (k y) -> p (x t) k y", k=1)
                                     .to_broadcast([P, 2 * NT1, TOPK, TOPK]), ALU.mult))
                for w in (8, 4, 2):
                    step(g.tensor_tensor(eq4[:, :, :, 0:w], eq4[:, :, :, 0:w], eq4[:, :, :, w:2 * w], ALU.add))
                step(g.tensor_tensor(ij[:, :, :, h * TOPK:(h + 1) * TOPK].rearrange("p x t k -> p (x t) k"),
                                     eq4[:, :, :, 0:1].rearrange("p n k y -> p n (k y)"),
                                     eq4[:, :, :, 1:2].rearrange("p n k y -> p n (k y)"), ALU.add))
            eq4 = eq[:, :, :, :, :].rearrange("p x t k y -> p (x t) k y")

            for h in range(PH):
                pool.wait_ge(sif_ready, 2 * h + 2)
                if h >= 1:
                    pool.wait_ge(fin_ready, h)
                cv = cand[:, :, :].rearrange("p t (x y) -> p t x y", x=TOPK)
                g.tensor_tensor(cv, sv[:, h, 0].rearrange("p t (x y) -> p t x y", y=1).to_broadcast([P, NT1, TOPK, TOPK]),
                                sv[:, h, 1].rearrange("p t (x y) -> p t x y", x=1).to_broadcast([P, NT1, TOPK, TOPK]),
                                ALU.add).then_inc(cand_ready, 1)
                if h >= 1:
                    picks(h - 1)
            picks(PH - 1)
            assert steps[0] == PICK_STEPS * PH
            for t in range(NT + 1):
                n0 = P // 4 * (t + 1) if t < NT else T // 4
                pool.wait_ge(g_out, n0)
                w = P if t < NT else NS
                for c in range(2):
                    pool.dma_start(g_scr[:, 64 * c:64 * (c + 1), t * P:t * P + w], gs[:, 64 * c:64 * (c + 1), 0:w])\
                        .then_inc(g_stored, 16)
            pool.wait_ge(g_stored, 32 * (NT + 1))
            for c in range(KC + 1):
                if c < KC:
                    g.tensor_tensor(acc[:, c, :], h_hi[:, c, :].bitcast(F32), h_lo[:, c, :].bitcast(F32), ALU.add)\
                        .then_inc(h_sum, 1)
                if c >= 1:
                    pool.wait_ge(h_sum, c)
                    g.tensor_scalar(acc[:, c - 1, :], acc[:, c - 1, :], ALPHA, None, ALU.mult).then_inc(acc_ready, 1)
            pool_less_mean(pool, norm3, acc)
            xs = o["xs"].rearrange("b s d -> (b s) d")
            for k in range(4):
                pool.wait_ge(o_a, 4 * (k + 1))
                pool.wait_ge(o_d, 4 * (k + 1))
                pool.dma_start(o["xp"][0].rearrange("(t p) d -> p t d", p=P)[:, :, k * 512:(k + 1) * 512],
                               res[:, k % 2].rearrange("p t c n -> p t (c n)")).then_inc(o_out[k % 2], 16)
                pool.dma_start(xs[:, k * 512:(k + 1) * 512], ress[:, k % 2].rearrange("p c n -> p (c n)"))\
                    .then_inc(o_out[k % 2], 16)
            for k in range(2):
                pool.wait_ge(o_out[k], 64)
            for k in range(2):
                pool.wait_ge(kt_stored[k], 16 * 8)
                pool.wait_ge(nat_stored[k], 16 * 16)
            pool.wait_ge(state_out, 16)


_INS = ["x_prompt", "x_sample", "mem_prompt", "cache_pool", "cache_mem_k", "cache_mem_v", "w_in", "pool_w", "pool_scale",
        "sgu_ln_g", "sgu_ln_b", "sgu_w", "sgu_b", "w_out", "ln1_g", "ln1_b", "w_mq", "w_mk", "w_mv", "w_mo",
        "ln2_g", "ln2_b", "peer_wq", "peer_subkeys", "peer_u", "peer_v", "ln3_g", "ln3_b"]
_OUTS = {"xp": (1, SEQ, D), "xs": (DB, DS, D), "pp": (1, 1, STATE, D_POOL), "k": (1, 1, MEM, AH, D // AH),
         "v": (1, 1, MEM, AH, D // AH), "ps": (1, DB, STATE, D_POOL), "vs": (1, DB, DS, D // 2)}


def kernel(**inputs):
    import numpy as _np
    import concourse.bacc as _bacc
    from concourse.bass_utils import run_bass_kernel_spmd as _run

    nc = _bacc.Bacc("TRN2", target_bir_lowering=False, num_devices=1)
    arrays, args = {}, {}
    for name in _INS:
        arr = _np.ascontiguousarray(inputs[name])
        arrays["in_" + name] = arr
        args[name] = nc.dram_tensor("in_" + name, arr.shape, F32, kind="ExternalInput").ap()
    outs = {name: nc.dram_tensor("out_" + name, shape, F32, kind="ExternalOutput").ap() for name, shape in _OUTS.items()}
    program(nc, args, outs)
    res = _run(nc, [arrays], core_ids=[0])
    return tuple(res.results[0]["out_" + name] for name in _OUTS)
```
